# Optimizing a Trainium2 kernel written in Bass

```python
import jax, jax.numpy as jnp
from jax import lax
import numpy as np
import math
import jax
import jax.numpy as jnp

D_MODEL = 1024
BATCH = 1
SEQ = 256
DEPTH = 1

D_MIX = D_MODEL
D_A = D_MIX // 2
D_B = D_MIX - D_A
HEAD_CH = 64
N_HEADS_A = D_A // HEAD_CH
N_HEADS_B = D_B // HEAD_CH
CONV_A_WIDTH = 3
CONV_B_WIDTH = 31
D_IN = 3 * D_A + 2 * D_B
N_GROUPS = 4
EXPERTS_PER_GROUP = 8
N_EXPERTS = N_GROUPS * EXPERTS_PER_GROUP
TOP_K_IN_GROUP = 2
D_EXPERT = D_MODEL // 2
EPS = 1e-6


def rmsnorm(x, g):
    xf = x.astype(jnp.float32)
    r = lax.rsqrt(jnp.mean(xf * xf, axis=-1, keepdims=True) + EPS)
    return (xf * r).astype(x.dtype) * g

def layernorm(x, g, b):
    xf = x.astype(jnp.float32)
    mu = jnp.mean(xf, axis=-1, keepdims=True)
    var = jnp.mean(jnp.square(xf - mu), axis=-1, keepdims=True)
    return ((xf - mu) * lax.rsqrt(var + EPS)).astype(x.dtype) * g + b

def head_rmsnorm(y, n_heads, gain):
    bsz, s, c = y.shape
    yh = y.reshape(bsz, s, n_heads, c // n_heads).astype(jnp.float32)
    yh = yh * lax.rsqrt(jnp.mean(yh * yh, axis=-1, keepdims=True) + EPS)
    return yh.reshape(bsz, s, c).astype(y.dtype) * gain

def depthwise_conv_centred(u, w):
    k = w.shape[0]
    pad = (k - 1) // 2
    return lax.conv_general_dilated(
        u, w[:, None, :].astype(u.dtype), window_strides=(1,), padding=[(pad, pad)],
        dimension_numbers=("NWC", "WIO", "NWC"), feature_group_count=u.shape[-1])

def mixer_block(h, w_in, conv_a_w, conv_b_w, conv_b_bias, ln_b_g, ln_b_b, beta_a, beta_b, w_out):
    proj = jnp.einsum("bsd,dc->bsc", h, w_in)
    a_in, a_b, a_c, b_val, b_gate = jnp.split(
        proj, [D_A, 2 * D_A, 3 * D_A, 3 * D_A + D_B], axis=-1)
    y_a = a_b * depthwise_conv_centred(a_c * a_in, conv_a_w)
    u = b_val * jax.nn.sigmoid(b_gate)
    u = depthwise_conv_centred(u, conv_b_w) + conv_b_bias
    y_b = jax.nn.silu(layernorm(u, ln_b_g, ln_b_b))
    y = jnp.concatenate([head_rmsnorm(y_a, N_HEADS_A, beta_a),
                         head_rmsnorm(y_b, N_HEADS_B, beta_b)], axis=-1)
    return jnp.einsum("bsc,cd->bsd", y, w_out)

def hierarchical_moe(h, w_route_group, b_route_group, w_route_expert, b_route_expert, w1, w3, w2):
    bsz, s, d = h.shape
    t = h.reshape(bsz * s, d)
    p_group = jax.nn.softmax((t @ w_route_group + b_route_group).astype(jnp.float32), axis=-1)
    g_idx = jnp.argmax(p_group, axis=-1)
    p_sel = jnp.take_along_axis(p_group, g_idx[:, None], axis=1)[:, 0]
    le = (t @ w_route_expert + b_route_expert).astype(jnp.float32)
    le = le.reshape(-1, N_GROUPS, EXPERTS_PER_GROUP)
    le_sel = jnp.take_along_axis(le, g_idx[:, None, None], axis=1)[:, 0]
    p_exp = jax.nn.softmax(le_sel, axis=-1)
    top_v, top_i = lax.top_k(p_exp, TOP_K_IN_GROUP)
    top_w = top_v / jnp.sum(top_v, axis=-1, keepdims=True)
    eid = g_idx[:, None] * EXPERTS_PER_GROUP + top_i
    combine = p_sel[:, None] * jnp.einsum(
        "tk,tke->te", top_w, jax.nn.one_hot(eid, N_EXPERTS, dtype=jnp.float32))
    combine = combine.astype(t.dtype)
    out = jnp.zeros_like(t)
    for e in range(N_EXPERTS):
        act = jax.nn.silu(t @ w1[e]) * (t @ w3[e])
        out = out + combine[:, e:e + 1] * (act @ w2[e])
    return out.reshape(bsz, s, d)

def first_inputs(seed: int = 0) -> dict:
    key = jax.random.key(seed)
    ks = jax.random.split(key, 20)
    f32 = jnp.float32
    nrm = lambda k, shape, scale: jax.random.normal(k, shape, f32) * scale
    L = DEPTH
    return {
        "x": jax.random.normal(ks[0], (BATCH, SEQ, D_MODEL), f32),
        "norm_mix_g": 1.0 + nrm(ks[1], (L, D_MODEL), 0.02),
        "w_in": nrm(ks[2], (L, D_MODEL, D_IN), D_MODEL ** -0.5),
        "conv_a_w": nrm(ks[3], (L, CONV_A_WIDTH, D_A), CONV_A_WIDTH ** -0.5),
        "conv_b_w": nrm(ks[4], (L, CONV_B_WIDTH, D_B), CONV_B_WIDTH ** -0.5),
        "conv_b_bias": nrm(ks[5], (L, D_B), 0.02),
        "ln_b_g": 1.0 + nrm(ks[6], (L, D_B), 0.02),
        "ln_b_b": nrm(ks[7], (L, D_B), 0.02),
        "beta_a": 1.0 + nrm(ks[8], (L, D_A), 0.02),
        "beta_b": 1.0 + nrm(ks[9], (L, D_B), 0.02),
        "w_out": nrm(ks[10], (L, D_MIX, D_MODEL), D_MIX ** -0.5),
        "norm_ffn_g": 1.0 + nrm(ks[11], (L, D_MODEL), 0.02),
        "w_route_group": nrm(ks[12], (L, D_MODEL, N_GROUPS), D_MODEL ** -0.5),
        "b_route_group": nrm(ks[13], (L, N_GROUPS), 0.01),
        "w_route_expert": nrm(ks[14], (L, D_MODEL, N_EXPERTS), D_MODEL ** -0.5),
        "b_route_expert": nrm(ks[15], (L, N_EXPERTS), 0.01),
        "w1": nrm(ks[16], (L, N_EXPERTS, D_MODEL, D_EXPERT), D_MODEL ** -0.5),
        "w3": nrm(ks[17], (L, N_EXPERTS, D_MODEL, D_EXPERT), D_MODEL ** -0.5),
        "w2": nrm(ks[18], (L, N_EXPERTS, D_EXPERT, D_MODEL), D_EXPERT ** -0.5),
        "norm_final_g": 1.0 + nrm(ks[19], (D_MODEL,), 0.02),
    }

def first_block(x, norm_mix_g, w_in, conv_a_w, conv_b_w, conv_b_bias, ln_b_g, ln_b_b,
              beta_a, beta_b, w_out, norm_ffn_g, w_route_group, b_route_group,
              w_route_expert, b_route_expert, w1, w3, w2, norm_final_g):
    for l in range(DEPTH):
        h = rmsnorm(x, norm_mix_g[l])
        x = x + mixer_block(h, w_in[l], conv_a_w[l], conv_b_w[l], conv_b_bias[l],
                            ln_b_g[l], ln_b_b[l], beta_a[l], beta_b[l], w_out[l])
        h = rmsnorm(x, norm_ffn_g[l])
        x = x + hierarchical_moe(h, w_route_group[l], b_route_group[l], w_route_expert[l],
                                 b_route_expert[l], w1[l], w3[l], w2[l])
    return rmsnorm(x, norm_final_g)


DEPTH_2 = 2

HG_HEADS = 4
HG_DK = 128
HG_DV = 128
HG_F = HG_HEADS * HG_DK
HG_V = HG_HEADS * HG_DV
HG_CHUNK = 64
SB_HEADS = 8
SB_DH = 64
SB_W = SB_HEADS * SB_DH
SB_BLOCK = 128
PEER_HEADS = 8
PEER_NKEYS = 128
PEER_N = PEER_NKEYS * PEER_NKEYS
PEER_DKEY = 128
PEER_TOPK = 16
PEER_TOK_BLOCK = 16
DN_ALPHA = (2.0 * DEPTH_2) ** 0.25
DN_BETA = (8.0 * DEPTH_2) ** -0.25
LN_EPS = 1e-5
RMS_EPS = 1e-6
IN_SIZES = (HG_F, HG_F, HG_V, HG_V, SB_W, SB_W, SB_W, D_MODEL, D_MODEL)
IN_WIDTH = sum(IN_SIZES)
IN_SPLITS = tuple(int(s) for s in np.cumsum(IN_SIZES)[:-1])


def layer_norm(x, g, b):
    xf = x.astype(jnp.float32)
    mu = jnp.mean(xf, axis=-1, keepdims=True)
    var = jnp.mean(jnp.square(xf - mu), axis=-1, keepdims=True)
    return (xf - mu) * lax.rsqrt(var + LN_EPS) * g + b

def head_rms_norm(o, g):
    of = o.astype(jnp.float32)
    return of * lax.rsqrt(jnp.mean(jnp.square(of), axis=-1, keepdims=True) + RMS_EPS) * g

def hgrn2_chunkwise(q, f_logit, v, lb):
    B, S, H, DK = q.shape
    DV = v.shape[-1]
    C = HG_CHUNK
    NC = S // C
    q = q.astype(jnp.float32)
    z = f_logit.astype(jnp.float32)
    v = v.astype(jnp.float32)
    lb = lb.reshape(H, DK)
    log_f = jnp.log(lb + (1.0 - lb) * jax.nn.sigmoid(z))
    k = (1.0 - lb) * jax.nn.sigmoid(-z)

    def chunks(a):
        return a.reshape(B, NC, C, H, a.shape[-1]).transpose(1, 0, 3, 2, 4)

    qc, kc, vc, gc = chunks(q), chunks(k), chunks(v), chunks(log_f)
    bc = jnp.cumsum(gc, axis=3)
    tri = jnp.tril(jnp.ones((C, C), dtype=bool))[:, :, None]

    def step(state, inp):
        q_, k_, v_, b_ = inp
        b_end = b_[:, :, -1:, :]
        inter = jnp.einsum('bhtd,bhde->bhte', q_ * jnp.exp(b_), state)
        diff = b_[:, :, :, None, :] - b_[:, :, None, :, :]
        decay = jnp.where(tri, jnp.exp(jnp.where(tri, diff, 0.0)), 0.0)
        scores = jnp.einsum('bhtd,bhsd,bhtsd->bhts', q_, k_, decay)
        intra = jnp.einsum('bhts,bhse->bhte', scores, v_)
        new_state = (jnp.exp(b_end[:, :, 0, :])[..., None] * state
                     + jnp.einsum('bhsd,bhse->bhde', k_ * jnp.exp(b_end - b_), v_))
        return new_state, inter + intra

    state0 = jnp.zeros((B, H, DK, DV), jnp.float32)
    _, o = lax.scan(step, state0, (qc, kc, vc, bc))
    return o.transpose(1, 0, 3, 2, 4).reshape(B, S, H, DV)

def stick_breaking_attention(q, k, v):
    B, S, H, d = q.shape
    scale = 1.0 / math.sqrt(d)
    qh = q.astype(jnp.float32).transpose(0, 2, 1, 3)
    kh = k.astype(jnp.float32).transpose(0, 2, 1, 3)
    vh = v.astype(jnp.float32).transpose(0, 2, 1, 3)
    outs = []
    for blk in range(S // SB_BLOCK):
        t0 = blk * SB_BLOCK
        t1 = t0 + SB_BLOCK
        z = jnp.einsum('bhtd,bhsd->bhts', qh[:, :, t0:t1], kh[:, :, :t1]) * scale
        tpos = t0 + jnp.arange(SB_BLOCK)[:, None]
        spos = jnp.arange(t1)[None, :]
        causal = spos < tpos
        log_1mb = jnp.where(causal, jax.nn.log_sigmoid(-z), 0.0)
        after = lax.cumsum(log_1mb, axis=3, reverse=True) - log_1mb
        w = jnp.where(causal, jnp.exp(jax.nn.log_sigmoid(z) + after), 0.0)
        outs.append(jnp.einsum('bhts,bhsd->bhtd', w, vh[:, :, :t1]))
    o = jnp.concatenate(outs, axis=2)
    return o.transpose(0, 2, 1, 3)

def peer_ffn(h, w_pq, sub_keys, peer_u, peer_v):
    B, S, D = h.shape
    half = PEER_DKEY // 2
    q = (h @ w_pq).reshape(B, S, PEER_HEADS, 2, half).astype(jnp.float32)
    s1 = jnp.einsum('bshd,hnd->bshn', q[..., 0, :], sub_keys[0].astype(jnp.float32))
    s2 = jnp.einsum('bshd,hnd->bshn', q[..., 1, :], sub_keys[1].astype(jnp.float32))
    v1, i1 = lax.top_k(s1, PEER_TOPK)
    v2, i2 = lax.top_k(s2, PEER_TOPK)
    cand = (v1[..., :, None] + v2[..., None, :]).reshape(B, S, PEER_HEADS, PEER_TOPK * PEER_TOPK)
    cand_idx = (i1[..., :, None] * PEER_NKEYS + i2[..., None, :]).reshape(B, S, PEER_HEADS, PEER_TOPK * PEER_TOPK)
    top, pos = lax.top_k(cand, PEER_TOPK)
    idx = jnp.take_along_axis(cand_idx, pos, axis=-1)
    gates = jax.nn.softmax(top, axis=-1)

    T = PEER_TOK_BLOCK
    nb = S // T

    def blockify(a):
        return a.reshape((B, nb, T) + a.shape[2:]).swapaxes(0, 1)

    def expert_block(args):
        hb, ib, gb = args
        u = peer_u[ib]
        act = jax.nn.gelu(jnp.einsum('btd,bthkd->bthk', hb, u), approximate=False)
        return jnp.einsum('bthk,bthkd->btd', gb * act, peer_v[ib])

    out = lax.map(expert_block, (blockify(h), blockify(idx), blockify(gates)))
    return out.swapaxes(0, 1).reshape(B, S, D)

def second_inputs(seed: int = 0) -> dict:
    key = jax.random.key(seed)
    ks = jax.random.split(key, 16)
    nrm = jax.random.normal
    f32 = jnp.float32
    D = D_MODEL
    return {
        "x": nrm(ks[0], (BATCH, SEQ, D), f32),
        "c": nrm(ks[1], (BATCH, D), f32),
        "w_ada": nrm(ks[2], (DEPTH_2, D, 6 * D), f32) * (0.5 * D ** -0.5),
        "b_ada": nrm(ks[3], (DEPTH_2, 6 * D), f32) * 0.01,
        "w_in": nrm(ks[4], (DEPTH_2, D, IN_WIDTH), f32) * D ** -0.5,
        "lb_logits": nrm(ks[5], (DEPTH_2, HG_F), f32) * 0.1,
        "hg_norm_g": 1.0 + 0.02 * nrm(ks[6], (DEPTH_2, HG_V), f32),
        "w_up_a": nrm(ks[7], (DEPTH_2, HG_V, D), f32) * HG_V ** -0.5,
        "w_up_b": nrm(ks[8], (DEPTH_2, SB_W, D), f32) * SB_W ** -0.5,
        "w_o": nrm(ks[9], (DEPTH_2, D, D), f32) * (DN_BETA * D ** -0.5),
        "w_pq": nrm(ks[10], (DEPTH_2, D, PEER_HEADS * PEER_DKEY), f32) * D ** -0.5,
        "sub_keys": nrm(ks[11], (DEPTH_2, 2, PEER_HEADS, PEER_NKEYS, PEER_DKEY // 2), f32) * (PEER_DKEY // 2) ** -0.5,
        "peer_u": nrm(ks[12], (DEPTH_2, PEER_N, D), f32) * D ** -0.5,
        "peer_v": nrm(ks[13], (DEPTH_2, PEER_N, D), f32) * DN_BETA,
        "ln_g": 1.0 + 0.02 * nrm(ks[14], (DEPTH_2, 2, D), f32),
        "ln_b": 0.02 * nrm(ks[15], (DEPTH_2, 2, D), f32),
    }

def second_block(x, c, w_ada, b_ada, w_in, lb_logits, hg_norm_g, w_up_a, w_up_b, w_o,
              w_pq, sub_keys, peer_u, peer_v, ln_g, ln_b):
    B, S, _ = x.shape
    p = jax.nn.softmax(lb_logits.astype(jnp.float32), axis=0)
    lower_bounds = jnp.cumsum(p, axis=0) - p[0:1]
    cond = jax.nn.silu(c)
    for l in range(DEPTH_2):
        mod = cond @ w_ada[l] + b_ada[l]
        sh1, sc1, gt1, sh2, sc2, gt2 = jnp.split(mod, 6, axis=-1)

        hm = x * (1.0 + sc1[:, None]) + sh1[:, None]
        proj = hm @ w_in[l]
        qa, fa, ia, ga, qb, kb, vb, gate_a, gate_b = jnp.split(proj, IN_SPLITS, axis=-1)
        oa = hgrn2_chunkwise(qa.reshape(B, S, HG_HEADS, HG_DK),
                             fa.reshape(B, S, HG_HEADS, HG_DK),
                             ia.reshape(B, S, HG_HEADS, HG_DV),
                             lower_bounds[l])
        oa = head_rms_norm(oa, hg_norm_g[l].reshape(HG_HEADS, HG_DV)).reshape(B, S, HG_V) * jax.nn.silu(ga)
        ob = stick_breaking_attention(qb.reshape(B, S, SB_HEADS, SB_DH),
                                      kb.reshape(B, S, SB_HEADS, SB_DH),
                                      vb.reshape(B, S, SB_HEADS, SB_DH)).reshape(B, S, SB_W)
        merged = jax.nn.sigmoid(gate_a) * (oa @ w_up_a[l]) + jax.nn.sigmoid(gate_b) * (ob @ w_up_b[l])
        y = (merged @ w_o[l]) * gt1[:, None]
        x = layer_norm(DN_ALPHA * x + y, ln_g[l, 0], ln_b[l, 0])

        hf = x * (1.0 + sc2[:, None]) + sh2[:, None]
        y = peer_ffn(hf, w_pq[l], sub_keys[l], peer_u[l], peer_v[l]) * gt2[:, None]
        x = layer_norm(DN_ALPHA * x + y, ln_g[l, 1], ln_b[l, 1])
    return x


def setup_inputs(seed=0):
    out = dict(first_inputs(seed))
    for name, value in second_inputs(seed + 1).items():
        if name != "x":
            out[name + "_2"] = value
    return out


def reference(
    x, norm_mix_g, w_in, conv_a_w, conv_b_w, conv_b_bias, ln_b_g, ln_b_b, beta_a, beta_b, w_out,
    norm_ffn_g, w_route_group, b_route_group, w_route_expert, b_route_expert, w1, w3, w2,
    norm_final_g, c_2, w_ada_2, b_ada_2, w_in_2, lb_logits_2, hg_norm_g_2, w_up_a_2, w_up_b_2,
    w_o_2, w_pq_2, sub_keys_2, peer_u_2, peer_v_2, ln_g_2, ln_b_2,
):
    x = first_block(
        x, norm_mix_g, w_in, conv_a_w, conv_b_w, conv_b_bias, ln_b_g, ln_b_b, beta_a, beta_b,
        w_out, norm_ffn_g, w_route_group, b_route_group, w_route_expert, b_route_expert, w1, w3,
        w2, norm_final_g,
    )
    return second_block(
        x, c_2, w_ada_2, b_ada_2, w_in_2, lb_logits_2, hg_norm_g_2, w_up_a_2, w_up_b_2, w_o_2,
        w_pq_2, sub_keys_2, peer_u_2, peer_v_2, ln_g_2, ln_b_2,
    )


_drawn_inputs = setup_inputs


def setup_inputs(seed=0):
    import zlib

    import numpy as np

    out = dict(_drawn_inputs(seed))
    spreads = {}
    factors = {'ln_b_g': 2.815,
     'ln_b_b': 3.039,
     'beta_a': 2.961,
     'beta_b': 2.81,
     'b_route_group': 28.863,
     'b_route_expert': 14.372,
     'b_ada_2': 4.988,
     'lb_logits_2': 8.0,
     'hg_norm_g_2': 37.703,
     'norm_ffn_g': 3.167}
    for name, (base, spread) in spreads.items():
        noise = np.random.default_rng([zlib.crc32(name.encode()), seed]).standard_normal(out[name].shape)
        drawn = base * np.exp(spread * noise) if base else spread * noise
        out[name] = jnp.asarray(drawn.astype(out[name].dtype))
    for name, factor in factors.items():
        out[name] = (out[name] * factor).astype(out[name].dtype)
    return out
```

```python
from contextlib import ExitStack

import concourse.bass as bass
from concourse import mybir

F32 = mybir.dt.float32
U32 = mybir.dt.uint32
ALU = mybir.AluOpType
ACT = mybir.ActivationFunctionType
AX = mybir.AxisListType

P = 128
D = 1024
S = 256
NT = S // P
DC = D // P
DA = 512
AC = DA // P
TAPS_A, TAPS_B = 3, 31
GROUPS, PER_GROUP = 4, 8
E = GROUPS * PER_GROUP
LAYERS = 2
HG = 4
SB = 8
PH, TOPK = 8, 16
K_ALL = PH * TOPK
PEER_ROWS = P * P
ALPHA = (2.0 * LAYERS) ** 0.25
NEG = -1.0e30

UNIT = 2048
RING = 8
BODY = 4

MIX_UNITS = 10 + 4
MOE_UNITS = 6 * E
ADA_UNITS = 12
ATT_UNITS = 6 + 2 + 4 + 2 + 2 * 6 + 4
PEER_UNITS = 4
LAYER_UNITS = 2 * ADA_UNITS + ATT_UNITS + PEER_UNITS

COLS = {}
_at = 0
for _name, _n in (("norm_mix_g", 8), ("conv_a_w", TAPS_A * 4), ("conv_b_w", TAPS_B * 4), ("conv_b_bias", 4),
                  ("ln_b_g", 4), ("ln_b_b", 4), ("beta_a", 4), ("beta_b", 4), ("norm_ffn_g", 8), ("c_2", 8),
                  ("lb_logits_2", 8), ("hg_norm_g_2", 8)):
    COLS[_name] = _at
    _at += _n
NCOLS = _at

CONSTS = ("ident", "ones", "heads64", "tri", 
          "neg00", "neg01", "neg11", "fill00", "fill01", "fill11") + tuple(f"level{m}" for m in (64, 32, 16, 8, 4, 2, 1))
NCONST = len(CONSTS)


class Signal:

    def __init__(self, sem):
        self.sem, self.base = sem, 0

    def n(self, k):
        return self.sem, self.base + k


class Chain:

    def __init__(self, sem):
        self.sem, self.count = sem, 0

    def link(self, eng, ins):
        self.count += 1
        ins.then_inc(self.sem, 1)
        eng.wait_ge(self.sem, self.count)


def build(nc, dram, out, stop_after=99):
    with ExitStack() as ctx:
        def sb(name, shape, dt=F32, where=ctx):
            return where.enter_context(nc.sbuf_tensor(name, shape, dt))

        def sem(name):
            return ctx.enter_context(nc.semaphore(name))

        signals = {}

        def signal(name):
            if name not in signals:
                signals[name] = Signal(sem(name))
            return signals[name]

        def advance(**made):
            for name, k in made.items():
                signals[name].base += k

        psum = ctx.enter_context(nc.psum_tensor("psum", [P, 8, 512], F32))
        ring = sb("ring", [P, RING, UNIT])
        x_row = sb("x_row", [P, NT, D])
        n_row = sb("n_row", [P, NT, D])
        hT = sb("hT", [P, DC, S])
        const = sb("const", [P, NCONST, P])
        cols = sb("cols", [P, NCOLS])
        stat = sb("stat", [P, 64])
        lb = sb("lb", [P, 4, 4 * LAYERS])
        condb = sb("condb", [P, DC, P])
        C = {name: const[:, i, :] for i, name in enumerate(CONSTS)}
        ident = C["ident"]

        def col(name, k=0, n=1):
            return cols[:, COLS[name] + k:COLS[name] + k + n]

        loaded = sem("loaded")
        w_land = [sem(f"w_land{s}") for s in range(RING)]
        w_used = sem("w_used")
        dve_chain, act_chain, pool_chain = Chain(sem("dve_chain")), Chain(sem("act_chain")), Chain(sem("pool_chain"))

        stream = []
        stream += [dram["w_in"][u] for u in range(10)] + [dram["w_out"][u] for u in range(4)]
        moe_at = len(stream)

        def moe_up(e):
            return [dram[w][e, half] for half in range(2) for w in ("w1", "w3")]

        def moe_down(e):
            return [dram["w2"][e, half] for half in range(2)]

        stream += moe_up(0)
        for e in range(E - 1):
            stream += moe_up(e + 1) + moe_down(e)
        stream += moe_down(E - 1)
        layer_at = []
        for l in range(LAYERS):
            layer_at.append(len(stream))
            win = dram["w_in_2"][l]
            stream += [dram["w_ada_2"][l, u] for u in range(12)]
            stream += [win[u] for u in (2, 3, 0, 1, 6, 7)]
            stream += [win[u] for u in (4, 5)]
            stream += [win[u] for u in (8, 9, 10, 11)]
            stream += [win[u] for u in (12, 13)]
            for q in range(2):
                stream += [win[u] for u in (14 + 2 * q, 15 + 2 * q, 18 + 2 * q, 19 + 2 * q)]
                stream += [dram["w_up_a_2"][l, q], dram["w_up_b_2"][l, q]]
            stream += [dram["w_o_2"][l, u] for u in range(4)]
            stream += [dram["w_ada_2"][l, 12 + u] for u in range(12)]
            stream += [dram["w_pq_2"][l, u] for u in range(4)]
        assert moe_at == MIX_UNITS and layer_at[0] == MIX_UNITS + MOE_UNITS
        assert len(stream) == layer_at[0] + LAYERS * LAYER_UNITS
        issued = [0]

        def load_unit(sp, u):
            if u >= RING:
                sp.wait_ge(w_used, u - RING + 1)
            sp.dma_start(ring[:, u % RING, :], stream[u]).then_inc(w_land[u % RING], 16)

        def load_until(sp, end):
            for u in range(issued[0], min(end + RING, len(stream))):
                load_unit(sp, u)
            issued[0] = min(end + RING, len(stream))

        def unit(pe, u):
            pe.wait_ge(w_land[u % RING], 16 * (u // RING + 1))
            return ring[:, u % RING, :]

        def pe_transpose(pe, src, ready, done, free=None):
            pe.wait_ge(*ready)
            for b in range(4):
                if free is not None:
                    pe.wait_ge(*free)
                for c in (2 * b, 2 * b + 1):
                    for i in range(NT):
                        at = (c % 2) * S + i * P
                        ins = pe.transpose(psum[:, b, at:at + P], src[:, i, c * P:(c + 1) * P], ident)
                ins.then_inc(done.sem, 1)


        def mixer():
            ph = ExitStack()
            projT = sb("mix_projT", [P, 20, S], where=ph)
            PA, PB = TAPS_A // 2, TAPS_B // 2
            ua = sb("mix_ua", [P, AC, S + 2 * PA], where=ph)
            ub = sb("mix_ub", [P, AC, S + 2 * PB], where=ph)
            sq = sb("mix_sq", [P, 2, AC * S], where=ph)
            yT = sb("mix_yT", [P, 2 * AC, S], where=ph)
            tmp = sb("mix_tmp", [P, AC * S], where=ph)
            ssum = signal("squares_summed")
            meansq = signal("mean_squares")
            rooted = signal("rooted")
            normed = signal("rows_normed")
            turned = signal("turned")
            turned_used = signal("turned_used")
            hT_done = signal("hT_done")
            proj = signal("proj_done")
            proj_out = signal("proj_copied")
            sig_in = signal("sig_in")
            sig = signal("sig_done")
            stat_in = signal("stat_in")
            stat_out = signal("stat_out")
            y_ready = signal("y_ready")
            y_out = signal("y_out")
            y3, t3 = yT[:, :, :], tmp[:, :].rearrange("p (c s) -> p c s", c=AC)

            with nc.Block() as block:
                @block.sync
                def _(sp):
                    for name, dst in (("x", x_row[:, :, :]), ("consts", const[:, :, :]), ("cols", cols[:, :])):
                        sp.dma_start(dst, dram[name]).then_inc(loaded, 16)
                    load_until(sp, MIX_UNITS)

                @block.scalar
                def _(act):
                    act.wait_ge(loaded, 48)
                    for i in range(NT):
                        act.activation(sq[:, i, :], x_row[:, i, :], ACT.Square,
                                       accum_out=stat[:, i:i + 1]).then_inc(ssum.sem, 1)
                    act.wait_ge(*meansq.n(1))
                    act.activation(stat[:, 2:4], stat[:, 2:4], ACT.Sqrt).then_inc(rooted.sem, 1)
                    act.wait_ge(*proj_out.n(10))
                    act.activation(projT[:, 16:20, :], projT[:, 16:20, :], ACT.Sigmoid).then_inc(sig.sem, 1)
                    act.wait_ge(*meansq.n(2))
                    act.activation(tmp[:, 0:S], tmp[:, 0:S], ACT.Sqrt).then_inc(rooted.sem, 1)
                    act.wait_ge(*sig_in.n(1))
                    act.activation(projT[:, 0:AC, :], yT[:, AC:2 * AC, :], ACT.Sigmoid).then_inc(sig.sem, 1)
                    act.wait_ge(*meansq.n(3))
                    act.activation(sq[:, :, :], sq[:, :, :], ACT.Sqrt).then_inc(rooted.sem, 1)

                @block.tensor
                def _(pe):
                    pe_transpose(pe, n_row, normed.n(NT), turned)
                    pe.wait_ge(*hT_done.n(4))
                    for u in range(10):
                        w = unit(pe, u).rearrange("p (c n) -> p c n", c=DC)
                        if u >= 4:
                            pe.wait_ge(*proj_out.n(u - 3))
                        for j in range(2):
                            for c in range(DC):
                                ins = pe.matmul(psum[:, 4 + u % 4, j * S:(j + 1) * S], w[:, c, j * P:(j + 1) * P],
                                                hT[:, c, :], start=(c == 0), stop=(c == DC - 1))
                            if j == 1:
                                ins.then_inc(w_used, 1)
                    pe.wait_ge(*stat_in.n(1))
                    for c in range(AC):
                        ins = pe.matmul(psum[:, 0, 0:S], C["ones"], ub[:, c, 0:S], start=(c == 0), stop=(c == AC - 1))
                    ins.then_inc(stat_out.sem, 1)
                    pe.wait_ge(*stat_in.n(2))
                    for c in range(AC):
                        ins = pe.matmul(psum[:, 1, 0:S], C["ones"], t3[:, c, :], start=(c == 0), stop=(c == AC - 1))
                    ins.then_inc(stat_out.sem, 1)
                    pe.wait_ge(*stat_in.n(3))
                    for b in range(4):
                        ins = pe.matmul(psum[:, b, :], C["heads64"], sq[:, b // 2, (b % 2) * 512:(b % 2) * 512 + 512],
                                        start=True, stop=True)
                    ins.then_inc(stat_out.sem, 1)
                    pe.wait_ge(*y_ready.n(1))
                    for k in range(4):
                        w = unit(pe, 10 + k).rearrange("p (c n) -> p c n", c=2)
                        for cc in range(2):
                            for i in range(NT):
                                for h in range(2):
                                    ins = pe.matmul(psum[:, 4 + 2 * i + h, :], yT[:, 2 * k + cc, i * P:(i + 1) * P],
                                                    w[:, cc, h * 512:(h + 1) * 512],
                                                    start=(k == 0 and cc == 0), stop=(k == 3 and cc == 1))
                        ins.then_inc(w_used, 1)

                @block.gpsimd
                def _(pool):
                    pool.memset(ua[:, :, :], 0.0)
                    pool.memset(ub[:, :, :], 0.0).then_inc(signal("pads_zero").sem, 1)

                @block.vector
                def _(dve):
                    link = lambda ins: dve_chain.link(dve, ins)
                    dve.wait_ge(*ssum.n(NT))
                    dve.tensor_scalar(stat[:, 2:4], stat[:, 0:2], 1.0 / D, 1e-6, ALU.mult, ALU.add).then_inc(meansq.sem, 1)
                    dve.wait_ge(*rooted.n(1))
                    link(dve.reciprocal(stat[:, 4:6], stat[:, 2:4]))
                    for i in range(NT):
                        dve.tensor_scalar(n_row[:, i, :], x_row[:, i, :], stat[:, 4 + i:5 + i], None,
                                          ALU.mult).then_inc(normed.sem, 1)
                    for b in range(4):
                        dve.wait_ge(*turned.n(b + 1))
                        dve.tensor_scalar(hT[:, 2 * b, :], psum[:, b, 0:S], col("norm_mix_g", 2 * b), None, ALU.mult)
                        dve.tensor_scalar(hT[:, 2 * b + 1, :], psum[:, b, S:2 * S], col("norm_mix_g", 2 * b + 1), None,
                                          ALU.mult).then_inc(hT_done.sem, 1)
                    for u in range(10):
                        dve.wait_ge(w_used, u + 1)
                        dve.tensor_copy(projT[:, 2 * u:2 * u + 2, :],
                                        psum[:, 4 + u % 4, :].rearrange("p (j s) -> p j s", j=2)).then_inc(proj_out.sem, 1)
                    dve.wait_ge(*proj_out.n(10))
                    dve.wait_ge(*signal("pads_zero").n(1))
                    link(dve.tensor_tensor(ua[:, :, PA:PA + S], projT[:, 8:12, :], projT[:, 0:4, :], ALU.mult))
                    for c in range(AC):
                        ins = dve.tensor_scalar(yT[:, c, :], ua[:, c, 0:S], col("conv_a_w", c), None, ALU.mult)
                    link(ins)
                    for j in range(1, TAPS_A):
                        for c in range(AC):
                            ins = dve.scalar_tensor_tensor(out=yT[:, c, :], in0=ua[:, c, j:j + S],
                                                           scalar=col("conv_a_w", j * AC + c), in1=yT[:, c, :],
                                                           op0=ALU.mult, op1=ALU.add)
                        link(ins)
                    link(dve.tensor_tensor(yT[:, 0:AC, :], yT[:, 0:AC, :], projT[:, 4:8, :], ALU.mult))
                    dve.wait_ge(*sig.n(1))
                    link(dve.tensor_tensor(ub[:, :, PB:PB + S], projT[:, 12:16, :], projT[:, 16:20, :], ALU.mult))
                    for c in range(AC):
                        ins = dve.tensor_scalar(yT[:, AC + c, :], ub[:, c, 0:S], col("conv_b_w", c), col("conv_b_bias", c),
                                                ALU.mult, ALU.add)
                    tap = signal("tap")
                    ins.then_inc(tap.sem, 1)
                    with dve.Fori(1, TAPS_B) as j:
                        dve.wait_ge(tap.sem, tap.base + j)
                        for c in range(AC):
                            ins = dve.scalar_tensor_tensor(
                                out=yT[:, AC + c, :], in0=ub[:, c, bass.ds(j, S)],
                                scalar=cols[:, bass.ds(j * AC + (COLS["conv_b_w"] + c), 1)],
                                in1=yT[:, AC + c, :], op0=ALU.mult, op1=ALU.add)
                        ins.then_inc(tap.sem, 1)
                    dve.wait_ge(*tap.n(TAPS_B))
                    yb = yT[:, AC:2 * AC, :]
                    dve.tensor_copy(ub[:, :, 0:S], yb).then_inc(stat_in.sem, 1)
                    dve.wait_ge(*stat_out.n(1))
                    link(dve.tensor_scalar(stat_mean, psum[:, 0, 0:S], 1.0 / DA, None, ALU.mult))
                    mean4 = stat_mean.unsqueeze(1).broadcast_to((P, AC, S))
                    link(dve.tensor_tensor(yb, yb, mean4, ALU.subtract))
                    dve.tensor_tensor(t3, yb, yb, ALU.mult).then_inc(stat_in.sem, 1)
                    dve.wait_ge(*stat_out.n(2))
                    dve.tensor_scalar(tmp[:, 0:S], psum[:, 1, 0:S], 1.0 / DA, 1e-6, ALU.mult, ALU.add).then_inc(meansq.sem, 1)
                    dve.wait_ge(*rooted.n(2))
                    link(dve.reciprocal(stat_mean, tmp[:, 0:S]))
                    link(dve.tensor_tensor(yb, yb, mean4, ALU.mult))
                    for c in range(AC):
                        ins = dve.tensor_scalar(yT[:, AC + c, :], yT[:, AC + c, :], col("ln_b_g", c), col("ln_b_b", c),
                                                ALU.mult, ALU.add)
                    ins.then_inc(sig_in.sem, 1)
                    dve.wait_ge(*sig_in.n(1))
                    dve.wait_ge(*sig.n(2))
                    link(dve.tensor_tensor(yb, yb, projT[:, 0:AC, :], ALU.mult))
                    sq8 = sq[:, :, :].rearrange("p b (c s) -> p (b c) s", c=AC)
                    dve.tensor_tensor(sq8, y3, y3, ALU.mult).then_inc(stat_in.sem, 1)
                    dve.wait_ge(*stat_out.n(3))
                    dve.tensor_scalar(sq[:, :, :].rearrange("p b (c s) -> p (b c) s", c=2), psum[:, 0:4, :],
                                      1.0 / 64, 1e-6, ALU.mult, ALU.add).then_inc(meansq.sem, 1)
                    dve.wait_ge(*rooted.n(3))
                    link(dve.reciprocal(sq8, sq8))
                    for c in range(2 * AC):
                        ins = dve.scalar_tensor_tensor(out=yT[:, c, :], in0=yT[:, c, :],
                                                       scalar=col("beta_a" if c < AC else "beta_b", c % AC),
                                                       in1=sq8[:, c, :], op0=ALU.mult, op1=ALU.mult)
                    ins.then_inc(y_ready.sem, 1)
                    dve.wait_ge(w_used, MIX_UNITS)
                    for i in range(NT):
                        dve.tensor_tensor(x_row[:, i, :].rearrange("p (h n) -> p h n", h=2), psum[:, 4 + 2 * i:6 + 2 * i, :],
                                          x_row[:, i, :].rearrange("p (h n) -> p h n", h=2), ALU.add)
            advance(squares_summed=NT, mean_squares=3, rooted=3, rows_normed=NT, turned=4, hT_done=4)
            ph.close()

        mean_buf = sb("mean_buf", [P, S])
        mod = sb("mod", [P, 3 * D])
        stat_mean = mean_buf[:, :]
        mixer()
        if stop_after <= 1:
            return

        def moe():
            ph = ExitStack()
            actT = sb("moe_actT", [P, 2, 4, S], where=ph)
            sg = sb("moe_sg", [P, 2, 2, S], where=ph)
            combine = sb("moe_combine", [P, NT, E], where=ph)
            wr = sb("moe_wr", [P, DC, GROUPS + E], where=ph)
            br = sb("moe_br", [P, GROUPS + E], where=ph)
            lg = sb("moe_lg", [P, NT, GROUPS + E], where=ph)
            pg = sb("moe_pg", [P, 8], where=ph)
            le = sb("moe_le", [P, 8], where=ph)
            top = sb("moe_top", [P, 2, 8], where=ph)
            topi = sb("moe_topi", [P, 2, 8], U32, where=ph)
            idf = sb("moe_idf", [P, 2, 8], where=ph)
            oh = sb("moe_oh", [P, 3, 8], where=ph)
            iota8 = sb("moe_iota8", [P, 8], where=ph)
            sm = sb("moe_sm", [P, 16], where=ph)
            junk = sb("moe_junk", [P, D], where=ph)
            gfin = sb("moe_gfin", [P, D], where=ph)
            ssum, meansq, rooted, normed = (signal(n) for n in ("squares_summed", "mean_squares", "rooted", "rows_normed"))
            turned, hT_done = signal("turned"), signal("hT_done")
            small = signal("router_loaded")
            logits = signal("logits")
            rt_in, rt_out = signal("route_exp_in"), signal("route_exp")
            sigm, acted, summed = (signal(n) for n in ("sigmoid_done", "act_done", "down_summed"))

            u0 = moe_at

            def up_done(e, half):
                return w_used, u0 + 2 * half + 2 if isinstance(e, int) and e == 0 else e * 6 + (u0 + 2 * half)

            def down_done(e):
                return w_used, u0 + MOE_UNITS if isinstance(e, int) and e == E - 1 else e * 6 + (u0 + 10)

            with nc.Block() as block:
                @block.sync
                def _(sp):
                    for dst, src in ((wr[:, :, :], dram["w_route"]), (br[:, :], dram["b_route"]),
                                     (iota8[:, :], dram["iota"][:, 0:8]), (gfin[:, :], dram["norm_final_g"])):
                        sp.dma_start(dst, src).then_inc(small.sem, 16)
                    load_until(sp, u0 + 4 + 6 * BODY - RING)
                    turns = (E - 1) // BODY
                    with sp.Fori(1, turns) as i:
                        u = 4
                        for k in range(BODY):
                            parts = [(dram[w], i * BODY + (k + 1), half) for half in range(2) for w in ("w1", "w3")]
                            parts += [(dram["w2"], i * BODY + k, half) for half in range(2)]
                            for src, e, half in parts:
                                at = u0 + u
                                sp.wait_ge(w_used, i * (6 * BODY) + (at - RING + 1))
                                sp.dma_start(ring[:, at % RING, :], src[e, half]).then_inc(w_land[at % RING], 16)
                                u += 1
                    issued[0] = u0 + 4 + 6 * BODY * turns
                    load_until(sp, u0 + MOE_UNITS)

                @block.scalar
                def _(act):
                    for i in range(NT):
                        act.activation(junk[:, :], x_row[:, i, :], ACT.Square,
                                       accum_out=stat[:, i:i + 1]).then_inc(ssum.sem, 1)
                        act.wait_ge(*ssum.n(i + 1))
                    act.wait_ge(*meansq.n(1))
                    act.activation(stat[:, 2:4], stat[:, 2:4], ACT.Sqrt).then_inc(rooted.sem, 1)
                    for i in range(NT):
                        act.wait_ge(*rt_in.n(2 * i + 1))
                        act.activation(pg[:, 0:GROUPS], pg[:, 0:GROUPS], ACT.Exp, accum_out=sm[:, 0:1]).then_inc(rt_out.sem, 1)
                        act.wait_ge(*rt_in.n(2 * i + 2))
                        act.activation(le[:, :], le[:, :], ACT.Exp, accum_out=sm[:, 1:2]).then_inc(rt_out.sem, 1)

                    def sigmoids(e, k):
                        for half in range(2):
                            act.wait_ge(*up_done(e, half))
                            if k is None or k > 0:
                                act.wait_ge(*acted.n(e * 2 + (half - 1)))
                            act.activation(sg[:, half, :, :], psum[:, half, :].rearrange("p (j s) -> p j s", j=2),
                                           ACT.Sigmoid).then_inc(sigm.sem, 1)
                    sigmoids(0, 0)
                    with act.Fori(1, E) as e:
                        sigmoids(e, None)
                    act.wait_ge(*summed.n(NT * E))
                    for i in range(NT):
                        act.activation(junk[:, :], x_row[:, i, :], ACT.Square,
                                       accum_out=stat[:, i:i + 1]).then_inc(ssum.sem, 1)
                        act.wait_ge(*ssum.n(NT + i + 1))
                    act.wait_ge(*meansq.n(2))
                    act.activation(stat[:, 2:4], stat[:, 2:4], ACT.Sqrt).then_inc(rooted.sem, 1)

                @block.tensor
                def _(pe):
                    pe_transpose(pe, n_row, normed.n(NT), turned)
                    pe.wait_ge(small.sem, 64)
                    pe.wait_ge(*hT_done.n(4))
                    for i in range(NT):
                        for c in range(DC):
                            ins = pe.matmul(psum[:, 4 + i, 0:GROUPS + E], hT[:, c, i * P:(i + 1) * P], wr[:, c, :],
                                            start=(c == 0), stop=(c == DC - 1))
                        ins.then_inc(logits.sem, 1)

                    def project_up(e, at, turn):
                        for half in range(2):
                            if turn is not None or at > u0:
                                pe.wait_ge(*acted.n(e * 2 + (half - 1)))
                            for w in range(2):
                                v = at + 2 * half + w
                                land = 16 * (v // RING + 1)
                                pe.wait_ge(w_land[v % RING], land if turn is None else turn * (16 * 6 * BODY // RING) + land)
                                wt = ring[:, v % RING, :].rearrange("p (c n) -> p c n", c=DC)
                                for j in range(2):
                                    for c in range(DC):
                                        ins = pe.matmul(psum[:, 2 * w + half, j * S:(j + 1) * S],
                                                        wt[:, c, j * P:(j + 1) * P], hT[:, c, :],
                                                        start=(c == 0), stop=(c == DC - 1))
                                ins.then_inc(w_used, 1)

                    def project_down(e, par, at, turn, first):
                        pe.wait_ge(*acted.n(e * 2 + 2))
                        if not first:
                            pe.wait_ge(*summed.n(e * NT))
                        for half in range(2):
                            v = at + half
                            land = 16 * (v // RING + 1)
                            pe.wait_ge(w_land[v % RING], land if turn is None else turn * (16 * 6 * BODY // RING) + land)
                            wt = ring[:, v % RING, :].rearrange("p (c n) -> p c n", c=2)
                            for cc in range(2):
                                for i in range(NT):
                                    for h in range(2):
                                        j = 2 * half + cc
                                        ins = pe.matmul(psum[:, 4 + 2 * i + h, :], actT[:, par, j, i * P:(i + 1) * P],
                                                        wt[:, cc, h * 512:(h + 1) * 512],
                                                        start=(j == 0), stop=(j == 3))
                            ins.then_inc(w_used, 1)

                    project_up(0, u0, None)
                    turns = (E - 1) // BODY
                    for k in range(BODY):
                        at = u0 + 4 + 6 * k
                        project_up(k + 1, at, None)
                        project_down(k, k % 2, at + 4, None, k == 0)
                    with pe.Fori(1, turns) as t:
                        for k in range(BODY):
                            at = u0 + 4 + 6 * k
                            project_up(t * BODY + (k + 1), at, t)
                            project_down(t * BODY + k, k % 2, at + 4, t, False)
                    for e in range(turns * BODY, E):
                        at = u0 + 4 + 6 * e
                        if e + 1 < E:
                            project_up(e + 1, at, None)
                            at += 4
                        project_down(e, e % 2, at, None, False)

                @block.vector
                def _(dve):
                    link = lambda ins: dve_chain.link(dve, ins)
                    dve.wait_ge(*ssum.n(NT))
                    dve.tensor_scalar(stat[:, 2:4], stat[:, 0:2], 1.0 / D, 1e-6, ALU.mult, ALU.add).then_inc(meansq.sem, 1)
                    dve.wait_ge(*rooted.n(1))
                    link(dve.reciprocal(stat[:, 4:6], stat[:, 2:4]))
                    for i in range(NT):
                        dve.tensor_scalar(n_row[:, i, :], x_row[:, i, :], stat[:, 4 + i:5 + i], None,
                                          ALU.mult).then_inc(normed.sem, 1)
                    for b in range(4):
                        dve.wait_ge(*turned.n(b + 1))
                        dve.tensor_scalar(hT[:, 2 * b, :], psum[:, b, 0:S], col("norm_ffn_g", 2 * b), None, ALU.mult)
                        dve.tensor_scalar(hT[:, 2 * b + 1, :], psum[:, b, S:2 * S], col("norm_ffn_g", 2 * b + 1), None,
                                          ALU.mult).then_inc(hT_done.sem, 1)
                    dve.wait_ge(small.sem, 64)
                    for i in range(NT):
                        dve.wait_ge(*logits.n(i + 1))
                        link(dve.tensor_tensor(lg[:, i, :], psum[:, 4 + i, 0:GROUPS + E], br[:, :], ALU.add))
                        link(dve.memset(pg[:, :], -1.0))
                        link(dve.tensor_reduce(sm[:, 2:3], lg[:, i, 0:GROUPS], AX.X, ALU.max))
                        dve.tensor_scalar(pg[:, 0:GROUPS], lg[:, i, 0:GROUPS], sm[:, 2:3], None,
                                          ALU.subtract).then_inc(rt_in.sem, 1)
                        dve.wait_ge(*rt_out.n(2 * i + 1))
                        link(dve.reciprocal(sm[:, 3:4], sm[:, 0:1]))
                        link(dve.tensor_scalar(pg[:, 0:GROUPS], pg[:, 0:GROUPS], sm[:, 3:4], None, ALU.mult))
                        link(dve.max(top[:, 0, :], pg[:, :]))
                        link(dve.max_index(topi[:, 0, :], top[:, 0, :], pg[:, :]))
                        link(dve.tensor_copy(idf[:, 0, :], topi[:, 0, :]))
                        link(dve.tensor_scalar(oh[:, 0, :], iota8[:, :], idf[:, 0, 0:1], None, ALU.is_equal))
                        link(dve.tensor_scalar(le[:, :], lg[:, i, GROUPS:GROUPS + 8], oh[:, 0, 0:1], None, ALU.mult))
                        for g in range(1, GROUPS):
                            link(dve.scalar_tensor_tensor(out=le[:, :], in0=lg[:, i, GROUPS + 8 * g:GROUPS + 8 * g + 8],
                                                          scalar=oh[:, 0, g:g + 1], in1=le[:, :], op0=ALU.mult, op1=ALU.add))
                        link(dve.tensor_reduce(sm[:, 4:5], le[:, :], AX.X, ALU.max))
                        dve.tensor_scalar(le[:, :], le[:, :], sm[:, 4:5], None, ALU.subtract).then_inc(rt_in.sem, 1)
                        dve.wait_ge(*rt_out.n(2 * i + 2))
                        link(dve.reciprocal(sm[:, 5:6], sm[:, 1:2]))
                        link(dve.tensor_scalar(le[:, :], le[:, :], sm[:, 5:6], None, ALU.mult))
                        link(dve.max(top[:, 1, :], le[:, :]))
                        link(dve.max_index(topi[:, 1, :], top[:, 1, :], le[:, :]))
                        link(dve.tensor_copy(idf[:, 1, :], topi[:, 1, :]))
                        link(dve.tensor_tensor(sm[:, 6:7], top[:, 1, 0:1], top[:, 1, 1:2], ALU.add))
                        link(dve.reciprocal(sm[:, 7:8], sm[:, 6:7]))
                        link(dve.tensor_tensor(sm[:, 8:9], sm[:, 7:8], top[:, 0, 0:1], ALU.mult))
                        link(dve.tensor_scalar(sm[:, 9:11], top[:, 1, 0:2], sm[:, 8:9], None, ALU.mult))
                        for k in range(2):
                            link(dve.tensor_scalar(oh[:, 1 + k, :], iota8[:, :], idf[:, 1, k:k + 1], sm[:, 9 + k:10 + k],
                                                   ALU.is_equal, ALU.mult))
                        link(dve.tensor_tensor(oh[:, 1, :], oh[:, 1, :], oh[:, 2, :], ALU.add))
                        for g in range(GROUPS):
                            link(dve.tensor_scalar(combine[:, i, 8 * g:8 * g + 8], oh[:, 1, :], oh[:, 0, g:g + 1], None,
                                                   ALU.mult))

                    def hidden(e, par):
                        for half in range(2):
                            two = lambda b: psum[:, b, :].rearrange("p (j s) -> p j s", j=2)
                            dve.wait_ge(*sigm.n(e * 2 + (half + 1)))
                            dve.tensor_tensor(sg[:, half, :, :], sg[:, half, :, :], two(half), ALU.mult).then_inc(gated.sem, 1)
                            dve.wait_ge(*gated.n(e * 2 + (half + 1)))
                            dve.tensor_tensor(actT[:, par, 2 * half:2 * half + 2, :], sg[:, half, :, :], two(2 + half),
                                              ALU.mult).then_inc(acted.sem, 1)

                    def add_expert(e, weight):
                        dve.wait_ge(*down_done(e))
                        for i in range(NT):
                            xr = x_row[:, i, :].rearrange("p (h n) -> p h n", h=2)
                            dve.scalar_tensor_tensor(out=xr, in0=psum[:, 4 + 2 * i:6 + 2 * i, :], scalar=weight(i), in1=xr,
                                                     op0=ALU.mult, op1=ALU.add).then_inc(summed.sem, 1)

                    gated = signal("gated")
                    hidden(0, 0)
                    hidden(1, 1)
                    add_expert(0, lambda i: combine[:, i, 0:1])
                    with dve.Fori(1, E // 2) as t:
                        for k in range(2):
                            hidden(t * 2 + k, k)
                            e = t * 2 + (k - 1)
                            add_expert(e, lambda i: combine[:, i, bass.ds(e, 1)])
                    add_expert(E - 1, lambda i: combine[:, i, E - 1:E])
                    dve.wait_ge(*ssum.n(2 * NT))
                    dve.tensor_scalar(stat[:, 2:4], stat[:, 0:2], 1.0 / D, 1e-6, ALU.mult, ALU.add).then_inc(meansq.sem, 1)
                    dve.wait_ge(*rooted.n(2))
                    link(dve.reciprocal(stat[:, 4:6], stat[:, 2:4]))
                    for i in range(NT):
                        dve.scalar_tensor_tensor(out=x_row[:, i, :], in0=x_row[:, i, :], scalar=stat[:, 4 + i:5 + i],
                                                 in1=gfin[:, :], op0=ALU.mult, op1=ALU.mult)
            advance(squares_summed=2 * NT, mean_squares=2, rooted=2, rows_normed=NT, turned=4, hT_done=4)
            ph.close()

        moe()
        if stop_after <= 2:
            return

        def ada_pe(pe, u):
            for k in range(ADA_UNITS):
                w = unit(pe, u + k).rearrange("p (c n) -> p c n", c=DC)
                if k >= 4:
                    pe.wait_ge(*signal("mod_added").n(k - 3))
                for c in range(DC):
                    ins = pe.matmul(psum[:, k % 4, 0:S], condb[:, c, :], w[:, c, :], start=(c == 0), stop=(c == DC - 1))
                ins.then_inc(w_used, 1)

        def ada_dve(dve, u, bias_landed):
            dve.wait_ge(*bias_landed)
            added = signal("mod_added")
            for k in range(ADA_UNITS):
                dve.wait_ge(w_used, u + k + 1)
                dve.tensor_tensor(mod[:, k * S:(k + 1) * S], mod[:, k * S:(k + 1) * S], psum[:, k % 4, 0:S],
                                  ALU.add).then_inc(added.sem, 1)
            dve.wait_ge(*added.n(ADA_UNITS))
            dve_chain.link(dve, dve.tensor_scalar(mod[:, D:2 * D], mod[:, D:2 * D], 1.0, None, ALU.add))
            for i in range(NT):
                ins = dve.tensor_tensor(n_row[:, i, :], x_row[:, i, :], mod[:, D:2 * D], ALU.mult)
            dve_chain.link(dve, ins)
            for i in range(NT):
                dve.tensor_tensor(n_row[:, i, :], n_row[:, i, :], mod[:, 0:D],
                                  ALU.add).then_inc(signal("rows_normed").sem, 1)

        def turn_copies(act):
            for b in range(4):
                act.wait_ge(*signal("turned").n(b + 1))
                act.activation(hT[:, 2 * b:2 * b + 2, :], psum[:, b, :].rearrange("p (j s) -> p j s", j=2),
                               ACT.Copy).then_inc(signal("hT_done").sem, 1)

        def residual_norm_dve(dve, banks, gb, gb_landed, root):
            link = lambda ins: dve_chain.link(dve, ins)
            for i in range(NT):
                ins = dve.tensor_tensor(n_row[:, i, :].rearrange("p (h n) -> p h n", h=2),
                                        psum[:, banks + 2 * i:banks + 2 * i + 2, :],
                                        mod[:, 2 * D:3 * D].rearrange("p (h n) -> p h n", h=2), ALU.mult)
            link(ins)
            for i in range(NT):
                ins = dve.scalar_tensor_tensor(out=x_row[:, i, :], in0=x_row[:, i, :], scalar=float(ALPHA),
                                               in1=n_row[:, i, :], op0=ALU.mult, op1=ALU.add)
            link(ins)
            for i in range(NT):
                for h in range(2):
                    ins = dve.bn_stats(stat[:, 16 + 12 * i + 6 * h:22 + 12 * i + 6 * h], x_row[:, i, h * 512:(h + 1) * 512])
            link(ins)
            for i in range(NT):
                ins = dve.bn_aggr(stat[:, 8 + 2 * i:10 + 2 * i], stat[:, 16 + 12 * i:28 + 12 * i])
            link(ins)
            var = stat[:, 8:12].rearrange("p (i k) -> p i k", k=2)[:, :, 1]
            dve.tensor_scalar(stat[:, 2:4], var, 1e-5, None, ALU.add).then_inc(signal("mean_squares").sem, 1)
            dve.wait_ge(*signal("rooted").n(root))
            link(dve.reciprocal(stat[:, 4:6], stat[:, 2:4]))
            for i in range(NT):
                ins = dve.tensor_scalar(x_row[:, i, :], x_row[:, i, :], stat[:, 8 + 2 * i:9 + 2 * i], stat[:, 4 + i:5 + i],
                                        ALU.subtract, ALU.mult)
            link(ins)
            dve.wait_ge(*gb_landed)
            for i in range(NT):
                ins = dve.tensor_tensor(x_row[:, i, :], x_row[:, i, :], gb[:, 0, :], ALU.mult)
            link(ins)
            for i in range(NT):
                ins = dve.tensor_tensor(x_row[:, i, :], x_row[:, i, :], gb[:, 1, :], ALU.add)
            return ins

        def attention(l):
            ph = ExitStack()
            projT = sb(f"att{l}_projT", [P, 20, S], where=ph)
            v_row = sb(f"att{l}_v_row", [P, 2, NT, 512], where=ph)
            hg = sb(f"att{l}_hg", [P, 8, 4 * S], where=ph)
            scT = sb(f"att{l}_scT", [P, 3, HG, P], where=ph)
            oT = sb(f"att{l}_oT", [P, 2, 4, S], where=ph)
            gb = sb(f"att{l}_gb", [P, 2, D], where=ph)
            u0 = layer_at[l]
            uq = u0 + ADA_UNITS
            um = uq + 14
            uo = um + 12
            end = uo + 4
            fa, qa, ga, qb, kb = (projT[:, 4 * n:4 * n + 4, :] for n in range(5))
            kT, bufA, bufB = (hg[:, n, :] for n in range(3))
            dec = [hg[:, 1, :], hg[:, 3, :]]
            qd = [hg[:, 4, :], hg[:, 5, :]]
            kd = [hg[:, 6, :], hg[:, 7, :]]
            heads = lambda a: a.rearrange("p (h s) -> p h s", h=HG)
            small = signal("layer_small")
            (turned, hT_done, normed, proj_out, gates_exp, logf_in, logf, d_in, decay, q_dec, k_dec, lvl, lvl_used, meansq,
             rooted, o_done, osq, oss, sg_done, z_done, soft, logs, inc, w_in, w_done, ob_done, ob_out, o_ready, gsig,
             merged, lbs) = (signal(n) for n in (
                 "turned", "hT_done", "rows_normed", "att_proj_copied", "forget_exps", "forget_in", "forget_log",
                 "decay_in", "decay", "q_decayed", "k_decayed", "level_products", "level_kept", "mean_squares", "rooted",
                 "hgrn_out", "hgrn_squares", "hgrn_sums", "silu_gate", "stick_z", "stick_soft", "stick_logs", "stick_sums",
                 "stick_w_in", "stick_w", "stick_out", "stick_copied", "heads_ready", "gates_sigmoid", "merged", "bounds"))
            sa, ls, wt = (hg[:, n, 0:768].rearrange("p (b n) -> p b n", b=2) for n in (2, 3, 6))
            mT = hg[:, 0:2, :].rearrange("p a (c s) -> p (a c) s", c=4)
            gate_sig = heads(hg[:, 4, :])
            LEVELS = (128, 64, 32, 16, 8, 4, 2, 1, 0)

            with nc.Block() as block:
                @block.sync
                def _(sp):
                    sp.dma_start(mod[:, :], dram["b_ada_2"][l, 0]).then_inc(small.sem, 16)
                    for k, n in enumerate(("ln_g_2", "ln_b_2")):
                        sp.dma_start(gb[:, k, :], dram[n][l, 0]).then_inc(signal("ln_rows").sem, 16)
                    load_until(sp, end)

                @block.gpsimd
                def _(pool):
                    pool.memset(scT[:, :, :, :], 0.0).then_inc(signal("scores_zero").sem, 1)
                    for n in range(8):
                        pool.wait_ge(*decay.n(n + 1))
                        pool.wait_ge(*logf_in.n(2))
                        if n >= 2:
                            pool.wait_ge(*lvl.n(n - 1))
                        pool.tensor_tensor(kd[n % 2], kT, dec[n % 2], ALU.mult).then_inc(k_dec.sem, 1)

                @block.scalar
                def _(act):
                    if l == 0:
                        act.activation(stat[:, 40:48], col("c_2", 0, 8), ACT.Sigmoid).then_inc(lbs.sem, 1)
                        act.wait_ge(*lbs.n(2))
                        act.activation(lb[:, 2, :], lb[:, 2, :], ACT.Exp).then_inc(lbs.sem, 1)
                    turn_copies(act)
                    for k in range(14):
                        act.wait_ge(w_used, uq + k + 1)
                        bank = psum[:, 4 + k % 4, :].rearrange("p (j s) -> p j s", j=2)
                        if k in (6, 7, 12, 13):
                            n = 0 if k < 8 else 1
                            at = (k % 2) * S
                            act.activation(v_row[:, n, :, at:at + S], bank, ACT.Copy).then_inc(proj_out.sem, 1)
                        else:
                            at = 2 * (k if k < 6 else k - 2)
                            act.activation(projT[:, at:at + 2, :], bank, ACT.Copy,
                                           scale=0.125 if k in (8, 9) else 1.0).then_inc(proj_out.sem, 1)
                        if k == 1:
                            act.wait_ge(*proj_out.n(2))
                            act.activation(heads(bufA), fa, ACT.Exp, scale=-1.0).then_inc(gates_exp.sem, 1)
                            act.activation(heads(kT), fa, ACT.Exp).then_inc(gates_exp.sem, 1)
                    act.wait_ge(*logf_in.n(1))
                    act.activation(bufA, bufA, ACT.Ln).then_inc(logf.sem, 1)
                    for n in range(8):
                        act.wait_ge(*d_in.n(n + 1))
                        act.activation(dec[n % 2], dec[n % 2], ACT.Exp).then_inc(decay.sem, 1)
                    act.wait_ge(*meansq.n(1))
                    act.activation(gate_sig, ga, ACT.Sigmoid).then_inc(sg_done.sem, 1)
                    act.activation(dec[0], dec[0], ACT.Sqrt).then_inc(rooted.sem, 1)

                    def softplus_part(h):
                        a = sa[:, h % 2, :]
                        act.wait_ge(*z_done.n(h + 1))
                        if h >= 2:
                            act.wait_ge(*logs.n(h - 1))
                        act_chain.link(act, act.activation(a, psum[:, 4 + h % 2, 0:384], ACT.Abs))
                        act_chain.link(act, act.activation(a, a, ACT.Exp, scale=-1.0))
                        act.activation(a, a, ACT.Ln, bias=1.0).then_inc(soft.sem, 1)

                    softplus_part(0)
                    softplus_part(1)
                    for h in range(SB):
                        act.wait_ge(*w_in.n(h + 1))
                        act.activation(wt[:, h % 2, :], wt[:, h % 2, :], ACT.Exp).then_inc(w_done.sem, 1)
                        if h + 2 < SB:
                            softplus_part(h + 2)
                        if h % 2 == 1:
                            act.wait_ge(*ob_done.n(h + 1))
                            act.activation(oT[:, 1, h // 2, :], psum[:, (h // 2) % 2, 0:S], ACT.Copy).then_inc(ob_out.sem, 1)
                    for q in range(2):
                        act.wait_ge(w_used, um + 6 * q + 4)
                        if q == 1:
                            act.wait_ge(*merged.n(1))
                        act.activation(hg[:, 4:6, :].rearrange("p a (b n) -> p (a b) n", b=2), psum[:, 0:4, :],
                                       ACT.Sigmoid).then_inc(gsig.sem, 1)
                    act.wait_ge(*meansq.n(2))
                    act.activation(stat[:, 2:4], stat[:, 2:4], ACT.Sqrt).then_inc(rooted.sem, 1)

                @block.tensor
                def _(pe):
                    if l == 0:
                        pe.wait_ge(*lbs.n(4))
                    ada_pe(pe, u0)
                    pe_transpose(pe, n_row, normed.n(NT), turned)
                    pe.wait_ge(*hT_done.n(4))
                    for k in range(14):
                        w = unit(pe, uq + k).rearrange("p (c n) -> p c n", c=DC)
                        if k >= 4:
                            pe.wait_ge(*proj_out.n(k - 3))
                        for j in range(2):
                            for c in range(DC):
                                if k in (6, 7, 12, 13):
                                    a, b = hT[:, c, j * P:(j + 1) * P], w[:, c, :]
                                else:
                                    a, b = w[:, c, j * P:(j + 1) * P], hT[:, c, :]
                                ins = pe.matmul(psum[:, 4 + k % 4, j * S:(j + 1) * S], a, b,
                                                start=(c == 0), stop=(c == DC - 1))
                        ins.then_inc(w_used, 1)
                    for n, m in enumerate(LEVELS):
                        if m:
                            pe.wait_ge(*q_dec.n(n + 1))
                            pe.wait_ge(*k_dec.n(n + 1))
                        if n >= 2:
                            pe.wait_ge(*lvl_used.n(n - 1))
                        kk, qq = (heads(kd[n % 2]), heads(qd[n % 2])) if m else (heads(kT), qa)
                        for i in range(NT) if m < P else (0,):
                            for h in range(HG):
                                ti = slice(P, 2 * P) if m == P else slice(i * P, (i + 1) * P)
                                ins = pe.matmul(psum[:, 2 * (n % 2) + i, h * P:(h + 1) * P],
                                                kk[:, h, i * P:(i + 1) * P], qq[:, h, ti], start=True, stop=True)
                        ins.then_inc(lvl.sem, 1)
                    pe.wait_ge(*lvl_used.n(len(LEVELS)))
                    for h in range(HG):
                        v = [v_row[:, 0, i, h * P:(h + 1) * P] for i in range(NT)]
                        at = (h % 2) * S
                        pe.matmul(psum[:, h // 2, at:at + P], v[0], scT[:, 0, h, :], start=True, stop=True)
                        pe.matmul(psum[:, h // 2, at + P:at + S], v[0], scT[:, 2, h, :], start=True, stop=False)
                        ins = pe.matmul(psum[:, h // 2, at + P:at + S], v[1], scT[:, 1, h, :], start=False, stop=True)
                    ins.then_inc(o_done.sem, 1)
                    pe.wait_ge(*osq.n(1))
                    for b in range(2):
                        ins = pe.matmul(psum[:, 2 + b, :], C["ones"], bufA[:, b * 512:(b + 1) * 512], start=True, stop=True)
                    ins.then_inc(oss.sem, 1)

                    tri, ones = C["tri"], C["ones"]

                    def qk(h, i, out, lo, hi, stop):
                        r = slice(64 * (h % 2), 64 * (h % 2) + 64)
                        return pe.matmul(out, kb[r, h // 2, i * P:(i + 1) * P], qb[r, h // 2, lo:hi], start=True, stop=stop)

                    def z(h):
                        qk(h, 0, psum[:, 4 + h % 2, 0:S], 0, S, True)
                        qk(h, 1, psum[:, 4 + h % 2, S:S + P], P, S, True).then_inc(z_done.sem, 1)

                    def weighted(h):
                        pe.wait_ge(*w_done.n(h + 1))
                        r = slice(64 * (h % 2), 64 * (h % 2) + 64)
                        c = h // 2
                        if c >= 2:
                            pe.wait_ge(*ob_out.n(c - 1))
                        o = psum[r, c % 2, :]
                        v = [v_row[:, 1, i, h * 64:(h + 1) * 64] for i in range(NT)]
                        pe.matmul(o[:, 0:P], v[0], wt[:, h % 2, 0:P], start=True, stop=True)
                        pe.matmul(o[:, P:S], v[0], wt[:, h % 2, P:S], start=True, stop=False)
                        pe.matmul(o[:, P:S], v[1], wt[:, h % 2, S:S + P], start=False, stop=True).then_inc(ob_done.sem, 1)

                    pe.wait_ge(*proj_out.n(14))
                    z(0)
                    z(1)
                    for h in range(SB):
                        pe.wait_ge(*logs.n(h + 1))
                        if h >= 2:
                            pe.wait_ge(*w_in.n(h - 1))
                        b, L = psum[:, 6 + h % 2, :], ls[:, h % 2, :]
                        qk(h, 0, b[:, 0:S], 0, S, False)
                        pe.matmul(b[:, P:S], ones, L[:, S:S + P], start=False, stop=False)
                        pe.matmul(b[:, 0:S], tri, L[:, 0:S], start=False, stop=True)
                        qk(h, 1, b[:, S:S + P], P, S, False)
                        pe.matmul(b[:, S:S + P], tri, L[:, S:S + P], start=False, stop=True).then_inc(inc.sem, 1)
                        if h >= 1:
                            weighted(h - 1)
                        if h + 2 < SB:
                            z(h + 2)
                    weighted(SB - 1)

                    pe.wait_ge(*o_ready.n(1))
                    pe.wait_ge(*ob_out.n(4))
                    for q in range(2):
                        for k in range(4):
                            w = unit(pe, um + 6 * q + k).rearrange("p (c n) -> p c n", c=DC)
                            if q == 1 and k == 0:
                                pe.wait_ge(*gsig.n(1))
                            for j in range(2):
                                for c in range(DC):
                                    ins = pe.matmul(psum[:, k, j * S:(j + 1) * S], w[:, c, j * P:(j + 1) * P],
                                                    hT[:, c, :], start=(c == 0), stop=(c == DC - 1))
                            ins.then_inc(w_used, 1)
                        for k in range(2):
                            w = unit(pe, um + 6 * q + 4 + k).rearrange("p (c n) -> p c n", c=4)
                            if q == 1 and k == 0:
                                pe.wait_ge(*merged.n(1))
                            for j in range(4):
                                for c in range(4):
                                    ins = pe.matmul(psum[:, 4 + 2 * k + j // 2, (j % 2) * S:(j % 2) * S + S],
                                                    w[:, c, j * P:(j + 1) * P], oT[:, k, c, :],
                                                    start=(c == 0), stop=(c == 3))
                            ins.then_inc(w_used, 1)
                    pe.wait_ge(*merged.n(2))
                    for k in range(4):
                        w = unit(pe, uo + k).rearrange("p (c n) -> p c n", c=2)
                        for cc in range(2):
                            for i in range(NT):
                                for hh in range(2):
                                    ins = pe.matmul(psum[:, 2 * i + hh, :], mT[:, 2 * k + cc, i * P:(i + 1) * P],
                                                    w[:, cc, hh * 512:(hh + 1) * 512],
                                                    start=(k == 0 and cc == 0), stop=(k == 3 and cc == 1))
                        ins.then_inc(w_used, 1)

                @block.vector
                def _(dve):
                    link = lambda ins: dve_chain.link(dve, ins)
                    if l == 0:
                        dve.wait_ge(*lbs.n(1))
                        link(dve.tensor_tensor(stat[:, 40:48], stat[:, 40:48], col("c_2", 0, 8), ALU.mult))
                        for c in range(DC):
                            ins = dve.tensor_scalar(condb[:, c, :], C["ones"], stat[:, 40 + c:41 + c], None, ALU.mult)
                        l0, l1 = col("lb_logits_2", 0, 4), col("lb_logits_2", 4, 4)
                        link(dve.tensor_tensor(lb[:, 3, 0:4], l0, l1, ALU.max))
                        for k, v in enumerate((l0, l1)):
                            ins = dve.tensor_tensor(lb[:, 2, 4 * k:4 * k + 4], v, lb[:, 3, 0:4], ALU.subtract)
                        ins.then_inc(lbs.sem, 1)
                        dve.wait_ge(*lbs.n(3))
                        link(dve.tensor_tensor(lb[:, 3, 0:4], lb[:, 2, 0:4], lb[:, 2, 4:8], ALU.add))
                        link(dve.reciprocal(lb[:, 3, 0:4], lb[:, 3, 0:4]))
                        for k in range(2):
                            ins = dve.tensor_tensor(lb[:, 2, 4 * k:4 * k + 4], lb[:, 2, 4 * k:4 * k + 4], lb[:, 3, 0:4], ALU.mult)
                        link(ins)
                        dve.tensor_tensor(lb[:, 0, 0:4], lb[:, 2, 0:4], lb[:, 2, 0:4], ALU.subtract)
                        link(dve.tensor_tensor(lb[:, 0, 4:8], lb[:, 2, 0:4], lb[:, 2, 4:8], ALU.add))
                        link(dve.tensor_tensor(lb[:, 0, 4:8], lb[:, 0, 4:8], lb[:, 2, 0:4], ALU.subtract))
                        link(dve.tensor_scalar(lb[:, 1, :], lb[:, 0, :], -1.0, 1.0, ALU.mult, ALU.add))
                        dve.engine_nop().then_inc(lbs.sem, 1)
                    ada_dve(dve, u0, small.n(16))

                    dve.wait_ge(*gates_exp.n(2))
                    for b in (bufA, kT):
                        ins = dve.tensor_scalar(b, b, 1.0, None, ALU.add)
                    link(ins)
                    for b in (bufA, kT):
                        ins = dve.reciprocal(b, b)
                    link(ins)
                    for h in range(HG):
                        ins = dve.tensor_scalar(heads(bufA)[:, h, :], heads(bufA)[:, h, :], lb[:, 1, 4 * l + h:4 * l + h + 1],
                                                lb[:, 0, 4 * l + h:4 * l + h + 1], ALU.mult, ALU.add)
                    ins.then_inc(logf_in.sem, 1)
                    for h in range(HG):
                        ins = dve.tensor_scalar(heads(kT)[:, h, :], heads(kT)[:, h, :], lb[:, 1, 4 * l + h:4 * l + h + 1],
                                                None, ALU.mult)
                    ins.then_inc(logf_in.sem, 1)
                    dve.wait_ge(*logf.n(1))
                    src, dst = bufA, bufB
                    step = 1
                    while step < P:
                        a, b = (v.rearrange("p (x t) -> p x t", t=P) for v in (src, dst))
                        dve.tensor_copy(b[:, :, 0:step], a[:, :, 0:step])
                        link(dve.tensor_tensor(b[:, :, step:P], a[:, :, step:P], a[:, :, 0:P - step], ALU.add))
                        src, dst = dst, src
                        step *= 2
                    cum = src

                    def distances(n):
                        m = LEVELS[n]
                        if n >= 2:
                            dve.wait_ge(*k_dec.n(n - 1))
                            dve.wait_ge(*q_dec.n(n - 1))
                        b = cum.rearrange("p (x two m) -> p x two m", two=2, m=m)
                        d = dec[n % 2].rearrange("p (x two m) -> p x two m", two=2, m=m)
                        x = 4 * S // (2 * m)
                        ref = b[:, :, 0, m - 1:m].broadcast_to((P, x, m))
                        if m == P:
                            dve.tensor_copy(d[:, :, 1, :], b[:, :, 1, :])
                        else:
                            dve.tensor_tensor(d[:, :, 1, :], b[:, :, 1, :], ref, ALU.subtract)
                        dve.tensor_tensor(d[:, :, 0, :], ref, b[:, :, 0, :], ALU.subtract).then_inc(d_in.sem, 1)

                    def keep_level(n):
                        m = LEVELS[n]
                        dve.wait_ge(*lvl.n(n + 1))
                        if n >= 1:
                            dve.wait_ge(*lvl_used.n(n))
                        if m == P:
                            dve.wait_ge(*signal("scores_zero").n(1))
                            dve.tensor_copy(scT[:, 2, :, :], psum[:, 0, :].rearrange("p (h t) -> p h t", h=HG)).then_inc(lvl_used.sem, 1)
                            return
                        mask = (C[f"level{m}"] if m else ident).bitcast(U32).unsqueeze(1).broadcast_to((P, HG, P))
                        for i in range(NT):
                            ins = dve.copy_predicated(scT[:, i, :, :], mask,
                                                      psum[:, 2 * (n % 2) + i, :].rearrange("p (h t) -> p h t", h=HG))
                        ins.then_inc(lvl_used.sem, 1)

                    distances(0)
                    for n in range(8):
                        if n + 1 < 8:
                            distances(n + 1)
                        dve.wait_ge(*decay.n(n + 1))
                        dve.wait_ge(*proj_out.n(4))
                        if n >= 2:
                            dve.wait_ge(*lvl.n(n - 1))
                        dve.tensor_tensor(heads(qd[n % 2]), qa, heads(dec[n % 2]), ALU.mult).then_inc(q_dec.sem, 1)
                        if n >= 1:
                            keep_level(n - 1)
                    keep_level(7)
                    keep_level(8)

                    dve.wait_ge(*o_done.n(1))
                    link(dve.tensor_copy(oT[:, 0, :, :], psum[:, 0:2, :].rearrange("p b (h s) -> p (b h) s", h=2)))
                    dve.tensor_tensor(heads(bufA), oT[:, 0, :, :], oT[:, 0, :, :], ALU.mult).then_inc(osq.sem, 1)
                    dve.wait_ge(*oss.n(1))
                    dve.tensor_scalar(bufA.rearrange("p (b n) -> p b n", b=2), psum[:, 2:4, :], 1.0 / 128, 1e-6,
                                      ALU.mult, ALU.add).then_inc(meansq.sem, 1)
                    dve.wait_ge(*rooted.n(1))
                    link(dve.reciprocal(bufA, bufA))
                    for h in range(HG):
                        ins = dve.scalar_tensor_tensor(out=oT[:, 0, h, :], in0=oT[:, 0, h, :],
                                                       scalar=col("hg_norm_g_2", 4 * l + h), in1=heads(bufA)[:, h, :],
                                                       op0=ALU.mult, op1=ALU.mult)
                    link(ins)
                    dve.wait_ge(*sg_done.n(1))
                    dve.wait_ge(*proj_out.n(6))
                    link(dve.tensor_tensor(ga, ga, gate_sig, ALU.mult))
                    dve.tensor_tensor(oT[:, 0, :, :], oT[:, 0, :, :], ga, ALU.mult).then_inc(o_ready.sem, 1)
                    dve.wait_ge(*o_ready.n(1))

                    neg = const[:, CONSTS.index("neg00"):CONSTS.index("neg00") + 3, :]
                    fill = const[:, CONSTS.index("fill00"):CONSTS.index("fill00") + 3, :]
                    three = lambda a: a.rearrange("p (k t) -> p k t", k=3)

                    def log_one_minus_beta(h):
                        dve.wait_ge(*soft.n(h + 1))
                        if h >= 2:
                            dve.wait_ge(*inc.n(h - 1))
                        link(dve.scalar_tensor_tensor(out=ls[:, h % 2, :], in0=psum[:, 4 + h % 2, 0:384], scalar=0.0,
                                                      in1=sa[:, h % 2, :], op0=ALU.max, op1=ALU.add))
                        dve.tensor_tensor(three(ls[:, h % 2, :]), three(ls[:, h % 2, :]), neg, ALU.mult).then_inc(logs.sem, 1)

                    log_one_minus_beta(0)
                    for h in range(SB):
                        if h + 1 < SB:
                            log_one_minus_beta(h + 1)
                        dve.wait_ge(*inc.n(h + 1))
                        if h >= 2:
                            dve.wait_ge(*ob_done.n(h - 1))
                        dve.tensor_tensor(three(wt[:, h % 2, :]), three(psum[:, 6 + h % 2, 0:384]), fill,
                                          ALU.add).then_inc(w_in.sem, 1)

                    for q in range(2):
                        dve.wait_ge(*gsig.n(q + 1))
                        dve.wait_ge(w_used, um + 6 * q + 6)
                        sgm = hg[:, 4:6, :].rearrange("p a (b n) -> p (a b) n", b=2)
                        for k in range(2):
                            ins = dve.tensor_tensor(sgm[:, 2 * k:2 * k + 2, :], sgm[:, 2 * k:2 * k + 2, :],
                                                    psum[:, 4 + 2 * k:6 + 2 * k, :], ALU.mult)
                        link(ins)
                        dve.tensor_tensor(hg[:, q, :], hg[:, 4, :], hg[:, 5, :], ALU.add).then_inc(merged.sem, 1)
                    dve.wait_ge(w_used, end)
                    residual_norm_dve(dve, 0, gb, signal("ln_rows").n(32), 2)
            advance(mod_added=ADA_UNITS, rows_normed=NT, turned=4, hT_done=4, att_proj_copied=14, forget_exps=2, forget_in=2,
                    forget_log=1, decay_in=8, decay=8, q_decayed=8, k_decayed=8, level_products=9, level_kept=9,
                    mean_squares=2, rooted=2, hgrn_out=1, hgrn_squares=1, hgrn_sums=1, silu_gate=1, stick_z=SB,
                    stick_soft=SB, stick_logs=SB, stick_sums=SB, stick_w_in=SB, stick_w=SB, stick_out=SB, stick_copied=4,
                    heads_ready=1, gates_sigmoid=2, merged=2, layer_small=16, ln_rows=32, scores_zero=1)
            ph.close()

        GS = 8
        TURNS = K_ALL // GS

        def peer(l):
            ph = ExitStack()
            slots = sb(f"peer{l}_slots", [P, GS, D], where=ph)
            qT = sb(f"peer{l}_qT", [P, PH, S], where=ph)
            keysT = sb(f"peer{l}_keysT", [P, PH, P], where=ph)
            cand = sb(f"peer{l}_cand", [P, PH, TOPK, TOPK], where=ph)
            rest = sb(f"peer{l}_rest", [P, 2 * PH, P], where=ph)
            best = sb(f"peer{l}_best", [P, 2 * PH, TOPK], where=ph)
            besti = sb(f"peer{l}_besti", [P, 2 * PH, TOPK], U32, where=ph)
            bestf = sb(f"peer{l}_bestf", [P, 2 * PH, TOPK], where=ph)
            top = sb(f"peer{l}_top", [P, PH, TOPK], where=ph)
            pos = sb(f"peer{l}_pos", [P, 3, K_ALL], U32, where=ph)
            posf = sb(f"peer{l}_posf", [P, 2, K_ALL], where=ph)
            key = sb(f"peer{l}_key", [P, 2, K_ALL], where=ph)
            idx = sb(f"peer{l}_idx", [P, NT, K_ALL], U32, where=ph)
            gate = sb(f"peer{l}_gate", [P, NT, K_ALL], where=ph)
            gsum = sb(f"peer{l}_gsum", [P, PH], where=ph)
            pre = sb(f"peer{l}_pre", [P, NT, K_ALL], where=ph)
            dots = sb(f"peer{l}_dots", [P, GS], where=ph)
            staged_idx = sb(f"peer{l}_staged_idx", [P, GS], U32, where=ph)
            diag = sb(f"peer{l}_diag", [P, GS, P], where=ph)
            iota = sb(f"peer{l}_iota", [P, TOPK], where=ph)
            gb = sb(f"peer{l}_gb", [P, 2, D], where=ph)
            u0 = layer_at[l] + ADA_UNITS + ATT_UNITS
            uq = u0 + ADA_UNITS
            end = uq + PEER_UNITS
            small, ln_rows = signal("layer_small"), signal("ln_rows")
            (turned, hT_done, normed, q_out, scored, keys_kept, idx_ready, gate_in, gate_exp, u_used, v_used, kept, gelu_in,
             gelu, weights, diagd, staged, meansq, rooted) = (signal(n) for n in (
                 "turned", "hT_done", "rows_normed", "query_copied", "key_scores", "keys_kept", "indices_ready", "gate_in",
                 "gate_exp", "u_used", "v_used", "dots_kept", "gelu_in", "gelu", "expert_weights", "diagonal", "staged",
                 "mean_squares", "rooted"))
            landed = [signal(f"gathered{s}") for s in range(GS)]
            u_tab, v_tab = dram["peer_u_2"], dram["peer_v_2"]
            rows_of = PEER_ROWS * l

            with nc.Block() as block:
                @block.sync
                def _(sp):
                    sp.dma_start(mod[:, :], dram["b_ada_2"][l, 1]).then_inc(small.sem, 16)
                    sp.dma_start(keysT[:, :, :], dram["sub_keys_2"][l]).then_inc(small.sem, 16)
                    sp.dma_start(iota[:, :], dram["iota"]).then_inc(small.sem, 16)
                    for k, n in enumerate(("ln_g_2", "ln_b_2")):
                        sp.dma_start(gb[:, k, :], dram[n][l, 1]).then_inc(ln_rows.sem, 16)
                    load_until(sp, end)
                    if l == LAYERS - 1:
                        sp.wait_ge(*signal("result").n(1))
                        sp.dma_start(out, x_row[:, :, :]).then_inc(signal("stored").sem, 16)
                        sp.wait_ge(*signal("stored").n(16))

                @block.gpsimd
                def _(pool):
                    def stage(i, j, s, free):
                        pool.wait_ge(*free)
                        k = j * GS + s
                        column = idx[:, i, k:k + 1] if isinstance(k, int) else idx[:, i, bass.ds(k, 1)]
                        pool.tensor_copy(staged_idx[:, s:s + 1], column).then_inc(staged.sem, 1)

                    def gather(table, s):
                        pool.indirect_dma_start(
                            out=slots[:, s, :], out_offset=None, in_=table,
                            in_offset=bass.IndirectOffsetOnAxis(ap=staged_idx[:, s:s + 1], axis=0),
                        ).then_inc(landed[s].sem, 16)

                    at = 0
                    for i in range(NT):
                        pool.wait_ge(*idx_ready.n(i + 1))
                        for table, used, before in ((u_tab, u_used, v_used), (v_tab, v_used, u_used)):
                            for s in range(GS):
                                if s > 0:
                                    pool.wait_ge(*staged.n(at + s))
                                k = K_ALL * (i + (before is u_used)) - GS + s + 1
                                stage(i, 0, s, before.n(k) if k > 0 else idx_ready.n(i + 1))
                                if s > 0:
                                    gather(table, s - 1)
                            with pool.Fori(1, TURNS) as j:
                                for s in range(GS):
                                    pool.wait_ge(*staged.n(j * GS + (at + s)))
                                    stage(i, j, s, used.n(j * GS + (i * K_ALL - GS + s + 1)))
                                    gather(table, (s - 1) % GS)
                            at += K_ALL
                            pool.wait_ge(*staged.n(at))
                            gather(table, GS - 1)

                def arrived(eng, s, rnd, j):
                    eng.wait_ge(*landed[s].n(j * 16 + 16 * (rnd * TURNS + 1)))

                @block.scalar
                def _(act):
                    turn_copies(act)
                    for k in range(4):
                        act.wait_ge(w_used, uq + k + 1)
                        act.activation(qT[:, 2 * k:2 * k + 2, :], psum[:, 4 + k, :].rearrange("p (j s) -> p j s", j=2),
                                       ACT.Copy).then_inc(q_out.sem, 1)
                    for i in range(NT):
                        act.wait_ge(*gate_in.n(i + 1))
                        act.activation(gate[:, i, :], gate[:, i, :], ACT.Exp).then_inc(gate_exp.sem, 1)
                        act.wait_ge(*gelu_in.n(i + 1))
                        act.activation(pre[:, i, :], pre[:, i, :], ACT.Gelu).then_inc(gelu.sem, 1)
                        act.wait_ge(*weights.n(i + 1))

                        def diagonal(j, s):
                            k = j * GS + s
                            w = pre[:, i, k:k + 1] if isinstance(k, int) else pre[:, i, bass.ds(k, 1)]
                            if i > 0 or not isinstance(j, int):
                                act.wait_ge(*v_used.n(k + (i * K_ALL - GS + 1)))
                            act.activation(diag[:, s, :], ident, ACT.Copy, scale=w).then_inc(diagd.sem, 1)

                        for s in range(GS):
                            diagonal(0, s)
                        with act.Fori(1, TURNS) as j:
                            for s in range(GS):
                                diagonal(j, s)
                    act.wait_ge(*meansq.n(1))
                    act.activation(stat[:, 2:4], stat[:, 2:4], ACT.Sqrt).then_inc(rooted.sem, 1)

                @block.tensor
                def _(pe):
                    ada_pe(pe, u0)
                    pe_transpose(pe, n_row, normed.n(NT), turned)
                    pe.wait_ge(*hT_done.n(4))
                    for k in range(PEER_UNITS):
                        w = unit(pe, uq + k).rearrange("p (c n) -> p c n", c=DC)
                        for j in range(2):
                            for c in range(DC):
                                ins = pe.matmul(psum[:, 4 + k, j * S:(j + 1) * S], w[:, c, j * P:(j + 1) * P], hT[:, c, :],
                                                start=(c == 0), stop=(c == DC - 1))
                        ins.then_inc(w_used, 1)
                    pe.wait_ge(*small.n(48))
                    pe.wait_ge(*q_out.n(4))

                    def score(i):
                        for half in range(2):
                            r = slice(64 * half, 64 * half + 64)
                            for h in range(PH):
                                ins = pe.matmul(psum[:, 2 * half + h // 4, (h % 4) * P:(h % 4 + 1) * P],
                                                qT[r, h, i * P:(i + 1) * P], keysT[r, h, :], start=True, stop=True)
                        ins.then_inc(scored.sem, 1)

                    def add_row(i, j, s, first=False, last=False):
                        arrived(pe, s, 2 * i + 1, j)
                        pe.wait_ge(*diagd.n(j * GS + (i * K_ALL + s + 1)))
                        for h in range(2):
                            ins = pe.matmul(psum[:, 4 + 2 * i + h, :], diag[:, s, :], slots[:, s, h * 512:(h + 1) * 512],
                                            start=first, stop=last)
                        ins.then_inc(v_used.sem, 1)

                    score(0)
                    pe.wait_ge(*keys_kept.n(1))
                    score(1)
                    for i in range(NT):
                        for s in range(GS):
                            add_row(i, 0, s, first=(s == 0))
                        with pe.Fori(1, TURNS - 1) as j:
                            for s in range(GS):
                                add_row(i, j, s)
                        for s in range(GS):
                            add_row(i, TURNS - 1, s, last=(s == GS - 1))

                @block.vector
                def _(dve):
                    link = lambda ins: dve_chain.link(dve, ins)
                    ada_dve(dve, u0, small.n(48))

                    def top16(n, values, rest_of, val, ind):
                        for g in range(n):
                            ins = dve.max(val(g)[:, 0:8], values(g))
                        link(ins)
                        for g in range(n):
                            dve.max_index(ind(g)[:, 0:8], val(g)[:, 0:8], values(g))
                        for g in range(n):
                            ins = dve.match_replace(out=rest_of(g), in_to_replace=val(g)[:, 0:8], in_values=values(g),
                                                    imm_value=NEG)
                        link(ins)
                        for g in range(n):
                            ins = dve.max(val(g)[:, 8:16], rest_of(g))
                        link(ins)
                        for g in range(n):
                            ins = dve.max_index(ind(g)[:, 8:16], val(g)[:, 8:16], rest_of(g))
                        return ins

                    def route(i):
                        dve.wait_ge(*scored.n(i + 1))
                        top16(2 * PH, lambda g: psum[:, g // 4, (g % 4) * P:(g % 4 + 1) * P], lambda g: rest[:, g, :],
                              lambda g: best[:, g, :], lambda g: besti[:, g, :]).then_inc(keys_kept.sem, 1)
                        dve.wait_ge(*keys_kept.n(i + 1))
                        dve.tensor_copy(bestf[:, :, :], besti[:, :, :])
                        shape = (P, PH, TOPK, TOPK)
                        link(dve.tensor_tensor(cand[:, :, :, :], best[:, 0:PH, :].unsqueeze(3).broadcast_to(shape),
                                               best[:, PH:2 * PH, :].unsqueeze(2).broadcast_to(shape), ALU.add))
                        pos8 = pos[:, 0, :].rearrange("p (h k) -> p h k", h=PH)
                        flat = rest[:, :, :].rearrange("p (h a) n -> p h (a n)", h=PH)
                        link(top16(PH, lambda h: cand[:, h, :, :].rearrange("p a b -> p (a b)"), lambda h: flat[:, h, :],
                                   lambda h: top[:, h, :], lambda h: pos8[:, h, :]))
                        dve.tensor_scalar(pos[:, 1, :], pos[:, 0, :], 4, None, ALU.logical_shift_right)
                        link(dve.tensor_scalar(pos[:, 2, :], pos[:, 0, :], 15, None, ALU.bitwise_and))
                        link(dve.tensor_copy(posf[:, :, :], pos[:, 1:3, :]))
                        hot = rest[:, :, :].rearrange("p (h a) (b n) -> p h (a b) n", h=PH, n=TOPK)
                        for half in range(2):
                            p8 = posf[:, half, :].rearrange("p (h k) -> p h k", h=PH)
                            link(dve.tensor_tensor(hot, p8.unsqueeze(3).broadcast_to(shape),
                                                   iota[:, :].unsqueeze(1).unsqueeze(1).broadcast_to(shape), ALU.is_equal))
                            link(dve.tensor_tensor(hot, hot, bestf[:, half * PH:(half + 1) * PH, :].unsqueeze(2)
                                                   .broadcast_to(shape), ALU.mult))
                            link(dve.tensor_reduce(key[:, half, :].rearrange("p (h k) -> p h k", h=PH), hot, AX.X, ALU.add))
                        link(dve.tensor_scalar(key[:, 0, :], key[:, 0, :], float(P), float(rows_of), ALU.mult, ALU.add))
                        dve.tensor_tensor(idx[:, i, :], key[:, 0, :], key[:, 1, :], ALU.add).then_inc(idx_ready.sem, 1)
                        g3 = gate[:, i, :].rearrange("p (h k) -> p h k", h=PH)
                        dve.tensor_tensor(g3, top[:, :, :], top[:, :, 0:1].broadcast_to((P, PH, TOPK)),
                                          ALU.subtract).then_inc(gate_in.sem, 1)
                        dve.wait_ge(*gate_exp.n(i + 1))
                        link(dve.tensor_reduce(gsum[:, :], g3, AX.X, ALU.add))
                        link(dve.reciprocal(gsum[:, :], gsum[:, :]))
                        link(dve.tensor_tensor(g3, g3, gsum[:, :].unsqueeze(2).broadcast_to((P, PH, TOPK)), ALU.mult))

                    for i in range(NT):
                        route(i)
                        with dve.Fori(0, TURNS) as j:
                            if True:
                                for s in range(GS):
                                    arrived(dve, s, 2 * i, j)
                                    dve.tensor_tensor_reduce(out=slots[:, s, :], in0=slots[:, s, :], in1=n_row[:, i, :],
                                                             scale=1.0, scalar=0.0, op0=ALU.mult, op1=ALU.add,
                                                             accum_out=dots[:, s:s + 1]).then_inc(u_used.sem, 1)
                                dve.wait_ge(*u_used.n(j * GS + (i * K_ALL + GS)))
                                dve.tensor_copy(pre[:, i, bass.ds(j * GS, GS)], dots[:, :]).then_inc(kept.sem, 1)
                                dve.wait_ge(*kept.n(j + (i * TURNS + 1)))
                        dve.engine_nop().then_inc(gelu_in.sem, 1)
                        dve.wait_ge(*gelu.n(i + 1))
                        dve.tensor_tensor(pre[:, i, :], pre[:, i, :], gate[:, i, :], ALU.mult).then_inc(weights.sem, 1)
                    dve.wait_ge(*v_used.n(NT * K_ALL))
                    ins = residual_norm_dve(dve, 4, gb, ln_rows.n(32), 1)
                    if l == LAYERS - 1:
                        ins.then_inc(signal("result").sem, 1)
            advance(mod_added=ADA_UNITS, rows_normed=NT, turned=4, hT_done=4, layer_small=48, ln_rows=32, query_copied=4,
                    key_scores=NT, keys_kept=NT, indices_ready=NT, gate_in=NT, gate_exp=NT, u_used=NT * K_ALL,
                    v_used=NT * K_ALL, dots_kept=NT * TURNS, gelu_in=NT, gelu=NT, expert_weights=NT,
                    diagonal=NT * K_ALL, staged=2 * NT * K_ALL, mean_squares=1, rooted=1,
                    **{f"gathered{s}": 2 * NT * TURNS * 16 for s in range(GS)})
            ph.close()

        for l in range(LAYERS):
            attention(l)
            if stop_after <= 3 + 2 * l:
                return
            peer(l)
            if stop_after <= 4 + 2 * l:
                return


def column_vectors(v):
    import numpy as np
    parts = []
    for name in COLS:
        a = np.asarray(v[name]).reshape(-1, P)
        parts.append(a.T)
    return np.ascontiguousarray(np.concatenate(parts, axis=1))


def constant_matrices():
    import numpy as np
    s, t = np.arange(P)[:, None], np.arange(P)[None, :]
    m = {"ident": s == t, "ones": s >= 0 * t, "heads64": s // 64 == t // 64, "tri": s >= t,
         "neg00": -1.0 * (s < t), "neg01": -1.0 * (s >= 0 * t), "neg11": -1.0 * (s < t),
         "fill00": NEG * (s >= t), "fill01": 0.0 * (s >= t), "fill11": NEG * (s >= t)}
    for h in (64, 32, 16, 8, 4, 2, 1):
        m[f"level{h}"] = (s // (2 * h) == t // (2 * h)) & (s % (2 * h) < h) & (t % (2 * h) >= h)
    return np.ascontiguousarray(np.stack([np.broadcast_to(m[n], (P, P)).astype(np.float32) for n in CONSTS], axis=1))


def layouts(v):
    import numpy as np
    v = {k: np.asarray(a) for k, a in v.items()}

    def by_columns(w, n):
        *lead, k, cols = w.shape
        w = w.reshape(*lead, k // P, P, cols // n, n)
        i = len(lead)
        w = w.transpose(*range(i), i + 2, i + 1, i, i + 3)
        return np.ascontiguousarray(w.reshape(*lead, cols // n, P, k // P * n))

    def by_rows(w, c):
        *lead, k, cols = w.shape
        w = w.reshape(*lead, k // P // c, c, P, cols)
        i = len(lead)
        w = w.transpose(*range(i), i, i + 2, i + 1, i + 3)
        return np.ascontiguousarray(w.reshape(*lead, k // P // c, P, c * cols))

    def rows(a, n=P):
        return np.ascontiguousarray(np.broadcast_to(a.reshape(1, -1), (n, a.size)))

    out = {
        "x": v["x"].reshape(NT, P, D).transpose(1, 0, 2),
        "consts": constant_matrices(),
        "cols": column_vectors(v),
        "iota": rows(np.arange(TOPK, dtype=np.float32)),
        "w_in": by_columns(v["w_in"][0], 256),
        "w_out": by_rows(v["w_out"][0], 2),
        "w_route": np.concatenate([v["w_route_group"][0], v["w_route_expert"][0]], axis=1)
                     .reshape(DC, P, GROUPS + E).transpose(1, 0, 2),
        "b_route": rows(np.concatenate([v["b_route_group"][0], v["b_route_expert"][0]])),
        "norm_final_g": rows(v["norm_final_g"]),
        "w1": by_columns(v["w1"][0], 256),
        "w3": by_columns(v["w3"][0], 256),
        "w2": by_rows(v["w2"][0], 2),
        "w_ada_2": by_columns(v["w_ada_2"], 256),
        "b_ada_2": np.broadcast_to(v["b_ada_2"].reshape(LAYERS, 2, 1, 3 * D), (LAYERS, 2, P, 3 * D)),
        "w_in_2": by_columns(v["w_in_2"], 256),
        "w_up_a_2": by_columns(v["w_up_a_2"], 512),
        "w_up_b_2": by_columns(v["w_up_b_2"], 512),
        "w_o_2": by_rows(v["w_o_2"], 2),
        "w_pq_2": by_columns(v["w_pq_2"], 256),
        "sub_keys_2": v["sub_keys_2"].transpose(0, 1, 4, 2, 3).reshape(LAYERS, P, PH, P),
        "peer_u_2": v["peer_u_2"].reshape(-1, D),
        "peer_v_2": v["peer_v_2"].reshape(-1, D),
        "ln_g_2": np.broadcast_to(v["ln_g_2"][:, :, None, :], (LAYERS, 2, P, D)),
        "ln_b_2": np.broadcast_to(v["ln_b_2"][:, :, None, :], (LAYERS, 2, P, D)),
    }
    return {k: np.ascontiguousarray(a) for k, a in out.items()}


def kernel(**inputs):
    import numpy as np
    import concourse.bacc as bacc
    from concourse.bass_utils import run_bass_kernel_spmd

    arrays = layouts(inputs)
    nc = bacc.Bacc("TRN2", target_bir_lowering=False, num_devices=1)
    dram = {n: nc.dram_tensor("in_" + n, a.shape, mybir.dt.from_np(a.dtype), kind="ExternalInput").ap()
            for n, a in arrays.items()}
    out = nc.dram_tensor("y", (P, NT, D), F32, kind="ExternalOutput").ap()
    build(nc, dram, out)
    got = run_bass_kernel_spmd(nc, [{"in_" + n: a for n, a in arrays.items()}], core_ids=[0]).results[0]["y"]
    return np.ascontiguousarray(got.transpose(1, 0, 2)).reshape(1, S, D)
```

```python
from contextlib import ExitStack

import concourse.bass as bass
from concourse import mybir

F32 = mybir.dt.float32
U32 = mybir.dt.uint32
ALU = mybir.AluOpType
ACT = mybir.ActivationFunctionType
AX = mybir.AxisListType

P = 128
D = 1024
S = 256
NT = S // P
DC = D // P
DA = 512
AC = DA // P
TAPS_A, TAPS_B = 3, 31
GROUPS, PER_GROUP = 4, 8
E = GROUPS * PER_GROUP
LAYERS = 2
HG = 4
SB = 8
PH, TOPK = 8, 16
K_ALL = PH * TOPK
PEER_ROWS = P * P
ALPHA = (2.0 * LAYERS) ** 0.25
NEG = -1.0e30

UNIT = 2048
RING = 8
TURN = 2
PAIR_UNITS = 12

MIX_UNITS = 10 + 4
MOE_UNITS = 6 * E
ADA_UNITS = 12
ATT_UNITS = 6 + 2 + 4 + 2 + 2 * 6 + 4
PEER_UNITS = 4
LAYER_UNITS = 2 * ADA_UNITS + ATT_UNITS + PEER_UNITS

COLS = {}
_at = 0
for _name, _n in (("norm_mix_g", 8), ("conv_a_w", TAPS_A * 4), ("conv_b_w", TAPS_B * 4), ("conv_b_bias", 4),
                  ("ln_b_g", 4), ("ln_b_b", 4), ("beta_a", 4), ("beta_b", 4), ("norm_ffn_g", 8), ("c_2", 8),
                  ("lb_logits_2", 8), ("hg_norm_g_2", 8)):
    COLS[_name] = _at
    _at += _n
NCOLS = _at

CONSTS = ("ident", "ones", "heads64", "tri", 
          "neg00", "neg01", "neg11", "fill00", "fill01", "fill11") + tuple(f"level{m}" for m in (64, 32, 16, 8, 4, 2, 1))
NCONST = len(CONSTS)


class Signal:

    def __init__(self, sem):
        self.sem, self.base = sem, 0

    def n(self, k):
        return self.sem, self.base + k


class Chain:

    def __init__(self, sem):
        self.sem, self.count = sem, 0

    def link(self, eng, ins):
        self.count += 1
        ins.then_inc(self.sem, 1)
        eng.wait_ge(self.sem, self.count)


def build(nc, dram, out, stop_after=99):
    with ExitStack() as ctx:
        def sb(name, shape, dt=F32, where=ctx):
            return where.enter_context(nc.sbuf_tensor(name, shape, dt))

        def sem(name):
            return ctx.enter_context(nc.semaphore(name))

        signals = {}

        def signal(name):
            if name not in signals:
                signals[name] = Signal(sem(name))
            return signals[name]

        def advance(**made):
            for name, k in made.items():
                signals[name].base += k

        psum = ctx.enter_context(nc.psum_tensor("psum", [P, 8, 512], F32))
        ring = sb("ring", [P, RING, UNIT])
        x_row = sb("x_row", [P, NT, D])
        n_row = sb("n_row", [P, NT, D])
        hT = sb("hT", [P, DC, S])
        const = sb("const", [P, NCONST, P])
        cols = sb("cols", [P, NCOLS])
        stat = sb("stat", [P, 64])
        lb = sb("lb", [P, 4, 4 * LAYERS])
        condb = sb("condb", [P, DC, P])
        C = {name: const[:, i, :] for i, name in enumerate(CONSTS)}
        ident = C["ident"]

        def col(name, k=0, n=1):
            return cols[:, COLS[name] + k:COLS[name] + k + n]

        loaded = sem("loaded")
        w_land = [sem(f"w_land{s}") for s in range(RING)]
        w_used = sem("w_used")
        dve_chain, act_chain, pool_chain = Chain(sem("dve_chain")), Chain(sem("act_chain")), Chain(sem("pool_chain"))

        stream = []
        stream += [dram["w_in"][u] for u in range(10)] + [dram["w_out"][u] for u in range(4)]
        moe_at = len(stream)

        def moe_units(p):
            return [(w, 2 * p + k, half) for w in ("w1", "w3", "w2") for half in range(2) for k in range(2)]

        for p in range(E // 2):
            stream += [dram[w][e, half] for w, e, half in moe_units(p)]
        layer_at = []
        for l in range(LAYERS):
            layer_at.append(len(stream))
            win = dram["w_in_2"][l]
            stream += [dram["w_ada_2"][l, u] for u in range(12)]
            stream += [win[u] for u in (2, 3, 0, 1, 6, 7)]
            stream += [win[u] for u in (4, 5)]
            stream += [win[u] for u in (8, 9, 10, 11)]
            stream += [win[u] for u in (12, 13)]
            for q in range(2):
                stream += [win[u] for u in (14 + 2 * q, 15 + 2 * q, 18 + 2 * q, 19 + 2 * q)]
                stream += [dram["w_up_a_2"][l, q], dram["w_up_b_2"][l, q]]
            stream += [dram["w_o_2"][l, u] for u in range(4)]
            stream += [dram["w_ada_2"][l, 12 + u] for u in range(12)]
            stream += [dram["w_pq_2"][l, u] for u in range(4)]
        assert moe_at == MIX_UNITS and layer_at[0] == MIX_UNITS + MOE_UNITS
        assert len(stream) == layer_at[0] + LAYERS * LAYER_UNITS
        issued = [0]

        def load_unit(sp, u):
            if u >= RING:
                sp.wait_ge(w_used, u - RING + 1)
            sp.dma_start(ring[:, u % RING, :], stream[u]).then_inc(w_land[u % RING], 16)

        def load_until(sp, end):
            for u in range(issued[0], min(end + RING, len(stream))):
                load_unit(sp, u)
            issued[0] = min(end + RING, len(stream))

        def unit(pe, u):
            pe.wait_ge(w_land[u % RING], 16 * (u // RING + 1))
            return ring[:, u % RING, :]

        def pe_transpose(pe, src, ready, done, free=None):
            pe.wait_ge(*ready)
            for b in range(4):
                if free is not None:
                    pe.wait_ge(*free)
                for c in (2 * b, 2 * b + 1):
                    for i in range(NT):
                        at = (c % 2) * S + i * P
                        ins = pe.transpose(psum[:, b, at:at + P], src[:, i, c * P:(c + 1) * P], ident)
                ins.then_inc(done.sem, 1)


        def mixer():
            ph = ExitStack()
            projT = sb("mix_projT", [P, 20, S], where=ph)
            PA, PB = TAPS_A // 2, TAPS_B // 2
            ua = sb("mix_ua", [P, AC, S + 2 * PA], where=ph)
            ub = sb("mix_ub", [P, AC, S + 2 * PB], where=ph)
            sq = sb("mix_sq", [P, 2, AC * S], where=ph)
            yT = sb("mix_yT", [P, 2 * AC, S], where=ph)
            tmp = sb("mix_tmp", [P, AC * S], where=ph)
            ssum = signal("squares_summed")
            meansq = signal("mean_squares")
            rooted = signal("rooted")
            normed = signal("rows_normed")
            turned = signal("turned")
            turned_used = signal("turned_used")
            hT_done = signal("hT_done")
            proj = signal("proj_done")
            proj_out = signal("proj_copied")
            sig_in = signal("sig_in")
            sig = signal("sig_done")
            stat_in = signal("stat_in")
            stat_out = signal("stat_out")
            y_ready = signal("y_ready")
            y_out = signal("y_out")
            y3, t3 = yT[:, :, :], tmp[:, :].rearrange("p (c s) -> p c s", c=AC)

            with nc.Block() as block:
                @block.sync
                def _(sp):
                    for name, dst in (("x", x_row[:, :, :]), ("consts", const[:, :, :]), ("cols", cols[:, :])):
                        sp.dma_start(dst, dram[name]).then_inc(loaded, 16)
                    load_until(sp, MIX_UNITS)

                @block.scalar
                def _(act):
                    act.wait_ge(loaded, 48)
                    for i in range(NT):
                        act.activation(sq[:, i, :], x_row[:, i, :], ACT.Square,
                                       accum_out=stat[:, i:i + 1]).then_inc(ssum.sem, 1)
                    act.wait_ge(*meansq.n(1))
                    act.activation(stat[:, 2:4], stat[:, 2:4], ACT.Sqrt).then_inc(rooted.sem, 1)
                    act.wait_ge(*proj_out.n(10))
                    act.activation(projT[:, 16:20, :], projT[:, 16:20, :], ACT.Sigmoid).then_inc(sig.sem, 1)
                    act.wait_ge(*meansq.n(2))
                    act.activation(tmp[:, 0:S], tmp[:, 0:S], ACT.Sqrt).then_inc(rooted.sem, 1)
                    act.wait_ge(*sig_in.n(1))
                    act.activation(projT[:, 0:AC, :], yT[:, AC:2 * AC, :], ACT.Sigmoid).then_inc(sig.sem, 1)
                    act.wait_ge(*meansq.n(3))
                    act.activation(sq[:, :, :], sq[:, :, :], ACT.Sqrt).then_inc(rooted.sem, 1)

                @block.tensor
                def _(pe):
                    pe_transpose(pe, n_row, normed.n(NT), turned)
                    pe.wait_ge(*hT_done.n(4))
                    for u in range(10):
                        w = unit(pe, u).rearrange("p (c n) -> p c n", c=DC)
                        if u >= 4:
                            pe.wait_ge(*proj_out.n(u - 3))
                        for j in range(2):
                            for c in range(DC):
                                ins = pe.matmul(psum[:, 4 + u % 4, j * S:(j + 1) * S], w[:, c, j * P:(j + 1) * P],
                                                hT[:, c, :], start=(c == 0), stop=(c == DC - 1))
                            if j == 1:
                                ins.then_inc(w_used, 1)
                    pe.wait_ge(*stat_in.n(1))
                    for c in range(AC):
                        ins = pe.matmul(psum[:, 0, 0:S], C["ones"], ub[:, c, 0:S], start=(c == 0), stop=(c == AC - 1))
                    ins.then_inc(stat_out.sem, 1)
                    pe.wait_ge(*stat_in.n(2))
                    for c in range(AC):
                        ins = pe.matmul(psum[:, 1, 0:S], C["ones"], t3[:, c, :], start=(c == 0), stop=(c == AC - 1))
                    ins.then_inc(stat_out.sem, 1)
                    pe.wait_ge(*stat_in.n(3))
                    for b in range(4):
                        ins = pe.matmul(psum[:, b, :], C["heads64"], sq[:, b // 2, (b % 2) * 512:(b % 2) * 512 + 512],
                                        start=True, stop=True)
                    ins.then_inc(stat_out.sem, 1)
                    pe.wait_ge(*y_ready.n(1))
                    for k in range(4):
                        w = unit(pe, 10 + k).rearrange("p (c n) -> p c n", c=2)
                        for cc in range(2):
                            for i in range(NT):
                                for h in range(2):
                                    ins = pe.matmul(psum[:, 4 + 2 * i + h, :], yT[:, 2 * k + cc, i * P:(i + 1) * P],
                                                    w[:, cc, h * 512:(h + 1) * 512],
                                                    start=(k == 0 and cc == 0), stop=(k == 3 and cc == 1))
                        ins.then_inc(w_used, 1)

                @block.gpsimd
                def _(pool):
                    pool.memset(ua[:, :, :], 0.0)
                    pool.memset(ub[:, :, :], 0.0).then_inc(signal("pads_zero").sem, 1)

                @block.vector
                def _(dve):
                    link = lambda ins: dve_chain.link(dve, ins)
                    dve.wait_ge(*ssum.n(NT))
                    dve.tensor_scalar(stat[:, 2:4], stat[:, 0:2], 1.0 / D, 1e-6, ALU.mult, ALU.add).then_inc(meansq.sem, 1)
                    dve.wait_ge(*rooted.n(1))
                    link(dve.reciprocal(stat[:, 4:6], stat[:, 2:4]))
                    for i in range(NT):
                        dve.tensor_scalar(n_row[:, i, :], x_row[:, i, :], stat[:, 4 + i:5 + i], None,
                                          ALU.mult).then_inc(normed.sem, 1)
                    for b in range(4):
                        dve.wait_ge(*turned.n(b + 1))
                        dve.tensor_scalar(hT[:, 2 * b, :], psum[:, b, 0:S], col("norm_mix_g", 2 * b), None, ALU.mult)
                        dve.tensor_scalar(hT[:, 2 * b + 1, :], psum[:, b, S:2 * S], col("norm_mix_g", 2 * b + 1), None,
                                          ALU.mult).then_inc(hT_done.sem, 1)
                    for u in range(10):
                        dve.wait_ge(w_used, u + 1)
                        dve.tensor_copy(projT[:, 2 * u:2 * u + 2, :],
                                        psum[:, 4 + u % 4, :].rearrange("p (j s) -> p j s", j=2)).then_inc(proj_out.sem, 1)
                    dve.wait_ge(*proj_out.n(10))
                    dve.wait_ge(*signal("pads_zero").n(1))
                    link(dve.tensor_tensor(ua[:, :, PA:PA + S], projT[:, 8:12, :], projT[:, 0:4, :], ALU.mult))
                    for c in range(AC):
                        ins = dve.tensor_scalar(yT[:, c, :], ua[:, c, 0:S], col("conv_a_w", c), None, ALU.mult)
                    link(ins)
                    for j in range(1, TAPS_A):
                        for c in range(AC):
                            ins = dve.scalar_tensor_tensor(out=yT[:, c, :], in0=ua[:, c, j:j + S],
                                                           scalar=col("conv_a_w", j * AC + c), in1=yT[:, c, :],
                                                           op0=ALU.mult, op1=ALU.add)
                        link(ins)
                    link(dve.tensor_tensor(yT[:, 0:AC, :], yT[:, 0:AC, :], projT[:, 4:8, :], ALU.mult))
                    dve.wait_ge(*sig.n(1))
                    link(dve.tensor_tensor(ub[:, :, PB:PB + S], projT[:, 12:16, :], projT[:, 16:20, :], ALU.mult))
                    for c in range(AC):
                        ins = dve.tensor_scalar(yT[:, AC + c, :], ub[:, c, 0:S], col("conv_b_w", c), col("conv_b_bias", c),
                                                ALU.mult, ALU.add)
                    tap = signal("tap")
                    ins.then_inc(tap.sem, 1)
                    with dve.Fori(1, TAPS_B) as j:
                        dve.wait_ge(tap.sem, tap.base + j)
                        for c in range(AC):
                            ins = dve.scalar_tensor_tensor(
                                out=yT[:, AC + c, :], in0=ub[:, c, bass.ds(j, S)],
                                scalar=cols[:, bass.ds(j * AC + (COLS["conv_b_w"] + c), 1)],
                                in1=yT[:, AC + c, :], op0=ALU.mult, op1=ALU.add)
                        ins.then_inc(tap.sem, 1)
                    dve.wait_ge(*tap.n(TAPS_B))
                    yb = yT[:, AC:2 * AC, :]
                    dve.tensor_copy(ub[:, :, 0:S], yb).then_inc(stat_in.sem, 1)
                    dve.wait_ge(*stat_out.n(1))
                    link(dve.tensor_scalar(stat_mean, psum[:, 0, 0:S], 1.0 / DA, None, ALU.mult))
                    mean4 = stat_mean.unsqueeze(1).broadcast_to((P, AC, S))
                    link(dve.tensor_tensor(yb, yb, mean4, ALU.subtract))
                    dve.tensor_tensor(t3, yb, yb, ALU.mult).then_inc(stat_in.sem, 1)
                    dve.wait_ge(*stat_out.n(2))
                    dve.tensor_scalar(tmp[:, 0:S], psum[:, 1, 0:S], 1.0 / DA, 1e-6, ALU.mult, ALU.add).then_inc(meansq.sem, 1)
                    dve.wait_ge(*rooted.n(2))
                    link(dve.reciprocal(stat_mean, tmp[:, 0:S]))
                    link(dve.tensor_tensor(yb, yb, mean4, ALU.mult))
                    for c in range(AC):
                        ins = dve.tensor_scalar(yT[:, AC + c, :], yT[:, AC + c, :], col("ln_b_g", c), col("ln_b_b", c),
                                                ALU.mult, ALU.add)
                    ins.then_inc(sig_in.sem, 1)
                    dve.wait_ge(*sig_in.n(1))
                    dve.wait_ge(*sig.n(2))
                    link(dve.tensor_tensor(yb, yb, projT[:, 0:AC, :], ALU.mult))
                    sq8 = sq[:, :, :].rearrange("p b (c s) -> p (b c) s", c=AC)
                    dve.tensor_tensor(sq8, y3, y3, ALU.mult).then_inc(stat_in.sem, 1)
                    dve.wait_ge(*stat_out.n(3))
                    dve.tensor_scalar(sq[:, :, :].rearrange("p b (c s) -> p (b c) s", c=2), psum[:, 0:4, :],
                                      1.0 / 64, 1e-6, ALU.mult, ALU.add).then_inc(meansq.sem, 1)
                    dve.wait_ge(*rooted.n(3))
                    link(dve.reciprocal(sq8, sq8))
                    for c in range(2 * AC):
                        ins = dve.scalar_tensor_tensor(out=yT[:, c, :], in0=yT[:, c, :],
                                                       scalar=col("beta_a" if c < AC else "beta_b", c % AC),
                                                       in1=sq8[:, c, :], op0=ALU.mult, op1=ALU.mult)
                    ins.then_inc(y_ready.sem, 1)
                    dve.wait_ge(w_used, MIX_UNITS)
                    for i in range(NT):
                        dve.tensor_tensor(x_row[:, i, :].rearrange("p (h n) -> p h n", h=2), psum[:, 4 + 2 * i:6 + 2 * i, :],
                                          x_row[:, i, :].rearrange("p (h n) -> p h n", h=2), ALU.add)
            advance(squares_summed=NT, mean_squares=3, rooted=3, rows_normed=NT, turned=4, hT_done=4)
            ph.close()

        mean_buf = sb("mean_buf", [P, S])
        mod = sb("mod", [P, 3 * D])
        stat_mean = mean_buf[:, :]
        mixer()
        if stop_after <= 1:
            return

        SLOTS = 64
        PAIRS = E // 2
        shared = ExitStack()
        combine = sb("combine", [P, NT, E], where=shared)
        rank = sb("rank", [P, NT, E], where=shared)
        overflow = sb("overflow", [P, 1], U32, where=shared)
        iota = sb("iota", [P, P], where=shared)
        gfin = sb("gfin", [P, D], where=shared)

        def moe():
            ph = ExitStack()
            pick = sb("moe_pick", [P, NT, E, SLOTS], where=ph)
            pickw = sb("moe_pickw", [P, E, SLOTS], where=ph)
            pickT = sb("moe_pickT", [P, PAIRS, NT, P], where=ph)
            pair_w = sb("moe_pair_w", [P, 2, NT, P], where=ph)
            hidden = sb("moe_hidden", [P, 512], where=ph)
            actT = sb("moe_actT", [P, 4, P], where=ph)
            sg = sb("moe_sg", [P, 512], where=ph)
            y_sb = sb("moe_y", [P, 2, D], where=ph)
            wr = sb("moe_wr", [P, DC, GROUPS + E], where=ph)
            br = sb("moe_br", [P, GROUPS + E], where=ph)
            lg = sb("moe_lg", [P, NT, GROUPS + E], where=ph)
            chosen = sb("moe_chosen", [P, NT, E], where=ph)
            pg = sb("moe_pg", [P, NT, 8], where=ph)
            le = sb("moe_le", [P, NT, 8], where=ph)
            top = sb("moe_top", [P, NT, 2, 8], where=ph)
            topi = sb("moe_topi", [P, NT, 2, 8], U32, where=ph)
            idf = sb("moe_idf", [P, NT, 2, 8], where=ph)
            oh = sb("moe_oh", [P, NT, 4, 8], where=ph)
            sm = sb("moe_sm", [P, NT, 16], where=ph)
            gffn = sb("moe_gffn", [P, D], where=ph)
            ssum, meansq, rooted, normed = (signal(n) for n in ("squares_summed", "mean_squares", "rooted", "rows_normed"))
            turned, hT_done = signal("turned"), signal("hT_done")
            small, logits = signal("layer_small"), signal("logits")
            rt_in, rt_out = signal("route_exp_in"), signal("route_exp")
            (chose, ranked, picked, pick_turned, pick_copied, filled, copied, sigm, gated, acted, act_turned, act_copied,
             y_copied, pair_ready, scattered) = (signal(n) for n in (
                 "chosen", "ranked", "picked", "pick_turned", "pick_copied", "rows_picked", "rows_copied", "sigmoid_done",
                 "gated", "act_done", "act_turned", "act_copied", "y_copied", "pair_weights", "scattered"))
            OUT, YB, U1, U3 = 0, 4, 6, 7
            u0 = moe_at
            turns = PAIRS // TURN

            def up_done(p):
                return w_used, p * PAIR_UNITS + (u0 + 8)

            def down_done(p):
                return w_used, p * PAIR_UNITS + (u0 + 12)

            with nc.Block() as block:
                @block.sync
                def _(sp):
                    for dst, src in ((gffn[:, :], dram["norm_ffn_g"]), (wr[:, :, :], dram["w_route"]),
                                     (br[:, :], dram["b_route"]), (iota[:, :], dram["iota"]),
                                     (gfin[:, :], dram["norm_final_g"])):
                        sp.dma_start(dst, src).then_inc(small.sem, 16)
                    load_until(sp, u0 + TURN * PAIR_UNITS - RING)
                    with sp.Fori(1, turns - 1) as t:
                        u = u0
                        for k in range(TURN):
                            for w, e, half in moe_units(t * TURN + k):
                                sp.wait_ge(w_used, t * (TURN * PAIR_UNITS) + (u - RING + 1))
                                sp.dma_start(ring[:, u % RING, :], dram[w][e, half]).then_inc(w_land[u % RING], 16)
                                u += 1
                    issued[0] = u0 + TURN * PAIR_UNITS * (turns - 1)
                    load_until(sp, u0 + MOE_UNITS)

                @block.gpsimd
                def _(pool):
                    def pair(p, par):
                        if not isinstance(p, int) or p >= 2:
                            pool.wait_ge(*scattered.n(p - 1))
                        src = pickT[:, p, :, :] if isinstance(p, int) else pickT[:, bass.ds(p, 1), :, :].squeeze(1)
                        pool.tensor_copy(pair_w[:, par, :, :], src).then_inc(pair_ready.sem, 1)

                    pool.wait_ge(*pick_copied.n(8))
                    pair(0, 0)
                    pair(1, 1)
                    with pool.Fori(1, PAIRS // 2) as i:
                        for par in range(2):
                            pair(i * 2 + par, par)

                @block.scalar
                def _(act):
                    for i in range(NT):
                        act.activation(pickw[:, 0:16, :].rearrange("p e s -> p (e s)"), x_row[:, i, :], ACT.Square,
                                       accum_out=stat[:, i:i + 1]).then_inc(ssum.sem, 1)
                        act.wait_ge(*ssum.n(i + 1))
                    act.wait_ge(*meansq.n(1))
                    act.activation(stat[:, 2:4], stat[:, 2:4], ACT.Sqrt).then_inc(rooted.sem, 1)
                    turn_copies(act)
                    for k in range(2):
                        act.wait_ge(*rt_in.n(k + 1))
                        for i in range(NT):
                            v = pg[:, i, 0:GROUPS] if k == 0 else le[:, i, :]
                            act.activation(v, v, ACT.Exp, accum_out=sm[:, i, k:k + 1]).then_inc(rt_out.sem, 1)
                    for b in range(8):
                        act.wait_ge(*pick_turned.n(b + 1))
                        i, p = b // 4, 4 * (b % 4)
                        act.activation(pickT[:, p:p + 4, i, :], psum[:, b, :].rearrange("p (a t) -> p a t", a=4),
                                       ACT.Copy).then_inc(pick_copied.sem, 1)

                    def copy_rows(p, half):
                        act.wait_ge(*filled.n(p * 2 + (half + 1)))
                        act.activation(hT[:, 4 * half:4 * half + 4, 0:P],
                                       psum[:, (U3, U1)[half], :].rearrange("p (c s) -> p c s", c=4),
                                       ACT.Copy).then_inc(copied.sem, 1)

                    def pair(p, par, first=False, last=False):
                        act.wait_ge(*up_done(p))
                        if not first:
                            act.wait_ge(*acted.n(p))
                        act.activation(sg[:, :], psum[:, U1, :], ACT.Sigmoid).then_inc(sigm.sem, 1)
                        act.wait_ge(*act_turned.n(p + 1))
                        act.activation(actT[:, :, :], psum[:, U1, :].rearrange("p (j s) -> p j s", j=4),
                                       ACT.Copy).then_inc(act_copied.sem, 1)
                        if not last:
                            for half in range(2):
                                copy_rows(p + 1, half)
                        act.wait_ge(*down_done(p))
                        if not isinstance(p, int) or p >= 2:
                            act.wait_ge(*scattered.n(p - 1))
                        act.activation(y_sb[:, par, :].rearrange("p (h n) -> p h n", h=2), psum[:, YB:YB + 2, :],
                                       ACT.Copy).then_inc(y_copied.sem, 1)

                    act.wait_ge(*ranked.n(3))
                    for half in range(2):
                        copy_rows(0, half)
                    pair(0, 0, first=True)
                    pair(1, 1)
                    with act.Fori(1, turns - 1) as t:
                        for k in range(TURN):
                            pair(t * TURN + k, k)
                    pair(PAIRS - 2, 0)
                    pair(PAIRS - 1, 1, last=True)

                @block.tensor
                def _(pe):
                    pe_transpose(pe, n_row, normed.n(NT), turned)
                    pe.wait_ge(*small.n(80))
                    pe.wait_ge(*hT_done.n(4))
                    for i in range(NT):
                        for c in range(DC):
                            ins = pe.matmul(psum[:, 4 + i, 0:GROUPS + E], hT[:, c, i * P:(i + 1) * P], wr[:, c, :],
                                            start=(c == 0), stop=(c == DC - 1))
                        ins.then_inc(logits.sem, 1)
                    pe.wait_ge(*chose.n(1))
                    less, minus = C["neg00"], C["neg01"]
                    pe.matmul(psum[:, 6, 0:E], less, chosen[:, 0, :], start=True, stop=True).then_inc(ranked.sem, 1)
                    pe.matmul(psum[:, 6, E:2 * E], less, chosen[:, 1, :], start=True, stop=False)
                    pe.matmul(psum[:, 6, E:2 * E], minus, chosen[:, 0, :], start=False, stop=True).then_inc(ranked.sem, 1)
                    pe.matmul(psum[:, 6, 2 * E:3 * E], minus, chosen[:, 0, :], start=True, stop=False)
                    pe.matmul(psum[:, 6, 2 * E:3 * E], minus, chosen[:, 1, :], start=False, stop=True).then_inc(ranked.sem, 1)
                    for i in range(NT):
                        pe.wait_ge(*picked.n(2 * i + 2))
                        for b in range(4):
                            for k in range(4):
                                e = 2 * (4 * b + k)
                                ins = pe.transpose(psum[:, 4 * i + b, k * P:(k + 1) * P],
                                                   pickw[:, e:e + 2, :].rearrange("p e s -> p (e s)"), ident)
                            ins.then_inc(pick_turned.sem, 1)

                    def fill(p, half):
                        for c in range(4):
                            for i in range(NT):
                                v = pick[:, i, :, :].rearrange("p e s -> p (e s)")
                                v = v[:, p * P:(p + 1) * P] if isinstance(p, int) else v[:, bass.ds(p * P, P)]
                                at = (4 * half + c) * P
                                ins = pe.matmul(psum[:, (U3, U1)[half], c * P:(c + 1) * P], n_row[:, i, at:at + P], v,
                                                start=(i == 0), stop=(i == NT - 1))
                        ins.then_inc(filled.sem, 1)

                    def landed_at(k, p, par):
                        if isinstance(p, int):
                            return unit(pe, u0 + PAIR_UNITS * p + k)
                        v = u0 + PAIR_UNITS * par + k
                        pe.wait_ge(w_land[v % RING], p * (16 * PAIR_UNITS // RING)
                                   + (16 * (v // RING + 1) - 16 * PAIR_UNITS * par // RING))
                        return ring[:, v % RING, :]

                    def side_by_side(p, par, k, chunks, product):
                        wt = [landed_at(k + j, p, par).rearrange("p (c n) -> p c n", c=chunks) for j in range(2)]
                        for c in range(chunks):
                            ins = [product(j, wt[j], c) for j in range(2)]
                        for j in range(2):
                            ins[j].then_inc(w_used, 1)

                    def scatter(p, par, first=False, last=False):
                        pe.wait_ge(*y_copied.n(p + 1))
                        pe.wait_ge(*pair_ready.n(p + 1))
                        for i in range(NT):
                            for h in range(2):
                                ins = pe.matmul(psum[:, OUT + 2 * i + h, :], pair_w[:, par, i, :],
                                                y_sb[:, par, h * 512:(h + 1) * 512], start=first, stop=last)
                        ins.then_inc(scattered.sem, 1)

                    def pair(p, par, before=None, last=False):
                        rows = lambda j: slice(j * SLOTS, (j + 1) * SLOTS)
                        pe.wait_ge(*copied.n(p * 2 + 2))
                        for w, bank in enumerate((U1, U3)):
                            for half in range(2):
                                side_by_side(p, par, 4 * w + 2 * half, 4, lambda j, wt, c: pe.matmul(
                                    psum[rows(j), bank, :], hT[:, 4 * half + c, rows(j)], wt[:, c, :],
                                    start=(half == 0 and c == 0), stop=(half == 1 and c == 3)))
                        if before is not None:
                            before()
                        pe.wait_ge(*acted.n(p + 1))
                        for j in range(4):
                            ins = pe.transpose(psum[:, U1, j * P:(j + 1) * P], hidden[:, j * P:(j + 1) * P], ident)
                        ins.then_inc(act_turned.sem, 1)
                        if not last:
                            fill(p + 1, 0)
                        pe.wait_ge(*act_copied.n(p + 1))
                        if not last:
                            fill(p + 1, 1)
                        for half in range(2):
                            def down(j, wt, c):
                                for h in range(2):
                                    ins = pe.matmul(psum[rows(j), YB + h, :], actT[:, 2 * half + c, rows(j)],
                                                    wt[:, c, h * 512:(h + 1) * 512],
                                                    start=(half == 0 and c == 0), stop=(half == 1 and c == 1))
                                return ins
                            side_by_side(p, par, 8 + 2 * half, 2, down)

                    pe.wait_ge(*pick_copied.n(8))
                    for half in range(2):
                        fill(0, half)
                    pair(0, 0)
                    pair(1, 1, lambda: scatter(0, 0, first=True))
                    with pe.Fori(1, turns - 1) as t:
                        for k in range(TURN):
                            pair(t * TURN + k, k, lambda: scatter(t * TURN + (k - 1), 1 - k))
                    for p in (PAIRS - 2, PAIRS - 1):
                        pair(p, p % 2, lambda: scatter(p - 1, (p - 1) % 2), last=(p == PAIRS - 1))
                    scatter(PAIRS - 1, 1, last=True)

                @block.vector
                def _(dve):
                    link = lambda ins: dve_chain.link(dve, ins)
                    dve.wait_ge(*ssum.n(NT))
                    dve.tensor_scalar(stat[:, 2:4], stat[:, 0:2], 1.0 / D, 1e-6, ALU.mult, ALU.add).then_inc(meansq.sem, 1)
                    dve.wait_ge(*rooted.n(1))
                    link(dve.reciprocal(stat[:, 4:6], stat[:, 2:4]))
                    dve.wait_ge(*small.n(80))
                    for i in range(NT):
                        dve.scalar_tensor_tensor(out=n_row[:, i, :], in0=x_row[:, i, :], scalar=stat[:, 4 + i:5 + i],
                                                 in1=gffn[:, :], op0=ALU.mult, op1=ALU.mult).then_inc(normed.sem, 1)
                    dve.wait_ge(*normed.n(NT))

                    def each(step):
                        for i in range(NT):
                            ins = step(i)
                        link(ins)

                    link(dve.memset(pg[:, :, :], -1.0))
                    dve.wait_ge(*logits.n(NT))
                    each(lambda i: dve.tensor_tensor(lg[:, i, :], psum[:, 4 + i, 0:GROUPS + E], br[:, :], ALU.add))
                    each(lambda i: dve.tensor_reduce(sm[:, i, 2:3], lg[:, i, 0:GROUPS], AX.X, ALU.max))
                    for i in range(NT):
                        ins = dve.tensor_scalar(pg[:, i, 0:GROUPS], lg[:, i, 0:GROUPS], sm[:, i, 2:3], None, ALU.subtract)
                    ins.then_inc(rt_in.sem, 1)
                    dve.wait_ge(*rt_out.n(NT))
                    each(lambda i: dve.reciprocal(sm[:, i, 3:4], sm[:, i, 0:1]))
                    each(lambda i: dve.tensor_scalar(pg[:, i, 0:GROUPS], pg[:, i, 0:GROUPS], sm[:, i, 3:4], None, ALU.mult))
                    each(lambda i: dve.max(top[:, i, 0, :], pg[:, i, :]))
                    each(lambda i: dve.max_index(topi[:, i, 0, :], top[:, i, 0, :], pg[:, i, :]))
                    each(lambda i: dve.tensor_copy(idf[:, i, 0, :], topi[:, i, 0, :]))
                    each(lambda i: dve.tensor_scalar(oh[:, i, 0, :], iota[:, 0:8], idf[:, i, 0, 0:1], None, ALU.is_equal))
                    each(lambda i: dve.tensor_scalar(le[:, i, :], lg[:, i, GROUPS:GROUPS + 8], oh[:, i, 0, 0:1], None, ALU.mult))
                    for g in range(1, GROUPS):
                        each(lambda i: dve.scalar_tensor_tensor(
                            out=le[:, i, :], in0=lg[:, i, GROUPS + 8 * g:GROUPS + 8 * g + 8],
                            scalar=oh[:, i, 0, g:g + 1], in1=le[:, i, :], op0=ALU.mult, op1=ALU.add))
                    each(lambda i: dve.tensor_reduce(sm[:, i, 4:5], le[:, i, :], AX.X, ALU.max))
                    for i in range(NT):
                        ins = dve.tensor_scalar(le[:, i, :], le[:, i, :], sm[:, i, 4:5], None, ALU.subtract)
                    ins.then_inc(rt_in.sem, 1)
                    dve.wait_ge(*rt_out.n(2 * NT))
                    each(lambda i: dve.reciprocal(sm[:, i, 5:6], sm[:, i, 1:2]))
                    each(lambda i: dve.tensor_scalar(le[:, i, :], le[:, i, :], sm[:, i, 5:6], None, ALU.mult))
                    each(lambda i: dve.max(top[:, i, 1, :], le[:, i, :]))
                    each(lambda i: dve.max_index(topi[:, i, 1, :], top[:, i, 1, :], le[:, i, :]))
                    each(lambda i: dve.tensor_copy(idf[:, i, 1, :], topi[:, i, 1, :]))
                    each(lambda i: dve.tensor_tensor(sm[:, i, 6:7], top[:, i, 1, 0:1], top[:, i, 1, 1:2], ALU.add))
                    each(lambda i: dve.reciprocal(sm[:, i, 7:8], sm[:, i, 6:7]))
                    each(lambda i: dve.tensor_tensor(sm[:, i, 8:9], sm[:, i, 7:8], top[:, i, 0, 0:1], ALU.mult))
                    each(lambda i: dve.tensor_scalar(sm[:, i, 9:11], top[:, i, 1, 0:2], sm[:, i, 8:9], None, ALU.mult))
                    for k in range(2):
                        each(lambda i: dve.tensor_scalar(oh[:, i, 1 + k, :], iota[:, 0:8], idf[:, i, 1, k:k + 1], None,
                                                         ALU.is_equal))
                    each(lambda i: dve.tensor_tensor(oh[:, i, 3, :], oh[:, i, 1, :], oh[:, i, 2, :], ALU.add))
                    each(lambda i: dve.tensor_scalar(oh[:, i, 1, :], oh[:, i, 1, :], sm[:, i, 9:10], None, ALU.mult))
                    each(lambda i: dve.scalar_tensor_tensor(out=oh[:, i, 1, :], in0=oh[:, i, 2, :], scalar=sm[:, i, 10:11],
                                                            in1=oh[:, i, 1, :], op0=ALU.mult, op1=ALU.add))
                    for g in range(GROUPS):
                        for i in range(NT):
                            for dst, src in ((combine, 1), (chosen, 3)):
                                ins = dve.tensor_scalar(dst[:, i, 8 * g:8 * g + 8], oh[:, i, src, :], oh[:, i, 0, g:g + 1],
                                                        None, ALU.mult)
                    ins.then_inc(chose.sem, 1)
                    dve.wait_ge(*chose.n(1))

                    dve.wait_ge(*ranked.n(3))
                    flat = lambda a: a.rearrange("p i e -> p (i e)")
                    dve.tensor_reduce(sm[:, 0, 11:12], psum[:, 6, 2 * E:3 * E], AX.X, ALU.min)
                    link(dve.tensor_scalar(flat(rank[:, :, :]), psum[:, 6, 0:2 * E], -1.0, 1.0, ALU.mult, ALU.add))
                    dve.tensor_scalar(overflow[:, :], sm[:, 0, 11:12], -float(SLOTS), None, ALU.is_lt)
                    link(dve.tensor_tensor(rank[:, :, :], rank[:, :, :], chosen[:, :, :], ALU.mult))
                    link(dve.tensor_scalar(rank[:, :, :], rank[:, :, :], -1.0, None, ALU.add))
                    for i in range(NT):
                        shape = (P, E, SLOTS)
                        dve.tensor_tensor(pick[:, i, :, :], iota[:, 0:SLOTS].unsqueeze(1).broadcast_to(shape),
                                          rank[:, i, :].unsqueeze(2).broadcast_to(shape), ALU.is_equal).then_inc(picked.sem, 1)
                        dve.wait_ge(*picked.n(2 * i + 1))
                        if i > 0:
                            dve.wait_ge(*pick_turned.n(4))
                        dve.tensor_tensor(pickw[:, :, :], pick[:, i, :, :], combine[:, i, :].unsqueeze(2).broadcast_to(shape),
                                          ALU.mult).then_inc(picked.sem, 1)

                    with dve.Fori(0, PAIRS) as p:
                        dve.wait_ge(*sigm.n(p + 1))
                        dve.tensor_tensor(sg[:, :], sg[:, :], psum[:, U1, :], ALU.mult).then_inc(gated.sem, 1)
                        dve.wait_ge(*gated.n(p + 1))
                        dve.tensor_tensor(hidden[:, :], sg[:, :], psum[:, U3, :], ALU.mult).then_inc(acted.sem, 1)
                    dve.wait_ge(*scattered.n(PAIRS))
                    for i in range(NT):
                        xr = x_row[:, i, :].rearrange("p (h n) -> p h n", h=2)
                        dve.tensor_tensor(xr, psum[:, OUT + 2 * i:OUT + 2 * i + 2, :], xr, ALU.add)
            advance(squares_summed=NT, mean_squares=1, rooted=1, rows_normed=NT, turned=4, hT_done=4, layer_small=80)
            ph.close()

        def moe_rest():
            ph = ExitStack()
            sel = sb("rest_sel", [P, NT, 2, P], where=ph)
            selT = sb("rest_selT", [P, NT, P], where=ph)
            rows = sb("rest_rows", [P, DC, P], where=ph)
            wbuf = sb("rest_w", [P, UNIT], where=ph)
            sg = sb("rest_sg", [P, 512], where=ph)
            hidden = sb("rest_hidden", [P, 512], where=ph)
            actT = sb("rest_actT", [P, 4, P], where=ph)
            y_sb = sb("rest_y", [P, D], where=ph)
            junk = sb("rest_junk", [P, D], where=ph)
            ssum, meansq, rooted = (signal(n) for n in ("squares_summed", "mean_squares", "rooted"))
            (selected, r_picked, r_copied, land, used, r_sig, gated, r_act, r_turned, r_act_copied, r_y, r_sum) = (
                signal(n) for n in ("rest_selected", "rest_picked", "rest_copied", "rest_landed", "rest_used",
                                    "rest_sigmoid", "rest_gated", "rest_act", "rest_turned", "rest_act_copied",
                                    "rest_y_copied", "rest_sum"))
            ROUNDS = -(-(S - SLOTS) // P)
            SUM, YB, U1, U3 = 0, 4, 6, 7

            def for_each_expert(eng, step, before=None):
                flag = eng.value_load(overflow[0:1, 0:1], min_val=0, max_val=1)
                with eng.If(flag):
                    with eng.Fori(0, ROUNDS) as c:
                        if before is not None:
                            before(c)
                        with eng.Fori(0, E) as e:
                            step(e, c * E + e)

            with nc.Block() as block:
                @block.sync
                def _(sp):
                    def step(e, x):
                        units = [dram[w][e, half] for w in ("w1", "w3", "w2") for half in range(2)]
                        for k, src in enumerate(units):
                            sp.wait_ge(*used.n(x * 6 + k))
                            sp.dma_start(wbuf[:, :], src).then_inc(land.sem, 16)
                    for_each_expert(sp, step)

                @block.scalar
                def _(act):
                    def step(e, x):
                        act.wait_ge(*used.n(x * 6 + 4))
                        act.activation(sg[:, :], psum[:, U1, :], ACT.Sigmoid).then_inc(r_sig.sem, 1)
                    for_each_expert(act, step)
                    act.wait_ge(*signal("moe_summed").n(1))
                    for i in range(NT):
                        act.activation(junk[:, :], x_row[:, i, :], ACT.Square,
                                       accum_out=stat[:, i:i + 1]).then_inc(ssum.sem, 1)
                        act.wait_ge(*ssum.n(i + 1))
                    act.wait_ge(*meansq.n(1))
                    act.activation(stat[:, 2:4], stat[:, 2:4], ACT.Sqrt).then_inc(rooted.sem, 1)

                @block.tensor
                def _(pe):
                    def step(e, x):
                        pe.wait_ge(*selected.n(x + 1))
                        for c in range(DC):
                            for i in range(NT):
                                ins = pe.matmul(psum[:, YB + c // 4, c % 4 * P:(c % 4 + 1) * P],
                                                n_row[:, i, c * P:(c + 1) * P], sel[:, i, 0, :],
                                                start=(i == 0), stop=(i == NT - 1))
                        for i in range(NT):
                            ins = pe.transpose(psum[:, U1, i * P:(i + 1) * P], sel[:, i, 1, :], ident)
                        ins.then_inc(r_picked.sem, 1)
                        pe.wait_ge(*r_copied.n(x + 1))
                        for w, bank in enumerate((U1, U3)):
                            for half in range(2):
                                pe.wait_ge(*land.n(x * 96 + 16 * (2 * w + half + 1)))
                                wt = wbuf[:, :].rearrange("p (c n) -> p c n", c=4)
                                for c in range(4):
                                    ins = pe.matmul(psum[:, bank, :], rows[:, 4 * half + c, :], wt[:, c, :],
                                                    start=(half == 0 and c == 0), stop=(half == 1 and c == 3))
                                ins.then_inc(used.sem, 1)
                        pe.wait_ge(*r_act.n(x + 1))
                        for j in range(4):
                            ins = pe.transpose(psum[:, U1, j * P:(j + 1) * P], hidden[:, j * P:(j + 1) * P], ident)
                        ins.then_inc(r_turned.sem, 1)
                        pe.wait_ge(*r_act_copied.n(x + 1))
                        for half in range(2):
                            pe.wait_ge(*land.n(x * 96 + 16 * (half + 5)))
                            wt = wbuf[:, :].rearrange("p (c n) -> p c n", c=2)
                            for cc in range(2):
                                for h in range(2):
                                    j = 2 * half + cc
                                    ins = pe.matmul(psum[:, YB + h, :], actT[:, j, :], wt[:, cc, h * 512:(h + 1) * 512],
                                                    start=(j == 0), stop=(j == 3))
                            ins.then_inc(used.sem, 1)
                        pe.wait_ge(*r_y.n(x + 1))
                        for i in range(NT):
                            for h in range(2):
                                ins = pe.matmul(psum[:, SUM + 2 * i + h, :], selT[:, i, :], y_sb[:, h * 512:(h + 1) * 512],
                                                start=True, stop=True)
                        ins.then_inc(r_sum.sem, 1)
                    for_each_expert(pe, step)

                @block.vector
                def _(dve):
                    def before(c):
                        dve.drain()
                        dve.tensor_scalar(rank[:, :, :], rank[:, :, :], -float(P), None, ALU.add)

                    def step(e, x):
                        dve.drain()
                        for i in range(NT):
                            r, w = rank[:, i, bass.ds(e, 1)], combine[:, i, bass.ds(e, 1)]
                            dve.tensor_scalar(sel[:, i, 0, :], iota[:, :], r, None, ALU.is_equal)
                            ins = dve.tensor_scalar(sel[:, i, 1, :], iota[:, :], r, w, ALU.is_equal, ALU.mult)
                        ins.then_inc(selected.sem, 1)
                        dve.wait_ge(*r_picked.n(x + 1))
                        dve.tensor_copy(selT[:, :, :], psum[:, U1, 0:NT * P].rearrange("p (i t) -> p i t", i=NT))
                        dve.tensor_copy(rows[:, :, :].rearrange("p (b c) s -> p b (c s)", b=2),
                                        psum[:, YB:YB + 2, :]).then_inc(r_copied.sem, 1)
                        dve.wait_ge(*r_sig.n(x + 1))
                        dve.tensor_tensor(sg[:, :], sg[:, :], psum[:, U1, :], ALU.mult).then_inc(gated.sem, 1)
                        dve.wait_ge(*gated.n(x + 1))
                        dve.tensor_tensor(hidden[:, :], sg[:, :], psum[:, U3, :], ALU.mult).then_inc(r_act.sem, 1)
                        dve.wait_ge(*r_turned.n(x + 1))
                        dve.tensor_copy(actT[:, :, :],
                                        psum[:, U1, :].rearrange("p (j s) -> p j s", j=4)).then_inc(r_act_copied.sem, 1)
                        dve.wait_ge(*used.n(x * 6 + 6))
                        dve.tensor_copy(y_sb[:, :].rearrange("p (h n) -> p h n", h=2), psum[:, YB:YB + 2, :]).then_inc(r_y.sem, 1)
                        dve.wait_ge(*r_sum.n(x + 1))
                        for i in range(NT):
                            xr = x_row[:, i, :].rearrange("p (h n) -> p h n", h=2)
                            dve.tensor_tensor(xr, psum[:, SUM + 2 * i:SUM + 2 * i + 2, :], xr, ALU.add)

                    dve.drain()
                    dve.tensor_scalar(rank[:, :, :], rank[:, :, :], float(P - SLOTS), None, ALU.add)
                    for_each_expert(dve, step, before)
                    dve.drain()
                    dve.engine_nop().then_inc(signal("moe_summed").sem, 1)
                    dve.wait_ge(*ssum.n(NT))
                    dve.tensor_scalar(stat[:, 2:4], stat[:, 0:2], 1.0 / D, 1e-6, ALU.mult, ALU.add).then_inc(meansq.sem, 1)
                    dve.wait_ge(*rooted.n(1))
                    dve_chain.link(dve, dve.reciprocal(stat[:, 4:6], stat[:, 2:4]))
                    for i in range(NT):
                        dve.scalar_tensor_tensor(out=x_row[:, i, :], in0=x_row[:, i, :], scalar=stat[:, 4 + i:5 + i],
                                                 in1=gfin[:, :], op0=ALU.mult, op1=ALU.mult)
            advance(squares_summed=NT, mean_squares=1, rooted=1)
            ph.close()
            shared.close()

        def ada_pe(pe, u):
            for k in range(ADA_UNITS):
                w = unit(pe, u + k).rearrange("p (c n) -> p c n", c=DC)
                if k >= 4:
                    pe.wait_ge(*signal("mod_added").n(k - 3))
                for c in range(DC):
                    ins = pe.matmul(psum[:, k % 4, 0:S], condb[:, c, :], w[:, c, :], start=(c == 0), stop=(c == DC - 1))
                ins.then_inc(w_used, 1)

        def ada_dve(dve, u, bias_landed):
            dve.wait_ge(*bias_landed)
            added = signal("mod_added")
            for k in range(ADA_UNITS):
                dve.wait_ge(w_used, u + k + 1)
                dve.tensor_tensor(mod[:, k * S:(k + 1) * S], mod[:, k * S:(k + 1) * S], psum[:, k % 4, 0:S],
                                  ALU.add).then_inc(added.sem, 1)
            dve.wait_ge(*added.n(ADA_UNITS))
            dve_chain.link(dve, dve.tensor_scalar(mod[:, D:2 * D], mod[:, D:2 * D], 1.0, None, ALU.add))
            for i in range(NT):
                ins = dve.tensor_tensor(n_row[:, i, :], x_row[:, i, :], mod[:, D:2 * D], ALU.mult)
            dve_chain.link(dve, ins)
            for i in range(NT):
                dve.tensor_tensor(n_row[:, i, :], n_row[:, i, :], mod[:, 0:D],
                                  ALU.add).then_inc(signal("rows_normed").sem, 1)

        def turn_copies(act):
            for b in range(4):
                act.wait_ge(*signal("turned").n(b + 1))
                act.activation(hT[:, 2 * b:2 * b + 2, :], psum[:, b, :].rearrange("p (j s) -> p j s", j=2),
                               ACT.Copy).then_inc(signal("hT_done").sem, 1)

        def residual_norm_dve(dve, banks, gb, gb_landed, root):
            link = lambda ins: dve_chain.link(dve, ins)
            for i in range(NT):
                ins = dve.tensor_tensor(n_row[:, i, :].rearrange("p (h n) -> p h n", h=2),
                                        psum[:, banks + 2 * i:banks + 2 * i + 2, :],
                                        mod[:, 2 * D:3 * D].rearrange("p (h n) -> p h n", h=2), ALU.mult)
            link(ins)
            for i in range(NT):
                ins = dve.scalar_tensor_tensor(out=x_row[:, i, :], in0=x_row[:, i, :], scalar=float(ALPHA),
                                               in1=n_row[:, i, :], op0=ALU.mult, op1=ALU.add)
            link(ins)
            for i in range(NT):
                for h in range(2):
                    ins = dve.bn_stats(stat[:, 16 + 12 * i + 6 * h:22 + 12 * i + 6 * h], x_row[:, i, h * 512:(h + 1) * 512])
            link(ins)
            for i in range(NT):
                ins = dve.bn_aggr(stat[:, 8 + 2 * i:10 + 2 * i], stat[:, 16 + 12 * i:28 + 12 * i])
            link(ins)
            var = stat[:, 8:12].rearrange("p (i k) -> p i k", k=2)[:, :, 1]
            dve.tensor_scalar(stat[:, 2:4], var, 1e-5, None, ALU.add).then_inc(signal("mean_squares").sem, 1)
            dve.wait_ge(*signal("rooted").n(root))
            link(dve.reciprocal(stat[:, 4:6], stat[:, 2:4]))
            for i in range(NT):
                ins = dve.tensor_scalar(x_row[:, i, :], x_row[:, i, :], stat[:, 8 + 2 * i:9 + 2 * i], stat[:, 4 + i:5 + i],
                                        ALU.subtract, ALU.mult)
            link(ins)
            dve.wait_ge(*gb_landed)
            for i in range(NT):
                ins = dve.tensor_tensor(x_row[:, i, :], x_row[:, i, :], gb[:, 0, :], ALU.mult)
            link(ins)
            for i in range(NT):
                ins = dve.tensor_tensor(x_row[:, i, :], x_row[:, i, :], gb[:, 1, :], ALU.add)
            return ins

        moe()
        moe_rest()
        if stop_after <= 2:
            return

        def attention(l):
            ph = ExitStack()
            projT = sb(f"att{l}_projT", [P, 20, S], where=ph)
            v_row = sb(f"att{l}_v_row", [P, 2, NT, 512], where=ph)
            hg = sb(f"att{l}_hg", [P, 8, 4 * S], where=ph)
            scT = sb(f"att{l}_scT", [P, 3, HG, P], where=ph)
            oT = sb(f"att{l}_oT", [P, 2, 4, S], where=ph)
            gb = sb(f"att{l}_gb", [P, 2, D], where=ph)
            u0 = layer_at[l]
            uq = u0 + ADA_UNITS
            um = uq + 14
            uo = um + 12
            end = uo + 4
            fa, qa, ga, qb, kb = (projT[:, 4 * n:4 * n + 4, :] for n in range(5))
            kT, bufA, bufB = (hg[:, n, :] for n in range(3))
            dec = [hg[:, 1, :], hg[:, 3, :]]
            qd = [hg[:, 4, :], hg[:, 5, :]]
            kd = [hg[:, 6, :], hg[:, 7, :]]
            heads = lambda a: a.rearrange("p (h s) -> p h s", h=HG)
            small = signal("layer_small")
            (turned, hT_done, normed, proj_out, gates_exp, logf_in, logf, d_in, decay, q_dec, k_dec, lvl, lvl_used, meansq,
             rooted, o_done, osq, oss, sg_done, z_done, soft, logs, inc, w_in, w_done, ob_done, ob_out, o_ready, gsig,
             merged, lbs) = (signal(n) for n in (
                 "turned", "hT_done", "rows_normed", "att_proj_copied", "forget_exps", "forget_in", "forget_log",
                 "decay_in", "decay", "q_decayed", "k_decayed", "level_products", "level_kept", "mean_squares", "rooted",
                 "hgrn_out", "hgrn_squares", "hgrn_sums", "silu_gate", "stick_z", "stick_soft", "stick_logs", "stick_sums",
                 "stick_w_in", "stick_w", "stick_out", "stick_copied", "heads_ready", "gates_sigmoid", "merged", "bounds"))
            sa, ls, wt = (hg[:, n, 0:768].rearrange("p (b n) -> p b n", b=2) for n in (2, 3, 6))
            mT = hg[:, 0:2, :].rearrange("p a (c s) -> p (a c) s", c=4)
            gate_sig = heads(hg[:, 4, :])
            LEVELS = (128, 64, 32, 16, 8, 4, 2, 1, 0)

            with nc.Block() as block:
                @block.sync
                def _(sp):
                    sp.dma_start(mod[:, :], dram["b_ada_2"][l, 0]).then_inc(small.sem, 16)
                    for k, n in enumerate(("ln_g_2", "ln_b_2")):
                        sp.dma_start(gb[:, k, :], dram[n][l, 0]).then_inc(signal("ln_rows").sem, 16)
                    load_until(sp, end)

                @block.gpsimd
                def _(pool):
                    pool.memset(scT[:, :, :, :], 0.0).then_inc(signal("scores_zero").sem, 1)
                    for n in range(8):
                        pool.wait_ge(*decay.n(n + 1))
                        pool.wait_ge(*logf_in.n(2))
                        if n >= 2:
                            pool.wait_ge(*lvl.n(n - 1))
                        pool.tensor_tensor(kd[n % 2], kT, dec[n % 2], ALU.mult).then_inc(k_dec.sem, 1)

                @block.scalar
                def _(act):
                    if l == 0:
                        act.activation(stat[:, 40:48], col("c_2", 0, 8), ACT.Sigmoid).then_inc(lbs.sem, 1)
                        act.wait_ge(*lbs.n(2))
                        act.activation(lb[:, 2, :], lb[:, 2, :], ACT.Exp).then_inc(lbs.sem, 1)
                    turn_copies(act)
                    for k in range(14):
                        act.wait_ge(w_used, uq + k + 1)
                        bank = psum[:, 4 + k % 4, :].rearrange("p (j s) -> p j s", j=2)
                        if k in (6, 7, 12, 13):
                            n = 0 if k < 8 else 1
                            at = (k % 2) * S
                            act.activation(v_row[:, n, :, at:at + S], bank, ACT.Copy).then_inc(proj_out.sem, 1)
                        else:
                            at = 2 * (k if k < 6 else k - 2)
                            act.activation(projT[:, at:at + 2, :], bank, ACT.Copy,
                                           scale=0.125 if k in (8, 9) else 1.0).then_inc(proj_out.sem, 1)
                        if k == 1:
                            act.wait_ge(*proj_out.n(2))
                            act.activation(heads(bufA), fa, ACT.Exp, scale=-1.0).then_inc(gates_exp.sem, 1)
                            act.activation(heads(kT), fa, ACT.Exp).then_inc(gates_exp.sem, 1)
                    act.wait_ge(*logf_in.n(1))
                    act.activation(bufA, bufA, ACT.Ln).then_inc(logf.sem, 1)
                    for n in range(8):
                        act.wait_ge(*d_in.n(n + 1))
                        act.activation(dec[n % 2], dec[n % 2], ACT.Exp).then_inc(decay.sem, 1)
                    act.wait_ge(*meansq.n(1))
                    act.activation(gate_sig, ga, ACT.Sigmoid).then_inc(sg_done.sem, 1)
                    act.activation(dec[0], dec[0], ACT.Sqrt).then_inc(rooted.sem, 1)

                    def softplus_part(h):
                        a = sa[:, h % 2, :]
                        act.wait_ge(*z_done.n(h + 1))
                        if h >= 2:
                            act.wait_ge(*logs.n(h - 1))
                        act_chain.link(act, act.activation(a, psum[:, 4 + h % 2, 0:384], ACT.Abs))
                        act_chain.link(act, act.activation(a, a, ACT.Exp, scale=-1.0))
                        act.activation(a, a, ACT.Ln, bias=1.0).then_inc(soft.sem, 1)

                    softplus_part(0)
                    softplus_part(1)
                    for h in range(SB):
                        act.wait_ge(*w_in.n(h + 1))
                        act.activation(wt[:, h % 2, :], wt[:, h % 2, :], ACT.Exp).then_inc(w_done.sem, 1)
                        if h + 2 < SB:
                            softplus_part(h + 2)
                        if h % 2 == 1:
                            act.wait_ge(*ob_done.n(h + 1))
                            act.activation(oT[:, 1, h // 2, :], psum[:, (h // 2) % 2, 0:S], ACT.Copy).then_inc(ob_out.sem, 1)
                    for q in range(2):
                        act.wait_ge(w_used, um + 6 * q + 4)
                        if q == 1:
                            act.wait_ge(*merged.n(1))
                        act.activation(hg[:, 4:6, :].rearrange("p a (b n) -> p (a b) n", b=2), psum[:, 0:4, :],
                                       ACT.Sigmoid).then_inc(gsig.sem, 1)
                    act.wait_ge(*meansq.n(2))
                    act.activation(stat[:, 2:4], stat[:, 2:4], ACT.Sqrt).then_inc(rooted.sem, 1)

                @block.tensor
                def _(pe):
                    if l == 0:
                        pe.wait_ge(*lbs.n(4))
                    ada_pe(pe, u0)
                    pe_transpose(pe, n_row, normed.n(NT), turned)
                    pe.wait_ge(*hT_done.n(4))
                    for k in range(14):
                        w = unit(pe, uq + k).rearrange("p (c n) -> p c n", c=DC)
                        if k >= 4:
                            pe.wait_ge(*proj_out.n(k - 3))
                        for j in range(2):
                            for c in range(DC):
                                if k in (6, 7, 12, 13):
                                    a, b = hT[:, c, j * P:(j + 1) * P], w[:, c, :]
                                else:
                                    a, b = w[:, c, j * P:(j + 1) * P], hT[:, c, :]
                                ins = pe.matmul(psum[:, 4 + k % 4, j * S:(j + 1) * S], a, b,
                                                start=(c == 0), stop=(c == DC - 1))
                        ins.then_inc(w_used, 1)
                    for n, m in enumerate(LEVELS):
                        if m:
                            pe.wait_ge(*q_dec.n(n + 1))
                            pe.wait_ge(*k_dec.n(n + 1))
                        if n >= 2:
                            pe.wait_ge(*lvl_used.n(n - 1))
                        kk, qq = (heads(kd[n % 2]), heads(qd[n % 2])) if m else (heads(kT), qa)
                        for i in range(NT) if m < P else (0,):
                            for h in range(HG):
                                ti = slice(P, 2 * P) if m == P else slice(i * P, (i + 1) * P)
                                ins = pe.matmul(psum[:, 2 * (n % 2) + i, h * P:(h + 1) * P],
                                                kk[:, h, i * P:(i + 1) * P], qq[:, h, ti], start=True, stop=True)
                        ins.then_inc(lvl.sem, 1)
                    pe.wait_ge(*lvl_used.n(len(LEVELS)))
                    for h in range(HG):
                        v = [v_row[:, 0, i, h * P:(h + 1) * P] for i in range(NT)]
                        at = (h % 2) * S
                        pe.matmul(psum[:, h // 2, at:at + P], v[0], scT[:, 0, h, :], start=True, stop=True)
                        pe.matmul(psum[:, h // 2, at + P:at + S], v[0], scT[:, 2, h, :], start=True, stop=False)
                        ins = pe.matmul(psum[:, h // 2, at + P:at + S], v[1], scT[:, 1, h, :], start=False, stop=True)
                    ins.then_inc(o_done.sem, 1)
                    pe.wait_ge(*osq.n(1))
                    for b in range(2):
                        ins = pe.matmul(psum[:, 2 + b, :], C["ones"], bufA[:, b * 512:(b + 1) * 512], start=True, stop=True)
                    ins.then_inc(oss.sem, 1)

                    tri, ones = C["tri"], C["ones"]

                    def qk(h, i, out, lo, hi, stop):
                        r = slice(64 * (h % 2), 64 * (h % 2) + 64)
                        return pe.matmul(out, kb[r, h // 2, i * P:(i + 1) * P], qb[r, h // 2, lo:hi], start=True, stop=stop)

                    def z(h):
                        qk(h, 0, psum[:, 4 + h % 2, 0:S], 0, S, True)
                        qk(h, 1, psum[:, 4 + h % 2, S:S + P], P, S, True).then_inc(z_done.sem, 1)

                    def weighted(h):
                        pe.wait_ge(*w_done.n(h + 1))
                        r = slice(64 * (h % 2), 64 * (h % 2) + 64)
                        c = h // 2
                        if c >= 2:
                            pe.wait_ge(*ob_out.n(c - 1))
                        o = psum[r, c % 2, :]
                        v = [v_row[:, 1, i, h * 64:(h + 1) * 64] for i in range(NT)]
                        pe.matmul(o[:, 0:P], v[0], wt[:, h % 2, 0:P], start=True, stop=True)
                        pe.matmul(o[:, P:S], v[0], wt[:, h % 2, P:S], start=True, stop=False)
                        pe.matmul(o[:, P:S], v[1], wt[:, h % 2, S:S + P], start=False, stop=True).then_inc(ob_done.sem, 1)

                    pe.wait_ge(*proj_out.n(14))
                    z(0)
                    z(1)
                    for h in range(SB):
                        pe.wait_ge(*logs.n(h + 1))
                        if h >= 2:
                            pe.wait_ge(*w_in.n(h - 1))
                        b, L = psum[:, 6 + h % 2, :], ls[:, h % 2, :]
                        qk(h, 0, b[:, 0:S], 0, S, False)
                        pe.matmul(b[:, P:S], ones, L[:, S:S + P], start=False, stop=False)
                        pe.matmul(b[:, 0:S], tri, L[:, 0:S], start=False, stop=True)
                        qk(h, 1, b[:, S:S + P], P, S, False)
                        pe.matmul(b[:, S:S + P], tri, L[:, S:S + P], start=False, stop=True).then_inc(inc.sem, 1)
                        if h >= 1:
                            weighted(h - 1)
                        if h + 2 < SB:
                            z(h + 2)
                    weighted(SB - 1)

                    pe.wait_ge(*o_ready.n(1))
                    pe.wait_ge(*ob_out.n(4))
                    for q in range(2):
                        for k in range(4):
                            w = unit(pe, um + 6 * q + k).rearrange("p (c n) -> p c n", c=DC)
                            if q == 1 and k == 0:
                                pe.wait_ge(*gsig.n(1))
                            for j in range(2):
                                for c in range(DC):
                                    ins = pe.matmul(psum[:, k, j * S:(j + 1) * S], w[:, c, j * P:(j + 1) * P],
                                                    hT[:, c, :], start=(c == 0), stop=(c == DC - 1))
                            ins.then_inc(w_used, 1)
                        for k in range(2):
                            w = unit(pe, um + 6 * q + 4 + k).rearrange("p (c n) -> p c n", c=4)
                            if q == 1 and k == 0:
                                pe.wait_ge(*merged.n(1))
                            for j in range(4):
                                for c in range(4):
                                    ins = pe.matmul(psum[:, 4 + 2 * k + j // 2, (j % 2) * S:(j % 2) * S + S],
                                                    w[:, c, j * P:(j + 1) * P], oT[:, k, c, :],
                                                    start=(c == 0), stop=(c == 3))
                            ins.then_inc(w_used, 1)
                    pe.wait_ge(*merged.n(2))
                    for k in range(4):
                        w = unit(pe, uo + k).rearrange("p (c n) -> p c n", c=2)
                        for cc in range(2):
                            for i in range(NT):
                                for hh in range(2):
                                    ins = pe.matmul(psum[:, 2 * i + hh, :], mT[:, 2 * k + cc, i * P:(i + 1) * P],
                                                    w[:, cc, hh * 512:(hh + 1) * 512],
                                                    start=(k == 0 and cc == 0), stop=(k == 3 and cc == 1))
                        ins.then_inc(w_used, 1)

                @block.vector
                def _(dve):
                    link = lambda ins: dve_chain.link(dve, ins)
                    if l == 0:
                        dve.wait_ge(*lbs.n(1))
                        link(dve.tensor_tensor(stat[:, 40:48], stat[:, 40:48], col("c_2", 0, 8), ALU.mult))
                        for c in range(DC):
                            ins = dve.tensor_scalar(condb[:, c, :], C["ones"], stat[:, 40 + c:41 + c], None, ALU.mult)
                        l0, l1 = col("lb_logits_2", 0, 4), col("lb_logits_2", 4, 4)
                        link(dve.tensor_tensor(lb[:, 3, 0:4], l0, l1, ALU.max))
                        for k, v in enumerate((l0, l1)):
                            ins = dve.tensor_tensor(lb[:, 2, 4 * k:4 * k + 4], v, lb[:, 3, 0:4], ALU.subtract)
                        ins.then_inc(lbs.sem, 1)
                        dve.wait_ge(*lbs.n(3))
                        link(dve.tensor_tensor(lb[:, 3, 0:4], lb[:, 2, 0:4], lb[:, 2, 4:8], ALU.add))
                        link(dve.reciprocal(lb[:, 3, 0:4], lb[:, 3, 0:4]))
                        for k in range(2):
                            ins = dve.tensor_tensor(lb[:, 2, 4 * k:4 * k + 4], lb[:, 2, 4 * k:4 * k + 4], lb[:, 3, 0:4], ALU.mult)
                        link(ins)
                        dve.tensor_tensor(lb[:, 0, 0:4], lb[:, 2, 0:4], lb[:, 2, 0:4], ALU.subtract)
                        link(dve.tensor_tensor(lb[:, 0, 4:8], lb[:, 2, 0:4], lb[:, 2, 4:8], ALU.add))
                        link(dve.tensor_tensor(lb[:, 0, 4:8], lb[:, 0, 4:8], lb[:, 2, 0:4], ALU.subtract))
                        link(dve.tensor_scalar(lb[:, 1, :], lb[:, 0, :], -1.0, 1.0, ALU.mult, ALU.add))
                        dve.engine_nop().then_inc(lbs.sem, 1)
                    ada_dve(dve, u0, small.n(16))

                    dve.wait_ge(*gates_exp.n(2))
                    for b in (bufA, kT):
                        ins = dve.tensor_scalar(b, b, 1.0, None, ALU.add)
                    link(ins)
                    for b in (bufA, kT):
                        ins = dve.reciprocal(b, b)
                    link(ins)
                    for h in range(HG):
                        ins = dve.tensor_scalar(heads(bufA)[:, h, :], heads(bufA)[:, h, :], lb[:, 1, 4 * l + h:4 * l + h + 1],
                                                lb[:, 0, 4 * l + h:4 * l + h + 1], ALU.mult, ALU.add)
                    ins.then_inc(logf_in.sem, 1)
                    for h in range(HG):
                        ins = dve.tensor_scalar(heads(kT)[:, h, :], heads(kT)[:, h, :], lb[:, 1, 4 * l + h:4 * l + h + 1],
                                                None, ALU.mult)
                    ins.then_inc(logf_in.sem, 1)
                    dve.wait_ge(*logf.n(1))
                    src, dst = bufA, bufB
                    step = 1
                    while step < P:
                        a, b = (v.rearrange("p (x t) -> p x t", t=P) for v in (src, dst))
                        dve.tensor_copy(b[:, :, 0:step], a[:, :, 0:step])
                        link(dve.tensor_tensor(b[:, :, step:P], a[:, :, step:P], a[:, :, 0:P - step], ALU.add))
                        src, dst = dst, src
                        step *= 2
                    cum = src

                    def distances(n):
                        m = LEVELS[n]
                        if n >= 2:
                            dve.wait_ge(*k_dec.n(n - 1))
                            dve.wait_ge(*q_dec.n(n - 1))
                        b = cum.rearrange("p (x two m) -> p x two m", two=2, m=m)
                        d = dec[n % 2].rearrange("p (x two m) -> p x two m", two=2, m=m)
                        x = 4 * S // (2 * m)
                        ref = b[:, :, 0, m - 1:m].broadcast_to((P, x, m))
                        if m == P:
                            dve.tensor_copy(d[:, :, 1, :], b[:, :, 1, :])
                        else:
                            dve.tensor_tensor(d[:, :, 1, :], b[:, :, 1, :], ref, ALU.subtract)
                        dve.tensor_tensor(d[:, :, 0, :], ref, b[:, :, 0, :], ALU.subtract).then_inc(d_in.sem, 1)

                    def keep_level(n):
                        m = LEVELS[n]
                        dve.wait_ge(*lvl.n(n + 1))
                        if n >= 1:
                            dve.wait_ge(*lvl_used.n(n))
                        if m == P:
                            dve.wait_ge(*signal("scores_zero").n(1))
                            dve.tensor_copy(scT[:, 2, :, :], psum[:, 0, :].rearrange("p (h t) -> p h t", h=HG)).then_inc(lvl_used.sem, 1)
                            return
                        mask = (C[f"level{m}"] if m else ident).bitcast(U32).unsqueeze(1).broadcast_to((P, HG, P))
                        for i in range(NT):
                            ins = dve.copy_predicated(scT[:, i, :, :], mask,
                                                      psum[:, 2 * (n % 2) + i, :].rearrange("p (h t) -> p h t", h=HG))
                        ins.then_inc(lvl_used.sem, 1)

                    distances(0)
                    for n in range(8):
                        if n + 1 < 8:
                            distances(n + 1)
                        dve.wait_ge(*decay.n(n + 1))
                        dve.wait_ge(*proj_out.n(4))
                        if n >= 2:
                            dve.wait_ge(*lvl.n(n - 1))
                        dve.tensor_tensor(heads(qd[n % 2]), qa, heads(dec[n % 2]), ALU.mult).then_inc(q_dec.sem, 1)
                        if n >= 1:
                            keep_level(n - 1)
                    keep_level(7)
                    keep_level(8)

                    dve.wait_ge(*o_done.n(1))
                    link(dve.tensor_copy(oT[:, 0, :, :], psum[:, 0:2, :].rearrange("p b (h s) -> p (b h) s", h=2)))
                    dve.tensor_tensor(heads(bufA), oT[:, 0, :, :], oT[:, 0, :, :], ALU.mult).then_inc(osq.sem, 1)
                    dve.wait_ge(*oss.n(1))
                    dve.tensor_scalar(bufA.rearrange("p (b n) -> p b n", b=2), psum[:, 2:4, :], 1.0 / 128, 1e-6,
                                      ALU.mult, ALU.add).then_inc(meansq.sem, 1)
                    dve.wait_ge(*rooted.n(1))
                    link(dve.reciprocal(bufA, bufA))
                    for h in range(HG):
                        ins = dve.scalar_tensor_tensor(out=oT[:, 0, h, :], in0=oT[:, 0, h, :],
                                                       scalar=col("hg_norm_g_2", 4 * l + h), in1=heads(bufA)[:, h, :],
                                                       op0=ALU.mult, op1=ALU.mult)
                    link(ins)
                    dve.wait_ge(*sg_done.n(1))
                    dve.wait_ge(*proj_out.n(6))
                    link(dve.tensor_tensor(ga, ga, gate_sig, ALU.mult))
                    dve.tensor_tensor(oT[:, 0, :, :], oT[:, 0, :, :], ga, ALU.mult).then_inc(o_ready.sem, 1)
                    dve.wait_ge(*o_ready.n(1))

                    neg = const[:, CONSTS.index("neg00"):CONSTS.index("neg00") + 3, :]
                    fill = const[:, CONSTS.index("fill00"):CONSTS.index("fill00") + 3, :]
                    three = lambda a: a.rearrange("p (k t) -> p k t", k=3)

                    def log_one_minus_beta(h):
                        dve.wait_ge(*soft.n(h + 1))
                        if h >= 2:
                            dve.wait_ge(*inc.n(h - 1))
                        link(dve.scalar_tensor_tensor(out=ls[:, h % 2, :], in0=psum[:, 4 + h % 2, 0:384], scalar=0.0,
                                                      in1=sa[:, h % 2, :], op0=ALU.max, op1=ALU.add))
                        dve.tensor_tensor(three(ls[:, h % 2, :]), three(ls[:, h % 2, :]), neg, ALU.mult).then_inc(logs.sem, 1)

                    log_one_minus_beta(0)
                    for h in range(SB):
                        if h + 1 < SB:
                            log_one_minus_beta(h + 1)
                        dve.wait_ge(*inc.n(h + 1))
                        if h >= 2:
                            dve.wait_ge(*ob_done.n(h - 1))
                        dve.tensor_tensor(three(wt[:, h % 2, :]), three(psum[:, 6 + h % 2, 0:384]), fill,
                                          ALU.add).then_inc(w_in.sem, 1)

                    for q in range(2):
                        dve.wait_ge(*gsig.n(q + 1))
                        dve.wait_ge(w_used, um + 6 * q + 6)
                        sgm = hg[:, 4:6, :].rearrange("p a (b n) -> p (a b) n", b=2)
                        for k in range(2):
                            ins = dve.tensor_tensor(sgm[:, 2 * k:2 * k + 2, :], sgm[:, 2 * k:2 * k + 2, :],
                                                    psum[:, 4 + 2 * k:6 + 2 * k, :], ALU.mult)
                        link(ins)
                        dve.tensor_tensor(hg[:, q, :], hg[:, 4, :], hg[:, 5, :], ALU.add).then_inc(merged.sem, 1)
                    dve.wait_ge(w_used, end)
                    residual_norm_dve(dve, 0, gb, signal("ln_rows").n(32), 2)
            advance(mod_added=ADA_UNITS, rows_normed=NT, turned=4, hT_done=4, att_proj_copied=14, forget_exps=2, forget_in=2,
                    forget_log=1, decay_in=8, decay=8, q_decayed=8, k_decayed=8, level_products=9, level_kept=9,
                    mean_squares=2, rooted=2, hgrn_out=1, hgrn_squares=1, hgrn_sums=1, silu_gate=1, stick_z=SB,
                    stick_soft=SB, stick_logs=SB, stick_sums=SB, stick_w_in=SB, stick_w=SB, stick_out=SB, stick_copied=4,
                    heads_ready=1, gates_sigmoid=2, merged=2, layer_small=16, ln_rows=32, scores_zero=1)
            ph.close()

        GS = 8
        TURNS = K_ALL // GS

        def peer(l):
            ph = ExitStack()
            slots = sb(f"peer{l}_slots", [P, GS, D], where=ph)
            qT = sb(f"peer{l}_qT", [P, PH, S], where=ph)
            keysT = sb(f"peer{l}_keysT", [P, PH, P], where=ph)
            cand = sb(f"peer{l}_cand", [P, PH, TOPK, TOPK], where=ph)
            rest = sb(f"peer{l}_rest", [P, 2 * PH, P], where=ph)
            best = sb(f"peer{l}_best", [P, 2 * PH, TOPK], where=ph)
            besti = sb(f"peer{l}_besti", [P, 2 * PH, TOPK], U32, where=ph)
            bestf = sb(f"peer{l}_bestf", [P, 2 * PH, TOPK], where=ph)
            top = sb(f"peer{l}_top", [P, PH, TOPK], where=ph)
            pos = sb(f"peer{l}_pos", [P, 3, K_ALL], U32, where=ph)
            posf = sb(f"peer{l}_posf", [P, 2, K_ALL], where=ph)
            key = sb(f"peer{l}_key", [P, 2, K_ALL], where=ph)
            idx = sb(f"peer{l}_idx", [P, NT, K_ALL], U32, where=ph)
            gate = sb(f"peer{l}_gate", [P, NT, K_ALL], where=ph)
            gsum = sb(f"peer{l}_gsum", [P, PH], where=ph)
            pre = sb(f"peer{l}_pre", [P, NT, K_ALL], where=ph)
            dots = sb(f"peer{l}_dots", [P, GS], where=ph)
            staged_idx = sb(f"peer{l}_staged_idx", [P, GS], U32, where=ph)
            diag = sb(f"peer{l}_diag", [P, GS, P], where=ph)
            iota = sb(f"peer{l}_iota", [P, TOPK], where=ph)
            gb = sb(f"peer{l}_gb", [P, 2, D], where=ph)
            u0 = layer_at[l] + ADA_UNITS + ATT_UNITS
            uq = u0 + ADA_UNITS
            end = uq + PEER_UNITS
            small, ln_rows = signal("layer_small"), signal("ln_rows")
            (turned, hT_done, normed, q_out, scored, keys_kept, idx_ready, gate_in, gate_exp, u_used, v_used, kept, gelu_in,
             gelu, weights, diagd, staged, meansq, rooted) = (signal(n) for n in (
                 "turned", "hT_done", "rows_normed", "query_copied", "key_scores", "keys_kept", "indices_ready", "gate_in",
                 "gate_exp", "u_used", "v_used", "dots_kept", "gelu_in", "gelu", "expert_weights", "diagonal", "staged",
                 "mean_squares", "rooted"))
            landed = [signal(f"gathered{s}") for s in range(GS)]
            u_tab, v_tab = dram["peer_u_2"], dram["peer_v_2"]
            rows_of = PEER_ROWS * l

            with nc.Block() as block:
                @block.sync
                def _(sp):
                    sp.dma_start(mod[:, :], dram["b_ada_2"][l, 1]).then_inc(small.sem, 16)
                    sp.dma_start(keysT[:, :, :], dram["sub_keys_2"][l]).then_inc(small.sem, 16)
                    sp.dma_start(iota[:, :], dram["iota"][:, 0:TOPK]).then_inc(small.sem, 16)
                    for k, n in enumerate(("ln_g_2", "ln_b_2")):
                        sp.dma_start(gb[:, k, :], dram[n][l, 1]).then_inc(ln_rows.sem, 16)
                    load_until(sp, end)
                    if l == LAYERS - 1:
                        sp.wait_ge(*signal("result").n(1))
                        sp.dma_start(out, x_row[:, :, :]).then_inc(signal("stored").sem, 16)
                        sp.wait_ge(*signal("stored").n(16))

                @block.gpsimd
                def _(pool):
                    def stage(i, j, s, free):
                        pool.wait_ge(*free)
                        k = j * GS + s
                        column = idx[:, i, k:k + 1] if isinstance(k, int) else idx[:, i, bass.ds(k, 1)]
                        pool.tensor_copy(staged_idx[:, s:s + 1], column).then_inc(staged.sem, 1)

                    def gather(table, s):
                        pool.indirect_dma_start(
                            out=slots[:, s, :], out_offset=None, in_=table,
                            in_offset=bass.IndirectOffsetOnAxis(ap=staged_idx[:, s:s + 1], axis=0),
                        ).then_inc(landed[s].sem, 16)

                    at = 0
                    for i in range(NT):
                        pool.wait_ge(*idx_ready.n(i + 1))
                        for table, used, before in ((u_tab, u_used, v_used), (v_tab, v_used, u_used)):
                            for s in range(GS):
                                if s > 0:
                                    pool.wait_ge(*staged.n(at + s))
                                k = K_ALL * (i + (before is u_used)) - GS + s + 1
                                stage(i, 0, s, before.n(k) if k > 0 else idx_ready.n(i + 1))
                                if s > 0:
                                    gather(table, s - 1)
                            with pool.Fori(1, TURNS) as j:
                                for s in range(GS):
                                    pool.wait_ge(*staged.n(j * GS + (at + s)))
                                    stage(i, j, s, used.n(j * GS + (i * K_ALL - GS + s + 1)))
                                    gather(table, (s - 1) % GS)
                            at += K_ALL
                            pool.wait_ge(*staged.n(at))
                            gather(table, GS - 1)

                def arrived(eng, s, rnd, j):
                    eng.wait_ge(*landed[s].n(j * 16 + 16 * (rnd * TURNS + 1)))

                @block.scalar
                def _(act):
                    turn_copies(act)
                    for k in range(4):
                        act.wait_ge(w_used, uq + k + 1)
                        act.activation(qT[:, 2 * k:2 * k + 2, :], psum[:, 4 + k, :].rearrange("p (j s) -> p j s", j=2),
                                       ACT.Copy).then_inc(q_out.sem, 1)
                    for i in range(NT):
                        act.wait_ge(*gate_in.n(i + 1))
                        act.activation(gate[:, i, :], gate[:, i, :], ACT.Exp).then_inc(gate_exp.sem, 1)
                        act.wait_ge(*gelu_in.n(i + 1))
                        act.activation(pre[:, i, :], pre[:, i, :], ACT.Gelu).then_inc(gelu.sem, 1)
                        act.wait_ge(*weights.n(i + 1))

                        def diagonal(j, s):
                            k = j * GS + s
                            w = pre[:, i, k:k + 1] if isinstance(k, int) else pre[:, i, bass.ds(k, 1)]
                            if i > 0 or not isinstance(j, int):
                                act.wait_ge(*v_used.n(k + (i * K_ALL - GS + 1)))
                            act.activation(diag[:, s, :], ident, ACT.Copy, scale=w).then_inc(diagd.sem, 1)

                        for s in range(GS):
                            diagonal(0, s)
                        with act.Fori(1, TURNS) as j:
                            for s in range(GS):
                                diagonal(j, s)
                    act.wait_ge(*meansq.n(1))
                    act.activation(stat[:, 2:4], stat[:, 2:4], ACT.Sqrt).then_inc(rooted.sem, 1)

                @block.tensor
                def _(pe):
                    ada_pe(pe, u0)
                    pe_transpose(pe, n_row, normed.n(NT), turned)
                    pe.wait_ge(*hT_done.n(4))
                    for k in range(PEER_UNITS):
                        w = unit(pe, uq + k).rearrange("p (c n) -> p c n", c=DC)
                        for j in range(2):
                            for c in range(DC):
                                ins = pe.matmul(psum[:, 4 + k, j * S:(j + 1) * S], w[:, c, j * P:(j + 1) * P], hT[:, c, :],
                                                start=(c == 0), stop=(c == DC - 1))
                        ins.then_inc(w_used, 1)
                    pe.wait_ge(*small.n(48))
                    pe.wait_ge(*q_out.n(4))

                    def score(i):
                        for half in range(2):
                            r = slice(64 * half, 64 * half + 64)
                            for h in range(PH):
                                ins = pe.matmul(psum[:, 2 * half + h // 4, (h % 4) * P:(h % 4 + 1) * P],
                                                qT[r, h, i * P:(i + 1) * P], keysT[r, h, :], start=True, stop=True)
                        ins.then_inc(scored.sem, 1)

                    def add_row(i, j, s, first=False, last=False):
                        arrived(pe, s, 2 * i + 1, j)
                        pe.wait_ge(*diagd.n(j * GS + (i * K_ALL + s + 1)))
                        for h in range(2):
                            ins = pe.matmul(psum[:, 4 + 2 * i + h, :], diag[:, s, :], slots[:, s, h * 512:(h + 1) * 512],
                                            start=first, stop=last)
                        ins.then_inc(v_used.sem, 1)

                    score(0)
                    pe.wait_ge(*keys_kept.n(1))
                    score(1)
                    for i in range(NT):
                        for s in range(GS):
                            add_row(i, 0, s, first=(s == 0))
                        with pe.Fori(1, TURNS - 1) as j:
                            for s in range(GS):
                                add_row(i, j, s)
                        for s in range(GS):
                            add_row(i, TURNS - 1, s, last=(s == GS - 1))

                @block.vector
                def _(dve):
                    link = lambda ins: dve_chain.link(dve, ins)
                    ada_dve(dve, u0, small.n(48))

                    def top16(n, values, rest_of, val, ind):
                        for g in range(n):
                            ins = dve.max(val(g)[:, 0:8], values(g))
                        link(ins)
                        for g in range(n):
                            dve.max_index(ind(g)[:, 0:8], val(g)[:, 0:8], values(g))
                        for g in range(n):
                            ins = dve.match_replace(out=rest_of(g), in_to_replace=val(g)[:, 0:8], in_values=values(g),
                                                    imm_value=NEG)
                        link(ins)
                        for g in range(n):
                            ins = dve.max(val(g)[:, 8:16], rest_of(g))
                        link(ins)
                        for g in range(n):
                            ins = dve.max_index(ind(g)[:, 8:16], val(g)[:, 8:16], rest_of(g))
                        return ins

                    def route(i):
                        dve.wait_ge(*scored.n(i + 1))
                        top16(2 * PH, lambda g: psum[:, g // 4, (g % 4) * P:(g % 4 + 1) * P], lambda g: rest[:, g, :],
                              lambda g: best[:, g, :], lambda g: besti[:, g, :]).then_inc(keys_kept.sem, 1)
                        dve.wait_ge(*keys_kept.n(i + 1))
                        dve.tensor_copy(bestf[:, :, :], besti[:, :, :])
                        shape = (P, PH, TOPK, TOPK)
                        link(dve.tensor_tensor(cand[:, :, :, :], best[:, 0:PH, :].unsqueeze(3).broadcast_to(shape),
                                               best[:, PH:2 * PH, :].unsqueeze(2).broadcast_to(shape), ALU.add))
                        pos8 = pos[:, 0, :].rearrange("p (h k) -> p h k", h=PH)
                        flat = rest[:, :, :].rearrange("p (h a) n -> p h (a n)", h=PH)
                        link(top16(PH, lambda h: cand[:, h, :, :].rearrange("p a b -> p (a b)"), lambda h: flat[:, h, :],
                                   lambda h: top[:, h, :], lambda h: pos8[:, h, :]))
                        dve.tensor_scalar(pos[:, 1, :], pos[:, 0, :], 4, None, ALU.logical_shift_right)
                        link(dve.tensor_scalar(pos[:, 2, :], pos[:, 0, :], 15, None, ALU.bitwise_and))
                        link(dve.tensor_copy(posf[:, :, :], pos[:, 1:3, :]))
                        hot = rest[:, :, :].rearrange("p (h a) (b n) -> p h (a b) n", h=PH, n=TOPK)
                        for half in range(2):
                            p8 = posf[:, half, :].rearrange("p (h k) -> p h k", h=PH)
                            link(dve.tensor_tensor(hot, p8.unsqueeze(3).broadcast_to(shape),
                                                   iota[:, :].unsqueeze(1).unsqueeze(1).broadcast_to(shape), ALU.is_equal))
                            link(dve.tensor_tensor(hot, hot, bestf[:, half * PH:(half + 1) * PH, :].unsqueeze(2)
                                                   .broadcast_to(shape), ALU.mult))
                            link(dve.tensor_reduce(key[:, half, :].rearrange("p (h k) -> p h k", h=PH), hot, AX.X, ALU.add))
                        link(dve.tensor_scalar(key[:, 0, :], key[:, 0, :], float(P), float(rows_of), ALU.mult, ALU.add))
                        dve.tensor_tensor(idx[:, i, :], key[:, 0, :], key[:, 1, :], ALU.add).then_inc(idx_ready.sem, 1)
                        g3 = gate[:, i, :].rearrange("p (h k) -> p h k", h=PH)
                        dve.tensor_tensor(g3, top[:, :, :], top[:, :, 0:1].broadcast_to((P, PH, TOPK)),
                                          ALU.subtract).then_inc(gate_in.sem, 1)
                        dve.wait_ge(*gate_exp.n(i + 1))
                        link(dve.tensor_reduce(gsum[:, :], g3, AX.X, ALU.add))
                        link(dve.reciprocal(gsum[:, :], gsum[:, :]))
                        link(dve.tensor_tensor(g3, g3, gsum[:, :].unsqueeze(2).broadcast_to((P, PH, TOPK)), ALU.mult))

                    for i in range(NT):
                        route(i)
                        with dve.Fori(0, TURNS) as j:
                            if True:
                                for s in range(GS):
                                    arrived(dve, s, 2 * i, j)
                                    dve.tensor_tensor_reduce(out=slots[:, s, :], in0=slots[:, s, :], in1=n_row[:, i, :],
                                                             scale=1.0, scalar=0.0, op0=ALU.mult, op1=ALU.add,
                                                             accum_out=dots[:, s:s + 1]).then_inc(u_used.sem, 1)
                                dve.wait_ge(*u_used.n(j * GS + (i * K_ALL + GS)))
                                dve.tensor_copy(pre[:, i, bass.ds(j * GS, GS)], dots[:, :]).then_inc(kept.sem, 1)
                                dve.wait_ge(*kept.n(j + (i * TURNS + 1)))
                        dve.engine_nop().then_inc(gelu_in.sem, 1)
                        dve.wait_ge(*gelu.n(i + 1))
                        dve.tensor_tensor(pre[:, i, :], pre[:, i, :], gate[:, i, :], ALU.mult).then_inc(weights.sem, 1)
                    dve.wait_ge(*v_used.n(NT * K_ALL))
                    ins = residual_norm_dve(dve, 4, gb, ln_rows.n(32), 1)
                    if l == LAYERS - 1:
                        ins.then_inc(signal("result").sem, 1)
            advance(mod_added=ADA_UNITS, rows_normed=NT, turned=4, hT_done=4, layer_small=48, ln_rows=32, query_copied=4,
                    key_scores=NT, keys_kept=NT, indices_ready=NT, gate_in=NT, gate_exp=NT, u_used=NT * K_ALL,
                    v_used=NT * K_ALL, dots_kept=NT * TURNS, gelu_in=NT, gelu=NT, expert_weights=NT,
                    diagonal=NT * K_ALL, staged=2 * NT * K_ALL, mean_squares=1, rooted=1,
                    **{f"gathered{s}": 2 * NT * TURNS * 16 for s in range(GS)})
            ph.close()

        for l in range(LAYERS):
            attention(l)
            if stop_after <= 3 + 2 * l:
                return
            peer(l)
            if stop_after <= 4 + 2 * l:
                return


def column_vectors(v):
    import numpy as np
    parts = []
    for name in COLS:
        a = np.asarray(v[name]).reshape(-1, P)
        parts.append(a.T)
    return np.ascontiguousarray(np.concatenate(parts, axis=1))


def constant_matrices():
    import numpy as np
    s, t = np.arange(P)[:, None], np.arange(P)[None, :]
    m = {"ident": s == t, "ones": s >= 0 * t, "heads64": s // 64 == t // 64, "tri": s >= t,
         "neg00": -1.0 * (s < t), "neg01": -1.0 * (s >= 0 * t), "neg11": -1.0 * (s < t),
         "fill00": NEG * (s >= t), "fill01": 0.0 * (s >= t), "fill11": NEG * (s >= t)}
    for h in (64, 32, 16, 8, 4, 2, 1):
        m[f"level{h}"] = (s // (2 * h) == t // (2 * h)) & (s % (2 * h) < h) & (t % (2 * h) >= h)
    return np.ascontiguousarray(np.stack([np.broadcast_to(m[n], (P, P)).astype(np.float32) for n in CONSTS], axis=1))


def layouts(v):
    import numpy as np
    v = {k: np.asarray(a) for k, a in v.items()}

    def by_columns(w, n):
        *lead, k, cols = w.shape
        w = w.reshape(*lead, k // P, P, cols // n, n)
        i = len(lead)
        w = w.transpose(*range(i), i + 2, i + 1, i, i + 3)
        return np.ascontiguousarray(w.reshape(*lead, cols // n, P, k // P * n))

    def by_rows(w, c):
        *lead, k, cols = w.shape
        w = w.reshape(*lead, k // P // c, c, P, cols)
        i = len(lead)
        w = w.transpose(*range(i), i, i + 2, i + 1, i + 3)
        return np.ascontiguousarray(w.reshape(*lead, k // P // c, P, c * cols))

    def rows(a, n=P):
        return np.ascontiguousarray(np.broadcast_to(a.reshape(1, -1), (n, a.size)))

    out = {
        "x": v["x"].reshape(NT, P, D).transpose(1, 0, 2),
        "consts": constant_matrices(),
        "cols": column_vectors(v),
        "iota": rows(np.arange(P, dtype=np.float32)),
        "w_in": by_columns(v["w_in"][0], 256),
        "w_out": by_rows(v["w_out"][0], 2),
        "w_route": np.concatenate([v["w_route_group"][0], v["w_route_expert"][0]], axis=1)
                     .reshape(DC, P, GROUPS + E).transpose(1, 0, 2),
        "b_route": rows(np.concatenate([v["b_route_group"][0], v["b_route_expert"][0]])),
        "norm_ffn_g": rows(v["norm_ffn_g"]),
        "norm_final_g": rows(v["norm_final_g"]),
        "w1": by_rows(v["w1"][0], 4),
        "w3": by_rows(v["w3"][0], 4),
        "w2": by_rows(v["w2"][0], 2),
        "w_ada_2": by_columns(v["w_ada_2"], 256),
        "b_ada_2": np.broadcast_to(v["b_ada_2"].reshape(LAYERS, 2, 1, 3 * D), (LAYERS, 2, P, 3 * D)),
        "w_in_2": by_columns(v["w_in_2"], 256),
        "w_up_a_2": by_columns(v["w_up_a_2"], 512),
        "w_up_b_2": by_columns(v["w_up_b_2"], 512),
        "w_o_2": by_rows(v["w_o_2"], 2),
        "w_pq_2": by_columns(v["w_pq_2"], 256),
        "sub_keys_2": v["sub_keys_2"].transpose(0, 1, 4, 2, 3).reshape(LAYERS, P, PH, P),
        "peer_u_2": v["peer_u_2"].reshape(-1, D),
        "peer_v_2": v["peer_v_2"].reshape(-1, D),
        "ln_g_2": np.broadcast_to(v["ln_g_2"][:, :, None, :], (LAYERS, 2, P, D)),
        "ln_b_2": np.broadcast_to(v["ln_b_2"][:, :, None, :], (LAYERS, 2, P, D)),
    }
    return {k: np.ascontiguousarray(a) for k, a in out.items()}


def kernel(**inputs):
    import numpy as np
    import concourse.bacc as bacc
    from concourse.bass_utils import run_bass_kernel_spmd

    arrays = layouts(inputs)
    nc = bacc.Bacc("TRN2", target_bir_lowering=False, num_devices=1)
    dram = {n: nc.dram_tensor("in_" + n, a.shape, mybir.dt.from_np(a.dtype), kind="ExternalInput").ap()
            for n, a in arrays.items()}
    out = nc.dram_tensor("y", (P, NT, D), F32, kind="ExternalOutput").ap()
    build(nc, dram, out)
    got = run_bass_kernel_spmd(nc, [{"in_" + n: a for n, a in arrays.items()}], core_ids=[0]).results[0]["y"]
    return np.ascontiguousarray(got.transpose(1, 0, 2)).reshape(1, S, D)
```

```python
from contextlib import ExitStack

import concourse.bass as bass
from concourse import mybir

F32 = mybir.dt.float32
U32 = mybir.dt.uint32
ALU = mybir.AluOpType
ACT = mybir.ActivationFunctionType
AX = mybir.AxisListType

P = 128
D = 1024
S = 256
NT = S // P
DC = D // P
DA = 512
AC = DA // P
TAPS_A, TAPS_B = 3, 31
GROUPS, PER_GROUP = 4, 8
E = GROUPS * PER_GROUP
LAYERS = 2
HG = 4
SB = 8
PH, TOPK = 8, 16
K_ALL = PH * TOPK
PEER_ROWS = P * P
ALPHA = (2.0 * LAYERS) ** 0.25
NEG = -1.0e30

UNIT = 2048
RING = 8
TURN = 2
PAIR_UNITS = 12

ADA_UNITS = 24
MIX_UNITS = 10 + ADA_UNITS + 4
MOE_UNITS = 6 * E
PROJ_UNITS = 6 + 2 + 4 + 2 + 8
PEER_UNITS = 4
MODC = 6 * DC

COLS = {}
_at = 0
for _name, _n in (("norm_mix_g", 8), ("conv_a_w", TAPS_A * 4), ("conv_b_w", TAPS_B * 4), ("conv_b_bias", 4),
                  ("ln_b_g", 4), ("ln_b_b", 4), ("beta_a", 4), ("beta_b", 4), ("norm_ffn_g", 8), ("c_2", 8),
                  ("lb_logits_2", 8), ("hg_norm_g_2", 8), ("b_ada_2", LAYERS * MODC)):
    COLS[_name] = _at
    _at += _n
NCOLS = _at

CONSTS = ("ident", "ones", "heads64", "tri", "quarters",
          "neg00", "neg01", "neg11", "fill00", "fill01", "fill11") + tuple(f"level{m}" for m in (64, 32, 16, 8, 4, 2, 1))
NCONST = len(CONSTS)


class Signal:

    def __init__(self, sem):
        self.sem, self.base = sem, 0

    def n(self, k):
        return self.sem, self.base + k


class Chain:

    def __init__(self, sem):
        self.sem, self.count = sem, 0

    def link(self, eng, ins):
        self.count += 1
        ins.then_inc(self.sem, 1)
        eng.wait_ge(self.sem, self.count)


def build(nc, dram, out, stop_after=99):
    with ExitStack() as ctx:
        def sb(name, shape, dt=F32, where=ctx):
            return where.enter_context(nc.sbuf_tensor(name, shape, dt))

        def sem(name):
            return ctx.enter_context(nc.semaphore(name))

        signals = {}

        def signal(name):
            if name not in signals:
                signals[name] = Signal(sem(name))
            return signals[name]

        def advance(**made):
            for name, k in made.items():
                signals[name].base += k

        psum = ctx.enter_context(nc.psum_tensor("psum", [P, 8, 512], F32))
        ring = sb("ring", [P, RING, UNIT])
        x_row = sb("x_row", [P, NT, D])
        n_row = sb("n_row", [P, NT, D])
        hT = sb("hT", [P, DC, S])
        const = sb("const", [P, NCONST, P])
        cols = sb("cols", [P, NCOLS])
        stat = sb("stat", [P, 64])
        lb = sb("lb", [P, 4, 4 * LAYERS])
        modc = sb("modc", [P, LAYERS, MODC])
        C = {name: const[:, i, :] for i, name in enumerate(CONSTS)}
        ident = C["ident"]

        def col(name, k=0, n=1):
            return cols[:, COLS[name] + k:COLS[name] + k + n]

        loaded = sem("loaded")
        w_land = [sem(f"w_land{s}") for s in range(RING)]
        w_used = sem("w_used")
        dve_chain, act_chain = Chain(sem("dve_chain")), Chain(sem("act_chain"))

        stream = []
        stream += [dram["w_in"][u] for u in range(10)]
        stream += [dram["w_ada_2"][0, u] for u in range(ADA_UNITS)]
        stream += [dram["w_out"][u] for u in range(4)]
        moe_at = len(stream)

        def moe_units(p):
            return [(w, 2 * p + k, half) for w in ("w1", "w3", "w2") for half in range(2) for k in range(2)]

        for p in range(E // 2):
            stream += [dram[w][e, half] for w, e, half in moe_units(p)]
        def ada_slots(l, k):
            if l + 1 == LAYERS or k < 6:
                return (), ()
            return ((2 * k - 12,), (2 * k - 11,)) if k < 14 else ((), (k + 2,))

        layer_at, proj_at, ada_at = [], [], []
        for l in range(LAYERS):
            layer_at.append(len(stream))
            proj_order = (2, 3, 0, 1, 6, 7) + (4, 5) + (8, 9, 10, 11) + (12, 13) + tuple(range(14, 22))
            proj_at.append([])
            ada_at.append([])
            for k, u in enumerate(proj_order):
                within, behind = ada_slots(l, k)
                for a in within:
                    ada_at[l].append(len(stream))
                    stream.append(dram["w_ada_2"][l + 1, a])
                proj_at[l].append(len(stream))
                stream.append(dram["w_in_2"][l, u])
                for a in behind:
                    ada_at[l].append(len(stream))
                    stream.append(dram["w_ada_2"][l + 1, a])
            for q in range(2):
                stream += [dram["w_up_a_2"][l, q], dram["w_up_b_2"][l, q]]
            stream += [dram["w_o_2"][l, u] for u in range(4)]
            stream += [dram["w_pq_2"][l, u] for u in range(4)]
        assert moe_at == MIX_UNITS and layer_at[0] == MIX_UNITS + MOE_UNITS
        issued = [0]

        def load_unit(sp, u):
            if u >= RING:
                sp.wait_ge(w_used, u - RING + 1)
            sp.dma_start(ring[:, u % RING, :], stream[u]).then_inc(w_land[u % RING], 16)

        def load_until(sp, end):
            for u in range(issued[0], min(end + RING, len(stream))):
                load_unit(sp, u)
            issued[0] = min(end + RING, len(stream))

        def unit(pe, u):
            pe.wait_ge(w_land[u % RING], 16 * (u // RING + 1))
            return ring[:, u % RING, :]

        def pe_transpose(pe, src, ready, done, free=None):
            pe.wait_ge(*ready)
            for b in range(4):
                if free is not None:
                    pe.wait_ge(*free)
                for c in (2 * b, 2 * b + 1):
                    for i in range(NT):
                        at = (c % 2) * S + i * P
                        ins = pe.transpose(psum[:, b, at:at + P], src[:, i, c * P:(c + 1) * P], ident)
                ins.then_inc(done.sem, 1)


        SIDE = 256

        def ada_products(pe, u, bank):
            w = unit(pe, u).rearrange("p (c n) -> p c n", c=DC)
            for c in range(DC):
                g = 32 * (c % 4)
                ins = pe.matmul(psum[g:g + 32, bank, 0:SIDE], cond[:, c:c + 1].broadcast_to((P, 32)), w[:, c, :],
                                start=(c < 4), stop=(c >= 4))
            ins.then_inc(w_used, 1)

        def ada_stage(act, u, bank, par=0):
            act.wait_ge(w_used, u + 1)
            act.activation(ada_part[:, par, :], psum[:, bank, 0:SIDE], ACT.Copy).then_inc(signal("ada_staged").sem, 1)

        def ada_columns(pe, k, bank, par=0):
            pe.wait_ge(*signal("ada_staged").n(k + 1))
            for j in range(2):
                to = SIDE + 2 * k + j
                ins = pe.matmul(psum[:, bank, to:to + 1], ada_part[:, par, j * P:(j + 1) * P], C["quarters"][:, 0:1],
                                start=True, stop=True)
            if k == ADA_UNITS - 1:
                ins.then_inc(signal("ada_done").sem, 1)

        def ada_copy(act, l, bank):
            act.wait_ge(*signal("ada_done").n(1))
            act.activation(modc[:, l, :], psum[:, bank, SIDE:SIDE + MODC], ACT.Copy).then_inc(signal("mod_copied").sem, 1)

        def finish_modulation(dve, l):
            dve.wait_ge(*signal("mod_copied").n(1))
            dve_chain.link(dve, dve.tensor_tensor(modc[:, l, :], modc[:, l, :], col("b_ada_2", l * MODC, MODC), ALU.add))
            for part in (1, 4):
                v = modc[:, l, part * DC:(part + 1) * DC]
                ins = dve.tensor_scalar(v, v, 1.0, None, ALU.add)
            dve_chain.link(dve, ins)

        def modulation_rows(pe, l, sub, bank):
            for k in range(2 * DC):
                v = modc[:, l, 3 * DC * sub + k:3 * DC * sub + k + 1].broadcast_to((P, P))
                ins = pe.matmul(psum[:, bank + k // 4, k % 4 * P:(k % 4 + 1) * P], v, ident, start=True, stop=True)
            ins.then_inc(signal("mod_rows").sem, 1)

        def gate_rows(pe, l, sub, bank):
            for k in range(DC):
                at = 3 * DC * sub + 2 * DC + k
                ins = pe.matmul(psum[:, bank + k // 4, k % 4 * P:(k % 4 + 1) * P],
                                modc[:, l, at:at + 1].broadcast_to((P, P)), ident, start=True, stop=True)
            ins.then_inc(signal("gate_rows").sem, 1)

        def copy_gate_row(act, bank):
            act.wait_ge(*signal("gate_rows").n(1))
            act.activation(gate_row[:, :].rearrange("p (h n) -> p h n", h=2), psum[:, bank:bank + 2, :],
                           ACT.Copy).then_inc(signal("gate_row").sem, 1)

        def modulate(dve, bank):
            x, n = ([a[:, i, :].rearrange("p (h n) -> p h n", h=2) for i in range(NT)] for a in (x_row, n_row))
            dve.wait_ge(*signal("mod_rows").n(1))
            for i in range(NT):
                ins = dve.tensor_tensor(n[i], x[i], psum[:, bank + 2:bank + 4, :], ALU.mult)
            dve_chain.link(dve, ins)
            for i in range(NT):
                dve.tensor_tensor(n[i], n[i], psum[:, bank:bank + 2, :], ALU.add).then_inc(signal("rows_normed").sem, 1)

        def mixer():
            ph = ExitStack()
            projT = sb("mix_projT", [P, 20, S], where=ph)
            PA, PB = TAPS_A // 2, TAPS_B // 2
            ua = sb("mix_ua", [P, AC, S + 2 * PA], where=ph)
            ub = sb("mix_ub", [P, AC, S + 2 * PB], where=ph)
            sq = sb("mix_sq", [P, 2, AC * S], where=ph)
            yT = sb("mix_yT", [P, 2 * AC, S], where=ph)
            tmp = sb("mix_tmp", [P, AC * S], where=ph)
            ssum = signal("squares_summed")
            meansq = signal("mean_squares")
            rooted = signal("rooted")
            normed = signal("rows_normed")
            turned = signal("turned")
            hT_done = signal("hT_done")
            proj_out = signal("proj_copied")
            sig_in = signal("sig_in")
            sig = signal("sig_done")
            stat_in = signal("stat_in")
            stat_out = signal("stat_out")
            y_ready = signal("y_ready")
            cond_in = signal("cond_ready")
            mod_copied = signal("mod_copied")
            y3, t3 = yT[:, :, :], tmp[:, :].rearrange("p (c s) -> p c s", c=AC)

            with nc.Block() as block:
                @block.sync
                def _(sp):
                    for name, dst in (("x", x_row[:, :, :]), ("consts", const[:, :, :]), ("cols", cols[:, :])):
                        sp.dma_start(dst, dram[name]).then_inc(loaded, 16)
                    load_until(sp, MIX_UNITS)

                @block.scalar
                def _(act):
                    act.wait_ge(loaded, 48)
                    for i in range(NT):
                        act.activation(sq[:, i, :], x_row[:, i, :], ACT.Square,
                                       accum_out=stat[:, i:i + 1]).then_inc(ssum.sem, 1)
                    act.wait_ge(*meansq.n(1))
                    act.activation(stat[:, 2:4], stat[:, 2:4], ACT.Sqrt).then_inc(rooted.sem, 1)
                    act.activation(cond[:, :], col("c_2", 0, DC), ACT.Sigmoid).then_inc(cond_in.sem, 1)
                    act.wait_ge(*proj_out.n(10))
                    act.activation(projT[:, 16:20, :], projT[:, 16:20, :], ACT.Sigmoid).then_inc(sig.sem, 1)
                    for k in range(ADA_UNITS):
                        ada_stage(act, 10 + k, 1 + k % 2, k % 2)
                    ada_copy(act, 0, 3)
                    act.wait_ge(*meansq.n(2))
                    act.activation(tmp[:, 0:S], tmp[:, 0:S], ACT.Sqrt).then_inc(rooted.sem, 1)
                    act.wait_ge(*sig_in.n(1))
                    act.activation(projT[:, 0:AC, :], yT[:, AC:2 * AC, :], ACT.Sigmoid).then_inc(sig.sem, 1)
                    act.wait_ge(*meansq.n(3))
                    act.activation(sq[:, :, :], sq[:, :, :], ACT.Sqrt).then_inc(rooted.sem, 1)

                @block.tensor
                def _(pe):
                    pe_transpose(pe, n_row, normed.n(NT), turned)
                    pe.wait_ge(*hT_done.n(4))
                    for u in range(10):
                        w = unit(pe, u).rearrange("p (c n) -> p c n", c=DC)
                        if u >= 4:
                            pe.wait_ge(*proj_out.n(u - 3))
                        for j in range(2):
                            for c in range(DC):
                                ins = pe.matmul(psum[:, 4 + u % 4, j * S:(j + 1) * S], w[:, c, j * P:(j + 1) * P],
                                                hT[:, c, :], start=(c == 0), stop=(c == DC - 1))
                            if j == 1:
                                ins.then_inc(w_used, 1)
                    pe.wait_ge(*cond_in.n(2))
                    for k in range(ADA_UNITS):
                        ada_products(pe, 10 + k, 1 + k % 2)
                        if k > 0:
                            ada_columns(pe, k - 1, 3, (k - 1) % 2)
                    ada_columns(pe, ADA_UNITS - 1, 3, (ADA_UNITS - 1) % 2)
                    pe.wait_ge(*stat_in.n(1))
                    for c in range(AC):
                        ins = pe.matmul(psum[:, 0, 0:S], C["ones"], ub[:, c, 0:S], start=(c == 0), stop=(c == AC - 1))
                    ins.then_inc(stat_out.sem, 1)
                    pe.wait_ge(*stat_in.n(2))
                    for c in range(AC):
                        ins = pe.matmul(psum[:, 1, 0:S], C["ones"], t3[:, c, :], start=(c == 0), stop=(c == AC - 1))
                    ins.then_inc(stat_out.sem, 1)
                    pe.wait_ge(*stat_in.n(3))
                    pe.wait_ge(*mod_copied.n(1))
                    for b in range(4):
                        ins = pe.matmul(psum[:, b, :], C["heads64"], sq[:, b // 2, (b % 2) * 512:(b % 2) * 512 + 512],
                                        start=True, stop=True)
                    ins.then_inc(stat_out.sem, 1)
                    for k in range(4):
                        pe.wait_ge(*y_ready.n(k + 1))
                        w = unit(pe, 10 + ADA_UNITS + k).rearrange("p (c n) -> p c n", c=2)
                        for cc in range(2):
                            for i in range(NT):
                                for h in range(2):
                                    ins = pe.matmul(psum[:, 4 + 2 * i + h, :], yT[:, 2 * k + cc, i * P:(i + 1) * P],
                                                    w[:, cc, h * 512:(h + 1) * 512],
                                                    start=(k == 0 and cc == 0), stop=(k == 3 and cc == 1))
                        ins.then_inc(w_used, 1)

                @block.gpsimd
                def _(pool):
                    pool.memset(ua[:, :, :], 0.0)
                    pool.memset(ub[:, :, :], 0.0).then_inc(signal("pads_zero").sem, 1)

                @block.vector
                def _(dve):
                    link = lambda ins: dve_chain.link(dve, ins)
                    dve.wait_ge(*ssum.n(NT))
                    dve.tensor_scalar(stat[:, 2:4], stat[:, 0:2], 1.0 / D, 1e-6, ALU.mult, ALU.add).then_inc(meansq.sem, 1)
                    dve.wait_ge(*rooted.n(1))
                    link(dve.reciprocal(stat[:, 4:6], stat[:, 2:4]))
                    for i in range(NT):
                        dve.tensor_scalar(n_row[:, i, :], x_row[:, i, :], stat[:, 4 + i:5 + i], None,
                                          ALU.mult).then_inc(normed.sem, 1)
                    dve.wait_ge(*cond_in.n(1))
                    dve.tensor_tensor(cond[:, :], cond[:, :], col("c_2", 0, DC), ALU.mult).then_inc(cond_in.sem, 1)
                    for b in range(4):
                        dve.wait_ge(*turned.n(b + 1))
                        dve.tensor_scalar(hT[:, 2 * b, :], psum[:, b, 0:S], col("norm_mix_g", 2 * b), None, ALU.mult)
                        dve.tensor_scalar(hT[:, 2 * b + 1, :], psum[:, b, S:2 * S], col("norm_mix_g", 2 * b + 1), None,
                                          ALU.mult).then_inc(hT_done.sem, 1)
                    for u in range(10):
                        dve.wait_ge(w_used, u + 1)
                        dve.tensor_copy(projT[:, 2 * u:2 * u + 2, :],
                                        psum[:, 4 + u % 4, :].rearrange("p (j s) -> p j s", j=2)).then_inc(proj_out.sem, 1)
                    dve.wait_ge(*proj_out.n(10))
                    dve.wait_ge(*signal("pads_zero").n(1))
                    link(dve.tensor_tensor(ua[:, :, PA:PA + S], projT[:, 8:12, :], projT[:, 0:4, :], ALU.mult))
                    for c in range(AC):
                        ins = dve.tensor_scalar(yT[:, c, :], ua[:, c, 0:S], col("conv_a_w", c), None, ALU.mult)
                    link(ins)
                    for j in range(1, TAPS_A):
                        for c in range(AC):
                            ins = dve.scalar_tensor_tensor(out=yT[:, c, :], in0=ua[:, c, j:j + S],
                                                           scalar=col("conv_a_w", j * AC + c), in1=yT[:, c, :],
                                                           op0=ALU.mult, op1=ALU.add)
                        link(ins)
                    link(dve.tensor_tensor(yT[:, 0:AC, :], yT[:, 0:AC, :], projT[:, 4:8, :], ALU.mult))
                    dve.wait_ge(*sig.n(1))
                    link(dve.tensor_tensor(ub[:, :, PB:PB + S], projT[:, 12:16, :], projT[:, 16:20, :], ALU.mult))
                    for c in range(AC):
                        ins = dve.tensor_scalar(yT[:, AC + c, :], ub[:, c, 0:S], col("conv_b_w", c), col("conv_b_bias", c),
                                                ALU.mult, ALU.add)
                    tap = signal("tap")
                    ins.then_inc(tap.sem, 1)
                    with dve.Fori(1, TAPS_B) as j:
                        dve.wait_ge(tap.sem, tap.base + j)
                        for c in range(AC):
                            ins = dve.scalar_tensor_tensor(
                                out=yT[:, AC + c, :], in0=ub[:, c, bass.ds(j, S)],
                                scalar=cols[:, bass.ds(j * AC + (COLS["conv_b_w"] + c), 1)],
                                in1=yT[:, AC + c, :], op0=ALU.mult, op1=ALU.add)
                        ins.then_inc(tap.sem, 1)
                    dve.wait_ge(*tap.n(TAPS_B))
                    yb = yT[:, AC:2 * AC, :]
                    dve.tensor_copy(ub[:, :, 0:S], yb).then_inc(stat_in.sem, 1)
                    dve.wait_ge(*stat_out.n(1))
                    link(dve.tensor_scalar(stat_mean, psum[:, 0, 0:S], 1.0 / DA, None, ALU.mult))
                    mean4 = stat_mean.unsqueeze(1).broadcast_to((P, AC, S))
                    link(dve.tensor_tensor(yb, yb, mean4, ALU.subtract))
                    dve.tensor_tensor(t3, yb, yb, ALU.mult).then_inc(stat_in.sem, 1)
                    dve.wait_ge(*stat_out.n(2))
                    dve.tensor_scalar(tmp[:, 0:S], psum[:, 1, 0:S], 1.0 / DA, 1e-6, ALU.mult, ALU.add).then_inc(meansq.sem, 1)
                    dve.wait_ge(*rooted.n(2))
                    link(dve.reciprocal(stat_mean, tmp[:, 0:S]))
                    link(dve.tensor_tensor(yb, yb, mean4, ALU.mult))
                    for c in range(AC):
                        ins = dve.tensor_scalar(yT[:, AC + c, :], yT[:, AC + c, :], col("ln_b_g", c), col("ln_b_b", c),
                                                ALU.mult, ALU.add)
                    ins.then_inc(sig_in.sem, 1)
                    dve.wait_ge(*sig_in.n(1))
                    dve.wait_ge(*sig.n(2))
                    link(dve.tensor_tensor(yb, yb, projT[:, 0:AC, :], ALU.mult))
                    sq8 = sq[:, :, :].rearrange("p b (c s) -> p (b c) s", c=AC)
                    dve.tensor_tensor(sq8, y3, y3, ALU.mult).then_inc(stat_in.sem, 1)
                    dve.wait_ge(*stat_out.n(3))
                    dve.tensor_scalar(sq[:, :, :].rearrange("p b (c s) -> p (b c) s", c=2), psum[:, 0:4, :],
                                      1.0 / 64, 1e-6, ALU.mult, ALU.add).then_inc(meansq.sem, 1)
                    dve.wait_ge(*rooted.n(3))
                    for k in range(AC):
                        link(dve.reciprocal(sq8[:, 2 * k:2 * k + 2, :], sq8[:, 2 * k:2 * k + 2, :]))
                        for c in (2 * k, 2 * k + 1):
                            ins = dve.scalar_tensor_tensor(out=yT[:, c, :], in0=yT[:, c, :],
                                                           scalar=col("beta_a" if c < AC else "beta_b", c % AC),
                                                           in1=sq8[:, c, :], op0=ALU.mult, op1=ALU.mult)
                        ins.then_inc(y_ready.sem, 1)
                    dve.wait_ge(w_used, MIX_UNITS)
                    for i in range(NT):
                        dve.tensor_tensor(x_row[:, i, :].rearrange("p (h n) -> p h n", h=2), psum[:, 4 + 2 * i:6 + 2 * i, :],
                                          x_row[:, i, :].rearrange("p (h n) -> p h n", h=2), ALU.add)
                    finish_modulation(dve, 0)
            advance(ada_staged=ADA_UNITS, ada_done=1, mod_copied=1, squares_summed=NT, mean_squares=3, rooted=3,
                    rows_normed=NT, turned=4, hT_done=4)
            ph.close()

        mean_buf = sb("mean_buf", [P, S])
        gate_row = sb("gate_row", [P, D])
        cond = sb("cond", [P, DC])
        ada_part = sb("ada_part", [P, 2, SIDE])
        stat_mean = mean_buf[:, :]
        mixer()
        if stop_after <= 1:
            return

        SLOTS = 64
        PAIRS = E // 2
        shared = ExitStack()
        combine = sb("combine", [P, NT, E], where=shared)
        rank = sb("rank", [P, NT, E], where=shared)
        overflow = sb("overflow", [P, 1], U32, where=shared)
        iota = sb("iota", [P, P], where=shared)
        gfin = sb("gfin", [P, D], where=shared)

        def moe():
            ph = ExitStack()
            pick = sb("moe_pick", [P, NT, E, SLOTS], where=ph)
            pickw = sb("moe_pickw", [P, E, SLOTS], where=ph)
            pickT = sb("moe_pickT", [P, PAIRS, NT, P], where=ph)
            pair_w = sb("moe_pair_w", [P, 2, NT, P], where=ph)
            hidden = sb("moe_hidden", [P, 512], where=ph)
            actT = sb("moe_actT", [P, 4, P], where=ph)
            sg = sb("moe_sg", [P, 512], where=ph)
            y_sb = sb("moe_y", [P, 2, D], where=ph)
            wr = sb("moe_wr", [P, DC, GROUPS + E], where=ph)
            br = sb("moe_br", [P, GROUPS + E], where=ph)
            lg = sb("moe_lg", [P, NT, GROUPS + E], where=ph)
            chosen = sb("moe_chosen", [P, NT, E], where=ph)
            pg = sb("moe_pg", [P, NT, 8], where=ph)
            le = sb("moe_le", [P, NT, 8], where=ph)
            top = sb("moe_top", [P, NT, 2, 8], where=ph)
            topi = sb("moe_topi", [P, NT, 2, 8], U32, where=ph)
            idf = sb("moe_idf", [P, NT, 2, 8], where=ph)
            oh = sb("moe_oh", [P, NT, 4, 8], where=ph)
            sm = sb("moe_sm", [P, NT, 16], where=ph)
            gffn = sb("moe_gffn", [P, D], where=ph)
            ssum, meansq, rooted, normed = (signal(n) for n in ("squares_summed", "mean_squares", "rooted", "rows_normed"))
            turned, hT_done = signal("turned"), signal("hT_done")
            small, logits = signal("layer_small"), signal("logits")
            rt_in, rt_out = signal("route_exp_in"), signal("route_exp")
            (chose, ranked, picked, pick_turned, pick_copied, filled, copied, sigm, gated, acted, act_turned, act_copied,
             y_copied, pair_ready, scattered) = (signal(n) for n in (
                 "chosen", "ranked", "picked", "pick_turned", "pick_copied", "rows_picked", "rows_copied", "sigmoid_done",
                 "gated", "act_done", "act_turned", "act_copied", "y_copied", "pair_weights", "scattered"))
            OUT, YB, U1, U3 = 0, 4, 6, 7
            u0 = moe_at
            turns = PAIRS // TURN

            def up_done(p):
                return w_used, p * PAIR_UNITS + (u0 + 8)

            def down_done(p):
                return w_used, p * PAIR_UNITS + (u0 + 12)

            with nc.Block() as block:
                @block.sync
                def _(sp):
                    for dst, src in ((gffn[:, :], dram["norm_ffn_g"]), (wr[:, :, :], dram["w_route"]),
                                     (br[:, :], dram["b_route"]), (iota[:, :], dram["iota"]),
                                     (gfin[:, :], dram["norm_final_g"])):
                        sp.dma_start(dst, src).then_inc(small.sem, 16)
                    load_until(sp, u0 + TURN * PAIR_UNITS - RING)
                    with sp.Fori(1, turns - 1) as t:
                        u = u0
                        for k in range(TURN):
                            for w, e, half in moe_units(t * TURN + k):
                                sp.wait_ge(w_used, t * (TURN * PAIR_UNITS) + (u - RING + 1))
                                sp.dma_start(ring[:, u % RING, :], dram[w][e, half]).then_inc(w_land[u % RING], 16)
                                u += 1
                    issued[0] = u0 + TURN * PAIR_UNITS * (turns - 1)
                    load_until(sp, u0 + MOE_UNITS)

                @block.gpsimd
                def _(pool):
                    def pair(p, par):
                        if not isinstance(p, int) or p >= 2:
                            pool.wait_ge(*scattered.n(p - 1))
                        src = pickT[:, p, :, :] if isinstance(p, int) else pickT[:, bass.ds(p, 1), :, :].squeeze(1)
                        pool.tensor_copy(pair_w[:, par, :, :], src).then_inc(pair_ready.sem, 1)

                    pool.wait_ge(*pick_copied.n(8))
                    pair(0, 0)
                    pair(1, 1)
                    with pool.Fori(1, PAIRS // 2) as i:
                        for par in range(2):
                            pair(i * 2 + par, par)

                @block.scalar
                def _(act):
                    for i in range(NT):
                        act.activation(pickw[:, 0:16, :].rearrange("p e s -> p (e s)"), x_row[:, i, :], ACT.Square,
                                       accum_out=stat[:, i:i + 1]).then_inc(ssum.sem, 1)
                        act.wait_ge(*ssum.n(i + 1))
                    act.wait_ge(*meansq.n(1))
                    act.activation(stat[:, 2:4], stat[:, 2:4], ACT.Sqrt).then_inc(rooted.sem, 1)
                    turn_copies(act)
                    for k in range(2):
                        act.wait_ge(*rt_in.n(k + 1))
                        for i in range(NT):
                            v = pg[:, i, 0:GROUPS] if k == 0 else le[:, i, :]
                            act.activation(v, v, ACT.Exp, accum_out=sm[:, i, k:k + 1]).then_inc(rt_out.sem, 1)

                    def copy_weights():
                        for b in range(8):
                            act.wait_ge(*pick_turned.n(b + 1))
                            i, p = b // 4, 4 * (b % 4)
                            act.activation(pickT[:, p:p + 4, i, :], psum[:, b % 4, :].rearrange("p (a t) -> p a t", a=4),
                                           ACT.Copy).then_inc(pick_copied.sem, 1)

                    def copy_rows(p, half):
                        act.wait_ge(*filled.n(p * 2 + (half + 1)))
                        act.activation(hT[:, 4 * half:4 * half + 4, 0:P],
                                       psum[:, (U3, U1)[half], :].rearrange("p (c s) -> p c s", c=4),
                                       ACT.Copy).then_inc(copied.sem, 1)

                    def pair(p, par, first=False, last=False):
                        act.wait_ge(*up_done(p))
                        if not first:
                            act.wait_ge(*acted.n(p))
                        act.activation(sg[:, :], psum[:, U1, :], ACT.Sigmoid).then_inc(sigm.sem, 1)
                        if first:
                            copy_weights()
                        act.wait_ge(*act_turned.n(p + 1))
                        act.activation(actT[:, :, :], psum[:, U1, :].rearrange("p (j s) -> p j s", j=4),
                                       ACT.Copy).then_inc(act_copied.sem, 1)
                        if not last:
                            for half in range(2):
                                copy_rows(p + 1, half)
                        act.wait_ge(*down_done(p))
                        if not isinstance(p, int) or p >= 2:
                            act.wait_ge(*scattered.n(p - 1))
                        act.activation(y_sb[:, par, :].rearrange("p (h n) -> p h n", h=2), psum[:, YB:YB + 2, :],
                                       ACT.Copy).then_inc(y_copied.sem, 1)

                    act.wait_ge(*ranked.n(3))
                    for half in range(2):
                        copy_rows(0, half)
                    pair(0, 0, first=True)
                    pair(1, 1)
                    with act.Fori(1, turns - 1) as t:
                        for k in range(TURN):
                            pair(t * TURN + k, k)
                    pair(PAIRS - 2, 0)
                    pair(PAIRS - 1, 1, last=True)

                @block.tensor
                def _(pe):
                    pe_transpose(pe, n_row, normed.n(NT), turned)
                    pe.wait_ge(*small.n(80))
                    pe.wait_ge(*hT_done.n(4))
                    for i in range(NT):
                        for c in range(DC):
                            ins = pe.matmul(psum[:, 4 + i, 0:GROUPS + E], hT[:, c, i * P:(i + 1) * P], wr[:, c, :],
                                            start=(c == 0), stop=(c == DC - 1))
                        ins.then_inc(logits.sem, 1)
                    pe.wait_ge(*chose.n(1))
                    less, minus = C["neg00"], C["neg01"]
                    pe.matmul(psum[:, 6, 0:E], less, chosen[:, 0, :], start=True, stop=True).then_inc(ranked.sem, 1)
                    pe.matmul(psum[:, 6, E:2 * E], less, chosen[:, 1, :], start=True, stop=False)
                    pe.matmul(psum[:, 6, E:2 * E], minus, chosen[:, 0, :], start=False, stop=True).then_inc(ranked.sem, 1)
                    pe.matmul(psum[:, 6, 2 * E:3 * E], minus, chosen[:, 0, :], start=True, stop=False)
                    pe.matmul(psum[:, 6, 2 * E:3 * E], minus, chosen[:, 1, :], start=False, stop=True).then_inc(ranked.sem, 1)

                    def turn_weights():
                        for i in range(NT):
                            pe.wait_ge(*picked.n(NT + i + 1))
                            for b in range(4):
                                if i > 0:
                                    pe.wait_ge(*pick_copied.n(b + 1))
                                for k in range(4):
                                    e = 2 * (4 * b + k)
                                    ins = pe.transpose(psum[:, b, k * P:(k + 1) * P],
                                                       pickw[:, e:e + 2, :].rearrange("p e s -> p (e s)"), ident)
                                ins.then_inc(pick_turned.sem, 1)

                    def fill(p, half):
                        for c in range(4):
                            for i in range(NT):
                                v = pick[:, i, :, :].rearrange("p e s -> p (e s)")
                                v = v[:, p * P:(p + 1) * P] if isinstance(p, int) else v[:, bass.ds(p * P, P)]
                                at = (4 * half + c) * P
                                ins = pe.matmul(psum[:, (U3, U1)[half], c * P:(c + 1) * P], n_row[:, i, at:at + P], v,
                                                start=(i == 0), stop=(i == NT - 1))
                        ins.then_inc(filled.sem, 1)

                    def landed_at(k, p, par):
                        if isinstance(p, int):
                            return unit(pe, u0 + PAIR_UNITS * p + k)
                        v = u0 + PAIR_UNITS * par + k
                        pe.wait_ge(w_land[v % RING], p * (16 * PAIR_UNITS // RING)
                                   + (16 * (v // RING + 1) - 16 * PAIR_UNITS * par // RING))
                        return ring[:, v % RING, :]

                    def side_by_side(p, par, k, chunks, product):
                        wt = [landed_at(k + j, p, par).rearrange("p (c n) -> p c n", c=chunks) for j in range(2)]
                        for c in range(chunks):
                            ins = [product(j, wt[j], c) for j in range(2)]
                        for j in range(2):
                            ins[j].then_inc(w_used, 1)

                    def scatter(p, par, first=False, last=False):
                        pe.wait_ge(*y_copied.n(p + 1))
                        pe.wait_ge(*pair_ready.n(p + 1))
                        for i in range(NT):
                            for h in range(2):
                                ins = pe.matmul(psum[:, OUT + 2 * i + h, :], pair_w[:, par, i, :],
                                                y_sb[:, par, h * 512:(h + 1) * 512], start=first, stop=last)
                        ins.then_inc(scattered.sem, 1)

                    def pair(p, par, before=None, last=False):
                        rows = lambda j: slice(j * SLOTS, (j + 1) * SLOTS)
                        pe.wait_ge(*copied.n(p * 2 + 2))
                        for w, bank in enumerate((U1, U3)):
                            for half in range(2):
                                side_by_side(p, par, 4 * w + 2 * half, 4, lambda j, wt, c: pe.matmul(
                                    psum[rows(j), bank, :], hT[:, 4 * half + c, rows(j)], wt[:, c, :],
                                    start=(half == 0 and c == 0), stop=(half == 1 and c == 3)))
                        if before is not None:
                            before()
                        pe.wait_ge(*acted.n(p + 1))
                        for j in range(4):
                            ins = pe.transpose(psum[:, U1, j * P:(j + 1) * P], hidden[:, j * P:(j + 1) * P], ident)
                        ins.then_inc(act_turned.sem, 1)
                        if not last:
                            fill(p + 1, 0)
                        pe.wait_ge(*act_copied.n(p + 1))
                        if not last:
                            fill(p + 1, 1)
                        for half in range(2):
                            def down(j, wt, c):
                                for h in range(2):
                                    ins = pe.matmul(psum[rows(j), YB + h, :], actT[:, 2 * half + c, rows(j)],
                                                    wt[:, c, h * 512:(h + 1) * 512],
                                                    start=(half == 0 and c == 0), stop=(half == 1 and c == 1))
                                return ins
                            side_by_side(p, par, 8 + 2 * half, 2, down)

                    pe.wait_ge(*picked.n(NT))
                    for half in range(2):
                        fill(0, half)
                    pair(0, 0, turn_weights)
                    pair(1, 1, lambda: scatter(0, 0, first=True))
                    with pe.Fori(1, turns - 1) as t:
                        for k in range(TURN):
                            pair(t * TURN + k, k, lambda: scatter(t * TURN + (k - 1), 1 - k))
                    for p in (PAIRS - 2, PAIRS - 1):
                        pair(p, p % 2, lambda: scatter(p - 1, (p - 1) % 2), last=(p == PAIRS - 1))
                    scatter(PAIRS - 1, 1, last=True)

                @block.vector
                def _(dve):
                    link = lambda ins: dve_chain.link(dve, ins)
                    dve.wait_ge(*ssum.n(NT))
                    dve.tensor_scalar(stat[:, 2:4], stat[:, 0:2], 1.0 / D, 1e-6, ALU.mult, ALU.add).then_inc(meansq.sem, 1)
                    dve.wait_ge(*rooted.n(1))
                    link(dve.reciprocal(stat[:, 4:6], stat[:, 2:4]))
                    dve.wait_ge(*small.n(80))
                    for i in range(NT):
                        dve.scalar_tensor_tensor(out=n_row[:, i, :], in0=x_row[:, i, :], scalar=stat[:, 4 + i:5 + i],
                                                 in1=gffn[:, :], op0=ALU.mult, op1=ALU.mult).then_inc(normed.sem, 1)
                    dve.wait_ge(*normed.n(NT))

                    def each(step):
                        for i in range(NT):
                            ins = step(i)
                        link(ins)

                    link(dve.memset(pg[:, :, :], -1.0))
                    dve.wait_ge(*logits.n(NT))
                    each(lambda i: dve.tensor_tensor(lg[:, i, :], psum[:, 4 + i, 0:GROUPS + E], br[:, :], ALU.add))
                    each(lambda i: dve.tensor_reduce(sm[:, i, 2:3], lg[:, i, 0:GROUPS], AX.X, ALU.max))
                    for i in range(NT):
                        ins = dve.tensor_scalar(pg[:, i, 0:GROUPS], lg[:, i, 0:GROUPS], sm[:, i, 2:3], None, ALU.subtract)
                    ins.then_inc(rt_in.sem, 1)
                    dve.wait_ge(*rt_out.n(NT))
                    each(lambda i: dve.reciprocal(sm[:, i, 3:4], sm[:, i, 0:1]))
                    each(lambda i: dve.tensor_scalar(pg[:, i, 0:GROUPS], pg[:, i, 0:GROUPS], sm[:, i, 3:4], None, ALU.mult))
                    each(lambda i: dve.max(top[:, i, 0, :], pg[:, i, :]))
                    each(lambda i: dve.max_index(topi[:, i, 0, :], top[:, i, 0, :], pg[:, i, :]))
                    each(lambda i: dve.tensor_copy(idf[:, i, 0, :], topi[:, i, 0, :]))
                    each(lambda i: dve.tensor_scalar(oh[:, i, 0, :], iota[:, 0:8], idf[:, i, 0, 0:1], None, ALU.is_equal))
                    each(lambda i: dve.tensor_scalar(le[:, i, :], lg[:, i, GROUPS:GROUPS + 8], oh[:, i, 0, 0:1], None, ALU.mult))
                    for g in range(1, GROUPS):
                        each(lambda i: dve.scalar_tensor_tensor(
                            out=le[:, i, :], in0=lg[:, i, GROUPS + 8 * g:GROUPS + 8 * g + 8],
                            scalar=oh[:, i, 0, g:g + 1], in1=le[:, i, :], op0=ALU.mult, op1=ALU.add))
                    each(lambda i: dve.tensor_reduce(sm[:, i, 4:5], le[:, i, :], AX.X, ALU.max))
                    for i in range(NT):
                        ins = dve.tensor_scalar(le[:, i, :], le[:, i, :], sm[:, i, 4:5], None, ALU.subtract)
                    ins.then_inc(rt_in.sem, 1)
                    dve.wait_ge(*rt_out.n(2 * NT))
                    each(lambda i: dve.reciprocal(sm[:, i, 5:6], sm[:, i, 1:2]))
                    each(lambda i: dve.tensor_scalar(le[:, i, :], le[:, i, :], sm[:, i, 5:6], None, ALU.mult))
                    each(lambda i: dve.max(top[:, i, 1, :], le[:, i, :]))
                    each(lambda i: dve.max_index(topi[:, i, 1, :], top[:, i, 1, :], le[:, i, :]))
                    each(lambda i: dve.tensor_copy(idf[:, i, 1, :], topi[:, i, 1, :]))
                    each(lambda i: dve.tensor_tensor(sm[:, i, 6:7], top[:, i, 1, 0:1], top[:, i, 1, 1:2], ALU.add))
                    each(lambda i: dve.reciprocal(sm[:, i, 7:8], sm[:, i, 6:7]))
                    each(lambda i: dve.tensor_tensor(sm[:, i, 8:9], sm[:, i, 7:8], top[:, i, 0, 0:1], ALU.mult))
                    each(lambda i: dve.tensor_scalar(sm[:, i, 9:11], top[:, i, 1, 0:2], sm[:, i, 8:9], None, ALU.mult))
                    for k in range(2):
                        each(lambda i: dve.tensor_scalar(oh[:, i, 1 + k, :], iota[:, 0:8], idf[:, i, 1, k:k + 1], None,
                                                         ALU.is_equal))
                    each(lambda i: dve.tensor_tensor(oh[:, i, 3, :], oh[:, i, 1, :], oh[:, i, 2, :], ALU.add))
                    each(lambda i: dve.tensor_scalar(oh[:, i, 1, :], oh[:, i, 1, :], sm[:, i, 9:10], None, ALU.mult))
                    each(lambda i: dve.scalar_tensor_tensor(out=oh[:, i, 1, :], in0=oh[:, i, 2, :], scalar=sm[:, i, 10:11],
                                                            in1=oh[:, i, 1, :], op0=ALU.mult, op1=ALU.add))
                    for g in range(GROUPS):
                        for i in range(NT):
                            for dst, src in ((combine, 1), (chosen, 3)):
                                ins = dve.tensor_scalar(dst[:, i, 8 * g:8 * g + 8], oh[:, i, src, :], oh[:, i, 0, g:g + 1],
                                                        None, ALU.mult)
                    ins.then_inc(chose.sem, 1)
                    dve.wait_ge(*chose.n(1))

                    dve.wait_ge(*ranked.n(3))
                    flat = lambda a: a.rearrange("p i e -> p (i e)")
                    dve.tensor_reduce(sm[:, 0, 11:12], psum[:, 6, 2 * E:3 * E], AX.X, ALU.min)
                    link(dve.tensor_scalar(flat(rank[:, :, :]), psum[:, 6, 0:2 * E], -1.0, 1.0, ALU.mult, ALU.add))
                    dve.tensor_scalar(overflow[:, :], sm[:, 0, 11:12], -float(SLOTS), None, ALU.is_lt)
                    link(dve.tensor_tensor(rank[:, :, :], rank[:, :, :], chosen[:, :, :], ALU.mult))
                    link(dve.tensor_scalar(rank[:, :, :], rank[:, :, :], -1.0, None, ALU.add))
                    shape = (P, E, SLOTS)
                    for i in range(NT):
                        dve.tensor_tensor(pick[:, i, :, :], iota[:, 0:SLOTS].unsqueeze(1).broadcast_to(shape),
                                          rank[:, i, :].unsqueeze(2).broadcast_to(shape), ALU.is_equal).then_inc(picked.sem, 1)
                    dve.wait_ge(*picked.n(NT))
                    for i in range(NT):
                        if i > 0:
                            dve.wait_ge(*pick_turned.n(4))
                        dve.tensor_tensor(pickw[:, :, :], pick[:, i, :, :], combine[:, i, :].unsqueeze(2).broadcast_to(shape),
                                          ALU.mult).then_inc(picked.sem, 1)

                    with dve.Fori(0, PAIRS) as p:
                        dve.wait_ge(*sigm.n(p + 1))
                        dve.tensor_tensor(sg[:, :], sg[:, :], psum[:, U1, :], ALU.mult).then_inc(gated.sem, 1)
                        dve.wait_ge(*gated.n(p + 1))
                        dve.tensor_tensor(hidden[:, :], sg[:, :], psum[:, U3, :], ALU.mult).then_inc(acted.sem, 1)
                    dve.wait_ge(*scattered.n(PAIRS))
                    for i in range(NT):
                        xr = x_row[:, i, :].rearrange("p (h n) -> p h n", h=2)
                        dve.tensor_tensor(xr, psum[:, OUT + 2 * i:OUT + 2 * i + 2, :], xr, ALU.add)
            advance(squares_summed=NT, mean_squares=1, rooted=1, rows_normed=NT, turned=4, hT_done=4, layer_small=80)
            ph.close()

        def moe_rest():
            ph = ExitStack()
            sel = sb("rest_sel", [P, NT, 2, P], where=ph)
            selT = sb("rest_selT", [P, NT, P], where=ph)
            rows = sb("rest_rows", [P, DC, P], where=ph)
            wbuf = sb("rest_w", [P, UNIT], where=ph)
            sg = sb("rest_sg", [P, 512], where=ph)
            hidden = sb("rest_hidden", [P, 512], where=ph)
            actT = sb("rest_actT", [P, 4, P], where=ph)
            y_sb = sb("rest_y", [P, D], where=ph)
            junk = sb("rest_junk", [P, D], where=ph)
            ssum, meansq, rooted = (signal(n) for n in ("squares_summed", "mean_squares", "rooted"))
            (selected, r_picked, r_copied, land, used, r_sig, gated, r_act, r_turned, r_act_copied, r_y, r_sum) = (
                signal(n) for n in ("rest_selected", "rest_picked", "rest_copied", "rest_landed", "rest_used",
                                    "rest_sigmoid", "rest_gated", "rest_act", "rest_turned", "rest_act_copied",
                                    "rest_y_copied", "rest_sum"))
            ROUNDS = -(-(S - SLOTS) // P)
            SUM, YB, U1, U3 = 0, 4, 6, 7

            def for_each_expert(eng, step, before=None):
                flag = eng.value_load(overflow[0:1, 0:1], min_val=0, max_val=1)
                with eng.If(flag):
                    with eng.Fori(0, ROUNDS) as c:
                        if before is not None:
                            before(c)
                        with eng.Fori(0, E) as e:
                            step(e, c * E + e)

            with nc.Block() as block:
                @block.sync
                def _(sp):
                    def step(e, x):
                        units = [dram[w][e, half] for w in ("w1", "w3", "w2") for half in range(2)]
                        for k, src in enumerate(units):
                            sp.wait_ge(*used.n(x * 6 + k))
                            sp.dma_start(wbuf[:, :], src).then_inc(land.sem, 16)
                    for_each_expert(sp, step)

                @block.scalar
                def _(act):
                    def step(e, x):
                        act.wait_ge(*used.n(x * 6 + 4))
                        act.activation(sg[:, :], psum[:, U1, :], ACT.Sigmoid).then_inc(r_sig.sem, 1)
                    for_each_expert(act, step)
                    act.wait_ge(*signal("moe_summed").n(1))
                    for i in range(NT):
                        act.activation(junk[:, :], x_row[:, i, :], ACT.Square,
                                       accum_out=stat[:, i:i + 1]).then_inc(ssum.sem, 1)
                        act.wait_ge(*ssum.n(i + 1))
                    act.wait_ge(*meansq.n(1))
                    act.activation(stat[:, 2:4], stat[:, 2:4], ACT.Sqrt).then_inc(rooted.sem, 1)

                @block.tensor
                def _(pe):
                    def step(e, x):
                        pe.wait_ge(*selected.n(x + 1))
                        for c in range(DC):
                            for i in range(NT):
                                ins = pe.matmul(psum[:, YB + c // 4, c % 4 * P:(c % 4 + 1) * P],
                                                n_row[:, i, c * P:(c + 1) * P], sel[:, i, 0, :],
                                                start=(i == 0), stop=(i == NT - 1))
                        for i in range(NT):
                            ins = pe.transpose(psum[:, U1, i * P:(i + 1) * P], sel[:, i, 1, :], ident)
                        ins.then_inc(r_picked.sem, 1)
                        pe.wait_ge(*r_copied.n(x + 1))
                        for w, bank in enumerate((U1, U3)):
                            for half in range(2):
                                pe.wait_ge(*land.n(x * 96 + 16 * (2 * w + half + 1)))
                                wt = wbuf[:, :].rearrange("p (c n) -> p c n", c=4)
                                for c in range(4):
                                    ins = pe.matmul(psum[:, bank, :], rows[:, 4 * half + c, :], wt[:, c, :],
                                                    start=(half == 0 and c == 0), stop=(half == 1 and c == 3))
                                ins.then_inc(used.sem, 1)
                        pe.wait_ge(*r_act.n(x + 1))
                        for j in range(4):
                            ins = pe.transpose(psum[:, U1, j * P:(j + 1) * P], hidden[:, j * P:(j + 1) * P], ident)
                        ins.then_inc(r_turned.sem, 1)
                        pe.wait_ge(*r_act_copied.n(x + 1))
                        for half in range(2):
                            pe.wait_ge(*land.n(x * 96 + 16 * (half + 5)))
                            wt = wbuf[:, :].rearrange("p (c n) -> p c n", c=2)
                            for cc in range(2):
                                for h in range(2):
                                    j = 2 * half + cc
                                    ins = pe.matmul(psum[:, YB + h, :], actT[:, j, :], wt[:, cc, h * 512:(h + 1) * 512],
                                                    start=(j == 0), stop=(j == 3))
                            ins.then_inc(used.sem, 1)
                        pe.wait_ge(*r_y.n(x + 1))
                        for i in range(NT):
                            for h in range(2):
                                ins = pe.matmul(psum[:, SUM + 2 * i + h, :], selT[:, i, :], y_sb[:, h * 512:(h + 1) * 512],
                                                start=True, stop=True)
                        ins.then_inc(r_sum.sem, 1)
                    for_each_expert(pe, step)
                    pe.wait_ge(*signal("moe_summed").n(1))
                    modulation_rows(pe, 0, 0, 0)

                @block.vector
                def _(dve):
                    def before(c):
                        dve.drain()
                        dve.tensor_scalar(rank[:, :, :], rank[:, :, :], -float(P), None, ALU.add)

                    def step(e, x):
                        dve.drain()
                        for i in range(NT):
                            r, w = rank[:, i, bass.ds(e, 1)], combine[:, i, bass.ds(e, 1)]
                            dve.tensor_scalar(sel[:, i, 0, :], iota[:, :], r, None, ALU.is_equal)
                            ins = dve.tensor_scalar(sel[:, i, 1, :], iota[:, :], r, w, ALU.is_equal, ALU.mult)
                        ins.then_inc(selected.sem, 1)
                        dve.wait_ge(*r_picked.n(x + 1))
                        dve.tensor_copy(selT[:, :, :], psum[:, U1, 0:NT * P].rearrange("p (i t) -> p i t", i=NT))
                        dve.tensor_copy(rows[:, :, :].rearrange("p (b c) s -> p b (c s)", b=2),
                                        psum[:, YB:YB + 2, :]).then_inc(r_copied.sem, 1)
                        dve.wait_ge(*r_sig.n(x + 1))
                        dve.tensor_tensor(sg[:, :], sg[:, :], psum[:, U1, :], ALU.mult).then_inc(gated.sem, 1)
                        dve.wait_ge(*gated.n(x + 1))
                        dve.tensor_tensor(hidden[:, :], sg[:, :], psum[:, U3, :], ALU.mult).then_inc(r_act.sem, 1)
                        dve.wait_ge(*r_turned.n(x + 1))
                        dve.tensor_copy(actT[:, :, :],
                                        psum[:, U1, :].rearrange("p (j s) -> p j s", j=4)).then_inc(r_act_copied.sem, 1)
                        dve.wait_ge(*used.n(x * 6 + 6))
                        dve.tensor_copy(y_sb[:, :].rearrange("p (h n) -> p h n", h=2), psum[:, YB:YB + 2, :]).then_inc(r_y.sem, 1)
                        dve.wait_ge(*r_sum.n(x + 1))
                        for i in range(NT):
                            xr = x_row[:, i, :].rearrange("p (h n) -> p h n", h=2)
                            dve.tensor_tensor(xr, psum[:, SUM + 2 * i:SUM + 2 * i + 2, :], xr, ALU.add)

                    dve.drain()
                    dve.tensor_scalar(rank[:, :, :], rank[:, :, :], float(P - SLOTS), None, ALU.add)
                    for_each_expert(dve, step, before)
                    dve.drain()
                    dve.engine_nop().then_inc(signal("moe_summed").sem, 1)
                    dve.wait_ge(*ssum.n(NT))
                    dve.tensor_scalar(stat[:, 2:4], stat[:, 0:2], 1.0 / D, 1e-6, ALU.mult, ALU.add).then_inc(meansq.sem, 1)
                    dve.wait_ge(*rooted.n(1))
                    dve_chain.link(dve, dve.reciprocal(stat[:, 4:6], stat[:, 2:4]))
                    for i in range(NT):
                        dve.scalar_tensor_tensor(out=x_row[:, i, :], in0=x_row[:, i, :], scalar=stat[:, 4 + i:5 + i],
                                                 in1=gfin[:, :], op0=ALU.mult, op1=ALU.mult)
            advance(squares_summed=NT, mean_squares=1, rooted=1)
            ph.close()
            shared.close()

        def turn_copies(act):
            for b in range(4):
                act.wait_ge(*signal("turned").n(b + 1))
                act.activation(hT[:, 2 * b:2 * b + 2, :], psum[:, b, :].rearrange("p (j s) -> p j s", j=2),
                               ACT.Copy).then_inc(signal("hT_done").sem, 1)

        def residual_norm(dve, i, banks, gb, gb_landed, root, more=None):
            link = lambda ins: dve_chain.link(dve, ins)
            halves = lambda a: a.rearrange("p (h n) -> p h n", h=2)
            x, n = x_row[:, i, :], n_row[:, i, :]
            y = psum[:, banks:banks + 2, :]
            if more is not None:
                link(dve.tensor_tensor(halves(n), y, halves(more), ALU.add))
                y = halves(n)
            link(dve.tensor_tensor(halves(n), y, halves(gate_row[:, :]), ALU.mult))
            link(dve.scalar_tensor_tensor(out=x, in0=x, scalar=float(ALPHA), in1=n, op0=ALU.mult, op1=ALU.add))
            for h in range(2):
                ins = dve.bn_stats(stat[:, 16 + 12 * i + 6 * h:22 + 12 * i + 6 * h], x[:, h * 512:(h + 1) * 512])
            link(ins)
            link(dve.bn_aggr(stat[:, 8 + 2 * i:10 + 2 * i], stat[:, 16 + 12 * i:28 + 12 * i]))
            dve.tensor_scalar(stat[:, 2 + i:3 + i], stat[:, 9 + 2 * i:10 + 2 * i], 1e-5, None,
                              ALU.add).then_inc(signal("mean_squares").sem, 1)
            dve.wait_ge(*signal("rooted").n(root))
            link(dve.reciprocal(stat[:, 4 + i:5 + i], stat[:, 2 + i:3 + i]))
            link(dve.tensor_scalar(x, x, stat[:, 8 + 2 * i:9 + 2 * i], stat[:, 4 + i:5 + i], ALU.subtract, ALU.mult))
            dve.wait_ge(*gb_landed)
            link(dve.tensor_tensor(x, x, gb[:, 0, :], ALU.mult))
            return dve.tensor_tensor(x, x, gb[:, 1, :], ALU.add)

        def root_of_tile(act, i, root):
            act.wait_ge(*signal("mean_squares").n(root))
            act.activation(stat[:, 2 + i:3 + i], stat[:, 2 + i:3 + i], ACT.Sqrt).then_inc(signal("rooted").sem, 1)

        moe()
        moe_rest()
        if stop_after <= 2:
            return

        def attention(l):
            ph = ExitStack()
            projT = sb(f"att{l}_projT", [P, 20, S], where=ph)
            v_row = sb(f"att{l}_v_row", [P, 2, NT, 512], where=ph)
            hg = sb(f"att{l}_hg", [P, 8, 4 * S], where=ph)
            scT = sb(f"att{l}_scT", [P, 3, HG, P], where=ph)
            oT = sb(f"att{l}_oT", [P, 2, 4, S], where=ph)
            gb = sb(f"att{l}_gb", [P, 2, D], where=ph)
            gates_b = sb(f"att{l}_gates_b", [P, DC, S], where=ph)
            pj, ad = proj_at[l], ada_at[l]
            um = layer_at[l] + len(pj) + len(ad)
            uo = um + 4
            end = uo + 4
            fa, qa, ga, qb, kb = (projT[:, 4 * n:4 * n + 4, :] for n in range(5))
            kT, bufA, bufB = (hg[:, n, :] for n in range(3))
            dec = [hg[:, 1, :], hg[:, 3, :]]
            qd = [hg[:, 4, :], hg[:, 5, :]]
            kd = [hg[:, 6, :], hg[:, 7, :]]
            heads = lambda a: a.rearrange("p (h s) -> p h s", h=HG)
            (turned, hT_done, normed, proj_out, gates_exp, logf_in, logf, d_in, decay, q_dec, k_dec, lvl, lvl_used, meansq,
             rooted, o_done, osq, oss, sg_done, z_done, soft, logs, inc, w_in, w_done, z_abs, z_max, ob_done, ob_out, o_ready,
             merged, lbs) = (signal(n) for n in (
                 "turned", "hT_done", "rows_normed", "att_proj_copied", "forget_exps", "forget_in", "forget_log",
                 "decay_in", "decay", "q_decayed", "k_decayed", "level_products", "level_kept", "mean_squares", "rooted",
                 "hgrn_out", "hgrn_squares", "hgrn_sums", "silu_gate", "stick_z", "stick_soft", "stick_logs", "stick_sums",
                 "stick_w_in", "stick_w", "stick_z_abs", "stick_z_max", "stick_out", "stick_copied", "heads_ready", "merged", "bounds"))
            sa, ls = ([hg[:, lo:lo + 3, :].rearrange("p a n -> p (a n)")[:, p * 768:(p + 1) * 768]
                       .rearrange("p (b n) -> p b n", b=2) for p in range(SB // 2)] for lo in (2, 5))
            FIRST_Z = PROJ_UNITS - SB // 2
            UP_BANKS = (2, 0, 4, 6)
            mT = hg[:, 0:2, :].rearrange("p a (c s) -> p (a c) s", c=4)
            gate_sig = heads(hg[:, 4, :])
            gates_a = n_row[:, :, :].rearrange("p i (c s) -> p (i c) s", s=S)
            gates = [g[:, 4 * q:4 * q + 4, :] for q in range(2) for g in (gates_a, gates_b)]
            mod_copied, first_out = signal("mod_copied"), signal("att_first_out")
            LEVELS = (128, 64, 32, 16, 8, 4, 2, 1, 0)
            FIRST_LEVEL = 6
            OUT_AFTER = FIRST_LEVEL + len(LEVELS)
            SUMS_AFTER = OUT_AFTER + 1
            PROJ_BANKS, ADA_BANK = 3, 7

            with nc.Block() as block:
                @block.sync
                def _(sp):
                    for k, n in enumerate(("ln_g_2", "ln_b_2")):
                        sp.dma_start(gb[:, k, :], dram[n][l, 0]).then_inc(signal("ln_rows").sem, 16)
                    load_until(sp, end)

                @block.gpsimd
                def _(pool):
                    pool.memset(scT[:, :, :, :], 0.0).then_inc(signal("scores_zero").sem, 1)
                    for n in range(8):
                        pool.wait_ge(*decay.n(n + 1))
                        pool.wait_ge(*logf_in.n(2))
                        if n >= 2:
                            pool.wait_ge(*lvl.n(n - 1))
                        pool.tensor_tensor(kd[n % 2], kT, dec[n % 2], ALU.mult).then_inc(k_dec.sem, 1)

                @block.scalar
                def _(act):
                    if l == 0:
                        act.wait_ge(*lbs.n(1))
                        act.activation(lb[:, 2, :], lb[:, 2, :], ACT.Exp).then_inc(lbs.sem, 1)
                    copy_gate_row(act, 4)
                    turn_copies(act)
                    for k in range(PROJ_UNITS):
                        within, behind = ada_slots(l, k)
                        for a in within:
                            ada_stage(act, ad[a], ADA_BANK)
                        act.wait_ge(w_used, pj[k] + 1)
                        bank = psum[:, 4 + k % PROJ_BANKS, :].rearrange("p (j s) -> p j s", j=2)
                        if k >= 14:
                            g = gates_a if k < 18 else gates_b
                            at = 2 * ((k - 14) % 4)
                            act.activation(g[:, at:at + 2, :], bank, ACT.Sigmoid).then_inc(proj_out.sem, 1)
                        elif k in (6, 7, 12, 13):
                            n = 0 if k < 8 else 1
                            at = (k % 2) * S
                            act.activation(v_row[:, n, :, at:at + S], bank, ACT.Copy).then_inc(proj_out.sem, 1)
                        else:
                            at = 2 * (k if k < 6 else k - 2)
                            act.activation(projT[:, at:at + 2, :], bank, ACT.Copy,
                                           scale=0.125 if k in (8, 9) else 1.0).then_inc(proj_out.sem, 1)
                        if k == 1:
                            act.wait_ge(*proj_out.n(2))
                            act.activation(heads(bufA), fa, ACT.Exp, scale=-1.0).then_inc(gates_exp.sem, 1)
                            act.activation(heads(kT), fa, ACT.Exp).then_inc(gates_exp.sem, 1)
                        if k == 3:
                            act.wait_ge(*logf_in.n(1))
                            act.activation(bufA, bufA, ACT.Ln).then_inc(logf.sem, 1)
                        n = k - FIRST_LEVEL + 1
                        if 0 <= n < 8:
                            act.wait_ge(*d_in.n(n + 1))
                            act.activation(dec[n % 2], dec[n % 2], ACT.Exp).then_inc(decay.sem, 1)
                        for a in behind:
                            ada_stage(act, ad[a], ADA_BANK)
                        if k == SUMS_AFTER + 1:
                            act.wait_ge(*meansq.n(1))
                            act.activation(gate_sig, ga, ACT.Sigmoid).then_inc(sg_done.sem, 1)
                            act.activation(dec[0], dec[0], ACT.Sqrt).then_inc(rooted.sem, 1)
                        p = k - FIRST_Z
                        if p >= 0:
                            act.wait_ge(*z_done.n(p + 1))
                            if p == 2:
                                act.wait_ge(*o_ready.n(1))
                            at = 2 * (p % 2)
                            act.activation(sa[p], psum[:, at:at + 2, 0:384], ACT.Abs).then_inc(z_abs.sem, 1)
                            act.wait_ge(*z_abs.n(p + 1))
                            act_chain.link(act, act.activation(sa[p], sa[p], ACT.Exp, scale=-1.0))

                    if l + 1 < LAYERS:
                        ada_copy(act, l + 1, ADA_BANK)

                    for p in range(SB // 2):
                        act.activation(sa[p], sa[p], ACT.Ln, bias=1.0).then_inc(soft.sem, 1)
                    for p in range(SB // 2):
                        act.wait_ge(*w_in.n(p + 1))
                        act.activation(sa[p], sa[p], ACT.Exp).then_inc(w_done.sem, 1)
                    for b in range(2):
                        act.wait_ge(*ob_done.n(2 * b + 2))
                        act.activation(oT[:, 1, 2 * b:2 * b + 2, :], psum[:, b, :].rearrange("p (c s) -> p c s", c=2),
                                       ACT.Copy).then_inc(ob_out.sem, 1)
                    for i in range(NT):
                        root_of_tile(act, i, 2 + i)

                @block.tensor
                def _(pe):
                    gate_rows(pe, l, 0, 4)
                    pe_transpose(pe, n_row, normed.n(NT), turned)
                    pe.wait_ge(*hT_done.n(4))
                    pe.wait_ge(*signal("gate_row").n(1))

                    def level(n):
                        m = LEVELS[n]
                        if m:
                            pe.wait_ge(*q_dec.n(n + 1))
                            pe.wait_ge(*k_dec.n(n + 1))
                        if n >= 2:
                            pe.wait_ge(*lvl_used.n(n - 1))
                        kk, qq = (heads(kd[n % 2]), heads(qd[n % 2])) if m else (heads(kT), qa)
                        for i in range(NT) if m < P else (0,):
                            for h in range(HG):
                                ti = slice(P, 2 * P) if m == P else slice(i * P, (i + 1) * P)
                                ins = pe.matmul(psum[:, 2 * (n % 2) + i, h * P:(h + 1) * P],
                                                kk[:, h, i * P:(i + 1) * P], qq[:, h, ti], start=True, stop=True)
                        ins.then_inc(lvl.sem, 1)

                    def outputs():
                        pe.wait_ge(*lvl_used.n(len(LEVELS)))
                        for h in range(HG):
                            v = [v_row[:, 0, i, h * P:(h + 1) * P] for i in range(NT)]
                            at = (h % 2) * S
                            pe.matmul(psum[:, h // 2, at:at + P], v[0], scT[:, 0, h, :], start=True, stop=True)
                            pe.matmul(psum[:, h // 2, at + P:at + S], v[0], scT[:, 2, h, :], start=True, stop=False)
                            ins = pe.matmul(psum[:, h // 2, at + P:at + S], v[1], scT[:, 1, h, :], start=False, stop=True)
                        ins.then_inc(o_done.sem, 1)

                    def square_sums():
                        pe.wait_ge(*osq.n(1))
                        for b in range(2):
                            ins = pe.matmul(psum[:, 2 + b, :], C["ones"], bufA[:, b * 512:(b + 1) * 512], start=True, stop=True)
                        ins.then_inc(oss.sem, 1)

                    tri, ones = C["tri"], C["ones"]

                    def qk(p, i, banks, lo, hi, stop):
                        at = S * i
                        for hh in range(2):
                            r = slice(64 * hh, 64 * hh + 64)
                            ins = pe.matmul(psum[:, banks + hh, at:at + hi - lo], kb[r, p, i * P:(i + 1) * P], qb[r, p, lo:hi],
                                            start=True, stop=stop)
                        return ins

                    def z(p):
                        at = 2 * (p % 2)
                        if p == 1:
                            pe.wait_ge(*meansq.n(1))
                        if p >= 2:
                            pe.wait_ge(*z_abs.n(p - 1))
                            pe.wait_ge(*z_max.n(p - 1))
                        qk(p, 0, at, 0, S, True)
                        qk(p, 1, at, P, S, True).then_inc(z_done.sem, 1)

                    def ada_step(a):
                        if a > 0:
                            ada_columns(pe, a - 1, ADA_BANK)
                        ada_products(pe, ad[a], ADA_BANK)

                    for k in range(PROJ_UNITS):
                        within, behind = ada_slots(l, k)
                        w = unit(pe, pj[k]).rearrange("p (c n) -> p c n", c=DC)
                        if k >= PROJ_BANKS:
                            pe.wait_ge(*proj_out.n(k - PROJ_BANKS + 1))
                        for j in range(2):
                            for c in range(DC):
                                if k in (6, 7, 12, 13):
                                    v, b = hT[:, c, j * P:(j + 1) * P], w[:, c, :]
                                else:
                                    v, b = w[:, c, j * P:(j + 1) * P], hT[:, c, :]
                                ins = pe.matmul(psum[:, 4 + k % PROJ_BANKS, j * S:(j + 1) * S], v, b,
                                                start=(c == 0), stop=(c == DC - 1))
                            if j == 0:
                                for a in within:
                                    ada_step(a)
                        ins.then_inc(w_used, 1)
                        if 0 <= k - FIRST_LEVEL < len(LEVELS):
                            level(k - FIRST_LEVEL)
                        if k == OUT_AFTER:
                            outputs()
                        if k == SUMS_AFTER:
                            square_sums()
                        for a in behind:
                            ada_step(a)
                        if k >= FIRST_Z:
                            z(k - FIRST_Z)
                    if l + 1 < LAYERS:
                        ada_columns(pe, ADA_UNITS - 1, ADA_BANK)

                    def sums(p):
                        L, at = ls[p], 4 + 2 * (p % 2)
                        pe.wait_ge(*logs.n(p + 1))
                        if p >= 2:
                            pe.wait_ge(*w_in.n(p - 1))
                        qk(p, 0, at, 0, S, False)
                        for hh in range(2):
                            b = psum[:, at + hh, :]
                            pe.matmul(b[:, P:S], ones, L[:, hh, S:S + P], start=False, stop=False)
                            pe.matmul(b[:, 0:S], tri, L[:, hh, 0:S], start=False, stop=True)
                        qk(p, 1, at, P, S, False)
                        for hh in range(2):
                            ins = pe.matmul(psum[:, at + hh, S:S + P], tri, L[:, hh, S:S + P], start=False, stop=True)
                        ins.then_inc(inc.sem, 1)

                    def weighted(p):
                        pe.wait_ge(*w_done.n(p + 1))
                        half = (p % 2) * S
                        for to, i, tile, start, stop in ((0, 0, 0, True, True), (P, 0, 1, True, False), (P, 1, 2, False, True)):
                            for hh in range(2):
                                h = 2 * p + hh
                                ins = pe.matmul(psum[64 * hh:64 * hh + 64, p // 2, half + to:half + to + P],
                                                v_row[:, 1, i, h * 64:(h + 1) * 64],
                                                sa[p][:, hh, tile * P:(tile + 1) * P], start=start, stop=stop)
                        ins.then_inc(ob_done.sem, 1)

                    def project_up(q, k):
                        w = unit(pe, um + 2 * q + k).rearrange("p (c n) -> p c n", c=4)
                        for j in range(4):
                            for c in range(4):
                                ins = pe.matmul(psum[:, UP_BANKS[2 * q + k] + j // 2, (j % 2) * S:(j % 2) * S + S],
                                                w[:, c, j * P:(j + 1) * P], oT[:, k, c, :],
                                                start=(c == 0), stop=(c == 3))
                        ins.then_inc(w_used, 1)

                    pe.wait_ge(*proj_out.n(PROJ_UNITS))
                    if l + 1 < LAYERS:
                        pe.wait_ge(*mod_copied.n(1))
                    pe.wait_ge(*o_ready.n(1))
                    pe.wait_ge(*z_abs.n(SB // 2))
                    pe.wait_ge(*z_max.n(SB // 2))
                    project_up(0, 0)
                    for p in range(SB // 2):
                        sums(p)
                        if p >= 2:
                            weighted(p - 2)
                    weighted(SB // 2 - 2)
                    weighted(SB // 2 - 1)

                    pe.wait_ge(*ob_out.n(2))
                    project_up(0, 1)
                    pe.wait_ge(*w_in.n(SB // 2))
                    project_up(1, 0)
                    project_up(1, 1)
                    for i in range(NT):
                        for k in range(4):
                            w = unit(pe, uo + k).rearrange("p (c n) -> p c n", c=2)
                            if i == 0 and k % 2 == 0:
                                pe.wait_ge(*merged.n(k // 2 + 1))
                            for cc in range(2):
                                for hh in range(2):
                                    ins = pe.matmul(psum[:, 2 * i + hh, :], mT[:, 2 * k + cc, i * P:(i + 1) * P],
                                                    w[:, cc, hh * 512:(hh + 1) * 512],
                                                    start=(k == 0 and cc == 0), stop=(k == 3 and cc == 1))
                            if i == NT - 1:
                                ins.then_inc(w_used, 1)
                        if i == 0:
                            ins.then_inc(first_out.sem, 1)
                    modulation_rows(pe, l, 1, 4)

                @block.vector
                def _(dve):
                    link = lambda ins: dve_chain.link(dve, ins)
                    modulate(dve, 0)
                    if l == 0:
                        l0, l1 = col("lb_logits_2", 0, 4), col("lb_logits_2", 4, 4)
                        link(dve.tensor_tensor(lb[:, 3, 0:4], l0, l1, ALU.max))
                        for k, v in enumerate((l0, l1)):
                            ins = dve.tensor_tensor(lb[:, 2, 4 * k:4 * k + 4], v, lb[:, 3, 0:4], ALU.subtract)
                        ins.then_inc(lbs.sem, 1)
                        dve.wait_ge(*lbs.n(2))
                        link(dve.tensor_tensor(lb[:, 3, 0:4], lb[:, 2, 0:4], lb[:, 2, 4:8], ALU.add))
                        link(dve.reciprocal(lb[:, 3, 0:4], lb[:, 3, 0:4]))
                        for k in range(2):
                            ins = dve.tensor_tensor(lb[:, 2, 4 * k:4 * k + 4], lb[:, 2, 4 * k:4 * k + 4], lb[:, 3, 0:4], ALU.mult)
                        link(ins)
                        dve.tensor_tensor(lb[:, 0, 0:4], lb[:, 2, 0:4], lb[:, 2, 0:4], ALU.subtract)
                        link(dve.tensor_tensor(lb[:, 0, 4:8], lb[:, 2, 0:4], lb[:, 2, 4:8], ALU.add))
                        link(dve.tensor_tensor(lb[:, 0, 4:8], lb[:, 0, 4:8], lb[:, 2, 0:4], ALU.subtract))
                        link(dve.tensor_scalar(lb[:, 1, :], lb[:, 0, :], -1.0, 1.0, ALU.mult, ALU.add))

                    dve.wait_ge(*gates_exp.n(2))
                    for b in (bufA, kT):
                        ins = dve.tensor_scalar(b, b, 1.0, None, ALU.add)
                    link(ins)
                    for b in (bufA, kT):
                        ins = dve.reciprocal(b, b)
                    link(ins)
                    for h in range(HG):
                        ins = dve.tensor_scalar(heads(bufA)[:, h, :], heads(bufA)[:, h, :], lb[:, 1, 4 * l + h:4 * l + h + 1],
                                                lb[:, 0, 4 * l + h:4 * l + h + 1], ALU.mult, ALU.add)
                    ins.then_inc(logf_in.sem, 1)
                    for h in range(HG):
                        ins = dve.tensor_scalar(heads(kT)[:, h, :], heads(kT)[:, h, :], lb[:, 1, 4 * l + h:4 * l + h + 1],
                                                None, ALU.mult)
                    ins.then_inc(logf_in.sem, 1)
                    dve.wait_ge(*logf.n(1))
                    src, dst = bufA, bufB
                    step = 1
                    while step < P:
                        a, b = (v.rearrange("p (x t) -> p x t", t=P) for v in (src, dst))
                        dve.tensor_copy(b[:, :, 0:step], a[:, :, 0:step])
                        link(dve.tensor_tensor(b[:, :, step:P], a[:, :, step:P], a[:, :, 0:P - step], ALU.add))
                        src, dst = dst, src
                        step *= 2
                    cum = src

                    def distances(n):
                        m = LEVELS[n]
                        if n >= 2:
                            dve.wait_ge(*k_dec.n(n - 1))
                            dve.wait_ge(*q_dec.n(n - 1))
                        b = cum.rearrange("p (x two m) -> p x two m", two=2, m=m)
                        d = dec[n % 2].rearrange("p (x two m) -> p x two m", two=2, m=m)
                        x = 4 * S // (2 * m)
                        ref = b[:, :, 0, m - 1:m].broadcast_to((P, x, m))
                        if m == P:
                            dve.tensor_copy(d[:, :, 1, :], b[:, :, 1, :])
                        else:
                            dve.tensor_tensor(d[:, :, 1, :], b[:, :, 1, :], ref, ALU.subtract)
                        dve.tensor_tensor(d[:, :, 0, :], ref, b[:, :, 0, :], ALU.subtract).then_inc(d_in.sem, 1)

                    def keep_level(n):
                        m = LEVELS[n]
                        dve.wait_ge(*lvl.n(n + 1))
                        if n >= 1:
                            dve.wait_ge(*lvl_used.n(n))
                        if m == P:
                            dve.wait_ge(*signal("scores_zero").n(1))
                            dve.tensor_copy(scT[:, 2, :, :], psum[:, 0, :].rearrange("p (h t) -> p h t", h=HG)).then_inc(lvl_used.sem, 1)
                            return
                        mask = (C[f"level{m}"] if m else ident).bitcast(U32).unsqueeze(1).broadcast_to((P, HG, P))
                        for i in range(NT):
                            ins = dve.copy_predicated(scT[:, i, :, :], mask,
                                                      psum[:, 2 * (n % 2) + i, :].rearrange("p (h t) -> p h t", h=HG))
                        ins.then_inc(lvl_used.sem, 1)

                    distances(0)
                    for n in range(8):
                        if n + 1 < 8:
                            distances(n + 1)
                        dve.wait_ge(*decay.n(n + 1))
                        dve.wait_ge(*proj_out.n(4))
                        if n >= 2:
                            dve.wait_ge(*lvl.n(n - 1))
                        dve.tensor_tensor(heads(qd[n % 2]), qa, heads(dec[n % 2]), ALU.mult).then_inc(q_dec.sem, 1)
                        if n >= 1:
                            keep_level(n - 1)
                    keep_level(7)
                    keep_level(8)

                    dve.wait_ge(*o_done.n(1))
                    link(dve.tensor_copy(oT[:, 0, :, :], psum[:, 0:2, :].rearrange("p b (h s) -> p (b h) s", h=2)))
                    dve.tensor_tensor(heads(bufA), oT[:, 0, :, :], oT[:, 0, :, :], ALU.mult).then_inc(osq.sem, 1)
                    dve.wait_ge(*oss.n(1))
                    dve.tensor_scalar(bufA.rearrange("p (b n) -> p b n", b=2), psum[:, 2:4, :], 1.0 / 128, 1e-6,
                                      ALU.mult, ALU.add).then_inc(meansq.sem, 1)
                    dve.wait_ge(*rooted.n(1))
                    link(dve.reciprocal(bufA, bufA))
                    for h in range(HG):
                        ins = dve.scalar_tensor_tensor(out=oT[:, 0, h, :], in0=oT[:, 0, h, :],
                                                       scalar=col("hg_norm_g_2", 4 * l + h), in1=heads(bufA)[:, h, :],
                                                       op0=ALU.mult, op1=ALU.mult)
                    link(ins)
                    dve.wait_ge(*sg_done.n(1))
                    dve.wait_ge(*proj_out.n(6))
                    link(dve.tensor_tensor(ga, ga, gate_sig, ALU.mult))
                    dve.tensor_tensor(oT[:, 0, :, :], oT[:, 0, :, :], ga, ALU.mult).then_inc(o_ready.sem, 1)
                    dve.wait_ge(*o_ready.n(1))

                    def masks(name):
                        at = CONSTS.index(name)
                        return const[:, at:at + 3, :].rearrange("p k t -> p (k t)").unsqueeze(1).broadcast_to((P, 2, 384))

                    for p in range(SB // 2):
                        dve.wait_ge(*z_abs.n(p + 1))
                        at = 2 * (p % 2)
                        dve.tensor_scalar(ls[p], psum[:, at:at + 2, 0:384], 0.0, None, ALU.max).then_inc(z_max.sem, 1)

                    def log_one_minus_beta(p):
                        dve.wait_ge(*soft.n(p + 1))
                        dve.wait_ge(*z_max.n(p + 1))
                        link(dve.tensor_tensor(ls[p], ls[p], sa[p], ALU.add))
                        dve.tensor_tensor(ls[p], ls[p], masks("neg00"), ALU.mult).then_inc(logs.sem, 1)

                    def weights_in(p):
                        dve.wait_ge(*inc.n(p + 1))
                        at = 4 + 2 * (p % 2)
                        dve.tensor_tensor(sa[p], psum[:, at:at + 2, 0:384], masks("fill00"), ALU.add).then_inc(w_in.sem, 1)

                    for p in range(SB // 2):
                        log_one_minus_beta(p)
                        if p >= 1:
                            weights_in(p - 1)
                    weights_in(SB // 2 - 1)

                    for q in range(2):
                        dve.wait_ge(w_used, um + 2 * q + 2)
                        for k in range(2):
                            g = gates[2 * q + k].rearrange("p (b j) s -> p b (j s)", b=2)
                            ins = dve.tensor_tensor(g, g, psum[:, UP_BANKS[2 * q + k]:UP_BANKS[2 * q + k] + 2, :], ALU.mult)
                        link(ins)
                        dve.tensor_tensor(mT[:, 4 * q:4 * q + 4, :], gates[2 * q], gates[2 * q + 1],
                                          ALU.add).then_inc(merged.sem, 1)
                    if l + 1 < LAYERS:
                        finish_modulation(dve, l + 1)
                    for i in range(NT):
                        dve.wait_ge(*(first_out.n(1) if i == 0 else (w_used, end)))
                        residual_norm(dve, i, 2 * i, gb, signal("ln_rows").n(32), 2 + i)
            if l + 1 < LAYERS:
                advance(ada_staged=ADA_UNITS, ada_done=1, mod_copied=1)
            advance(mod_rows=1, gate_rows=1, gate_row=1, rows_normed=NT, turned=4, hT_done=4, att_proj_copied=PROJ_UNITS,
                    forget_exps=2, forget_in=2,
                    forget_log=1, decay_in=8, decay=8, q_decayed=8, k_decayed=8, level_products=9, level_kept=9,
                    att_first_out=1, mean_squares=3, rooted=3, hgrn_out=1, hgrn_squares=1, hgrn_sums=1, silu_gate=1, stick_z=SB // 2,
                    stick_soft=SB // 2, stick_logs=SB // 2, stick_sums=SB // 2, stick_w_in=SB // 2, stick_w=SB // 2, stick_out=SB // 2, stick_copied=2,
                    stick_z_abs=SB // 2, stick_z_max=SB // 2,
                    heads_ready=1, merged=2, ln_rows=32, scores_zero=1)
            ph.close()

        GS = 8
        TURNS = K_ALL // GS
        DVE_SLOTS = (3, 7)
        DVE_FROM = (4, 0)

        def peer(l):
            ph = ExitStack()
            slots = sb(f"peer{l}_slots", [P, GS, D], where=ph)
            qT = sb(f"peer{l}_qT", [P, PH, S], where=ph)
            keysT = sb(f"peer{l}_keysT", [P, PH, P], where=ph)
            cand = sb(f"peer{l}_cand", [P, PH, TOPK, TOPK], where=ph)
            rest = sb(f"peer{l}_rest", [P, 2 * PH, P], where=ph)
            best = sb(f"peer{l}_best", [P, 2 * PH, TOPK], where=ph)
            besti = sb(f"peer{l}_besti", [P, 2 * PH, TOPK], U32, where=ph)
            bestf = sb(f"peer{l}_bestf", [P, 2 * PH, TOPK], where=ph)
            top = sb(f"peer{l}_top", [P, PH, TOPK], where=ph)
            pos = sb(f"peer{l}_pos", [P, 3, K_ALL], U32, where=ph)
            posf = sb(f"peer{l}_posf", [P, 2, K_ALL], where=ph)
            key = sb(f"peer{l}_key", [P, 2, K_ALL], where=ph)
            idx = sb(f"peer{l}_idx", [P, NT, K_ALL], U32, where=ph)
            gate = sb(f"peer{l}_gate", [P, NT, K_ALL], where=ph)
            gsum = sb(f"peer{l}_gsum", [P, PH], where=ph)
            pre = sb(f"peer{l}_pre", [P, NT, K_ALL], where=ph)
            dots = sb(f"peer{l}_dots", [P, GS], where=ph)
            staged_idx = sb(f"peer{l}_staged_idx", [P, GS], U32, where=ph)
            diag = sb(f"peer{l}_diag", [P, GS, P], where=ph)
            iota = sb(f"peer{l}_iota", [P, TOPK], where=ph)
            gb = sb(f"peer{l}_gb", [P, 2, D], where=ph)
            end = layer_at[l + 1] if l + 1 < LAYERS else len(stream)
            uq = end - PEER_UNITS
            small, ln_rows = signal("layer_small"), signal("ln_rows")
            acc = cand[:, :, :, :].rearrange("p h a b -> p (h a b)").rearrange("p (i d) -> p i d", i=NT)
            (turned, hT_done, normed, q_out, scored, keys_kept, idx_ready, gate_in, gate_exp, u_used, kept, gelu_in,
             gelu, weights, diagd, staged, meansq, rooted) = (signal(n) for n in (
                 "turned", "hT_done", "rows_normed", "query_copied", "key_scores", "keys_kept", "indices_ready", "gate_in",
                 "gate_exp", "u_used", "dots_kept", "gelu_in", "gelu", "expert_weights", "diagonal", "staged",
                 "mean_squares", "rooted"))
            landed = [signal(f"gathered{s}") for s in range(GS)]
            q_done = signal("query_done")
            v_used = [signal(f"v_used{s}") for s in range(GS)]

            def diagonals(i, j):
                fewer = GS - len(DVE_SLOTS)
                per_tile = [GS * d + fewer * (TURNS - d) for d in DVE_FROM]
                if isinstance(j, int) and j <= DVE_FROM[i]:
                    return sum(per_tile[:i]) + GS * j
                if isinstance(j, int):
                    return sum(per_tile[:i]) + GS * DVE_FROM[i] + fewer * (j - DVE_FROM[i])
                return None

            def pe_slots(shared):
                return [s for s in range(GS) if not (shared and s in DVE_SLOTS)]

            def turns_of(eng, i, turn, before_shared=None):
                first = DVE_FROM[i]
                turn(0, pe_slots(first == 0), diagonals(i, 0))
                for lo, hi, shared in ((1, first, False), (max(first, 1), TURNS - 1, True)):
                    if shared and before_shared is not None:
                        before_shared()
                    if hi > lo:
                        some = pe_slots(shared)
                        with eng.Fori(lo, hi) as j:
                            turn(j, some, j * len(some) + (diagonals(i, lo) - lo * len(some)))
                turn(TURNS - 1, pe_slots(True), diagonals(i, TURNS - 1))

            u_tab, v_tab = dram["peer_u_2"], dram["peer_v_2"]
            rows_of = PEER_ROWS * l

            with nc.Block() as block:
                @block.sync
                def _(sp):
                    sp.dma_start(keysT[:, :, :], dram["sub_keys_2"][l]).then_inc(small.sem, 16)
                    sp.dma_start(iota[:, :], dram["iota"][:, 0:TOPK]).then_inc(small.sem, 16)
                    for k, n in enumerate(("ln_g_2", "ln_b_2")):
                        sp.dma_start(gb[:, k, :], dram[n][l, 1]).then_inc(ln_rows.sem, 16)
                    load_until(sp, end)
                    if l == LAYERS - 1:
                        for i in range(NT):
                            sp.wait_ge(*signal("result").n(i + 1))
                            sp.dma_start(out[:, i, :], x_row[:, i, :]).then_inc(signal("stored").sem, 16)
                        sp.wait_ge(*signal("stored").n(NT * 16))

                @block.gpsimd
                def _(pool):
                    def stage(i, j, s, free):
                        pool.wait_ge(*free)
                        k = j * GS + s
                        column = idx[:, i, k:k + 1] if isinstance(k, int) else idx[:, i, bass.ds(k, 1)]
                        pool.tensor_copy(staged_idx[:, s:s + 1], column).then_inc(staged.sem, 1)

                    def gather(table, s):
                        pool.indirect_dma_start(
                            out=slots[:, s, :], out_offset=None, in_=table,
                            in_offset=bass.IndirectOffsetOnAxis(ap=staged_idx[:, s:s + 1], axis=0),
                        ).then_inc(landed[s].sem, 16)

                    at = 0
                    for i in range(NT):
                        pool.wait_ge(*idx_ready.n(i * 2 + 1))
                        for table in (u_tab, v_tab):
                            for s in range(GS):
                                if s > 0:
                                    pool.wait_ge(*staged.n(at + s))
                                if table is v_tab:
                                    free = u_used.n(K_ALL * (i + 1) - GS + s + 1)
                                else:
                                    free = v_used[s].n(i * TURNS) if i > 0 else idx_ready.n(1)
                                stage(i, 0, s, free)
                                if s > 0:
                                    gather(table, s - 1)
                            for lo, hi in ((1, TURNS // 2), (TURNS // 2, TURNS)):
                                if lo > 1 and i == 0 and table is u_tab:
                                    pool.wait_ge(*idx_ready.n(2))
                                with pool.Fori(lo, hi) as j:
                                    for s in range(GS):
                                        pool.wait_ge(*staged.n(j * GS + (at + s)))
                                        stage(i, j, s, v_used[s].n(j + i * TURNS) if table is v_tab else
                                              u_used.n(j * GS + (i * K_ALL - GS + s + 1)))
                                        gather(table, (s - 1) % GS)
                            at += K_ALL
                            pool.wait_ge(*staged.n(at))
                            gather(table, GS - 1)

                def arrived(eng, s, rnd, j):
                    eng.wait_ge(*landed[s].n(j * 16 + 16 * (rnd * TURNS + 1)))

                @block.scalar
                def _(act):
                    copy_gate_row(act, 0)
                    turn_copies(act)
                    for i in range(NT):
                        for k in range(PEER_UNITS):
                            act.wait_ge(*(q_done.n(k + 1) if i == 0 else (w_used, uq + k + 1)))
                            of_tile = slice(i * P, (i + 1) * P)
                            act.activation(qT[:, 2 * k:2 * k + 2, of_tile],
                                           psum[:, 4 + k, :].rearrange("p (j s) -> p j s", j=2)[:, :, of_tile],
                                           ACT.Copy).then_inc(q_out.sem, 1)

                    def gate_exps(i):
                        act.wait_ge(*gate_in.n(i + 1))
                        act.activation(gate[:, i, :], gate[:, i, :], ACT.Exp).then_inc(gate_exp.sem, 1)

                    for i in range(NT):
                        if i == 0:
                            gate_exps(0)
                        act.wait_ge(*gelu_in.n(i + 1))
                        act.activation(pre[:, i, :], pre[:, i, :], ACT.Gelu).then_inc(gelu.sem, 1)
                        act.wait_ge(*weights.n(i + 1))

                        def turn(j, slots_, first):
                            for s in slots_:
                                k = j * GS + s
                                w = pre[:, i, k:k + 1] if isinstance(k, int) else pre[:, i, bass.ds(k, 1)]
                                if i > 0 or not isinstance(j, int) or j > 0:
                                    act.wait_ge(*v_used[s].n(j + i * TURNS))
                                act.activation(diag[:, s, :], ident, ACT.Copy, scale=w).then_inc(diagd.sem, 1)

                        turns_of(act, i, turn, lambda: gate_exps(1) if i == 0 else root_of_tile(act, 0, 1))
                    root_of_tile(act, 1, 2)

                @block.tensor
                def _(pe):
                    gate_rows(pe, l, 1, 0)
                    pe.wait_ge(*signal("gate_row").n(1))
                    pe_transpose(pe, n_row, normed.n(NT), turned)
                    pe.wait_ge(*hT_done.n(4))
                    def score(i):
                        for half in range(2):
                            r = slice(64 * half, 64 * half + 64)
                            for h in range(PH):
                                ins = pe.matmul(psum[:, 2 * half + h // 4, (h % 4) * P:(h % 4 + 1) * P],
                                                qT[r, h, i * P:(i + 1) * P], keysT[r, h, :], start=True, stop=True)
                        ins.then_inc(scored.sem, 1)

                    for i in range(NT):
                        for k in range(PEER_UNITS):
                            w = unit(pe, uq + k).rearrange("p (c n) -> p c n", c=DC)
                            for j in range(2):
                                for c in range(DC):
                                    at = j * S + i * P
                                    ins = pe.matmul(psum[:, 4 + k, at:at + P], w[:, c, j * P:(j + 1) * P],
                                                    hT[:, c, i * P:(i + 1) * P], start=(c == 0), stop=(c == DC - 1))
                            ins.then_inc(*((q_done.sem, 1) if i == 0 else (w_used, 1)))
                        if i == 0:
                            pe.wait_ge(*small.n(32))
                            pe.wait_ge(*q_out.n(PEER_UNITS))
                            score(0)
                    pe.wait_ge(*keys_kept.n(1))
                    pe.wait_ge(*q_out.n(2 * PEER_UNITS))
                    score(1)
                    for i in range(NT):
                        def turn(j, slots_, first):
                            for n, s in enumerate(slots_):
                                arrived(pe, s, 2 * i + 1, j)
                                pe.wait_ge(*diagd.n(first + (n + 1)))
                                last = isinstance(j, int) and j == TURNS - 1 and s == slots_[-1]
                                for h in range(2):
                                    ins = pe.matmul(psum[:, 4 + 2 * i + h, :], diag[:, s, :],
                                                    slots[:, s, h * 512:(h + 1) * 512],
                                                    start=isinstance(j, int) and j == 0 and s == 0, stop=last)
                                ins.then_inc(v_used[s].sem, 1)

                        turns_of(pe, i, turn)
                    if l + 1 < LAYERS:
                        pe.wait_ge(*keys_kept.n(NT))
                        modulation_rows(pe, l + 1, 0, 0)

                @block.vector
                def _(dve):
                    link = lambda ins: dve_chain.link(dve, ins)
                    modulate(dve, 4)
                    dve.wait_ge(*small.n(32))

                    def top16(rows, values, rest_of, val, ind):
                        for g in rows:
                            ins = dve.max(val(g)[:, 0:8], values(g))
                        link(ins)
                        for g in rows:
                            dve.max_index(ind(g)[:, 0:8], val(g)[:, 0:8], values(g))
                        for g in rows:
                            ins = dve.match_replace(out=rest_of(g), in_to_replace=val(g)[:, 0:8], in_values=values(g),
                                                    imm_value=NEG)
                        link(ins)
                        for g in rows:
                            ins = dve.max(val(g)[:, 8:16], rest_of(g))
                        link(ins)
                        for g in rows:
                            ins = dve.max_index(ind(g)[:, 8:16], val(g)[:, 8:16], rest_of(g))
                        return ins

                    def best_keys(i, lo, hi):
                        dve.wait_ge(*scored.n(i + 1))
                        ins = top16([half * PH + h for half in range(2) for h in range(lo, hi)],
                                    lambda g: psum[:, g // 4, (g % 4) * P:(g % 4 + 1) * P], lambda g: rest[:, g, :],
                                    lambda g: best[:, g, :], lambda g: besti[:, g, :])
                        if hi == PH:
                            ins.then_inc(keys_kept.sem, 1)
                            dve.wait_ge(*keys_kept.n(i + 1))
                        else:
                            link(ins)
                        for a in (lo, PH + lo):
                            dve.tensor_copy(bestf[:, a:a + hi - lo, :], besti[:, a:a + hi - lo, :])
                        shape = (P, hi - lo, TOPK, TOPK)
                        link(dve.tensor_tensor(cand[:, lo:hi, :, :], best[:, lo:hi, :].unsqueeze(3).broadcast_to(shape),
                                               best[:, PH + lo:PH + hi, :].unsqueeze(2).broadcast_to(shape), ALU.add))

                    def best_sums(i, lo, hi):
                        pos8 = pos[:, 0, :].rearrange("p (h k) -> p h k", h=PH)
                        flat = rest[:, :, :].rearrange("p (h a) n -> p h (a n)", h=PH)
                        link(top16(range(lo, hi), lambda h: cand[:, h, :, :].rearrange("p a b -> p (a b)"),
                                   lambda h: flat[:, h, :], lambda h: top[:, h, :], lambda h: pos8[:, h, :]))

                    def expert_numbers(i, lo, hi):
                        ks = slice(lo * TOPK, hi * TOPK)
                        shape = (P, hi - lo, TOPK, TOPK)
                        dve.tensor_scalar(pos[:, 1, ks], pos[:, 0, ks], 4, None, ALU.logical_shift_right)
                        link(dve.tensor_scalar(pos[:, 2, ks], pos[:, 0, ks], 15, None, ALU.bitwise_and))
                        link(dve.tensor_copy(posf[:, :, ks], pos[:, 1:3, ks]))
                        hot = rest[:, :, :].rearrange("p (h a) (b n) -> p h (a b) n", h=PH, n=TOPK)[:, lo:hi, :, :]
                        for half in range(2):
                            p8 = posf[:, half, ks].rearrange("p (h k) -> p h k", h=hi - lo)
                            link(dve.tensor_tensor(hot, p8.unsqueeze(3).broadcast_to(shape),
                                                   iota[:, :].unsqueeze(1).unsqueeze(1).broadcast_to(shape), ALU.is_equal))
                            link(dve.tensor_tensor(hot, hot, bestf[:, half * PH + lo:half * PH + hi, :].unsqueeze(2)
                                                   .broadcast_to(shape), ALU.mult))
                            link(dve.tensor_reduce(key[:, half, ks].rearrange("p (h k) -> p h k", h=hi - lo), hot,
                                                   AX.X, ALU.add))
                        link(dve.tensor_scalar(key[:, 0, ks], key[:, 0, ks], float(P), float(rows_of), ALU.mult, ALU.add))
                        dve.tensor_tensor(idx[:, i, ks], key[:, 0, ks], key[:, 1, ks], ALU.add).then_inc(idx_ready.sem, 1)

                    def gates(i):
                        g3 = gate[:, i, :].rearrange("p (h k) -> p h k", h=PH)
                        dve.tensor_tensor(g3, top[:, :, :], top[:, :, 0:1].broadcast_to((P, PH, TOPK)),
                                          ALU.subtract).then_inc(gate_in.sem, 1)
                        dve.wait_ge(*gate_exp.n(i + 1))
                        link(dve.tensor_reduce(gsum[:, :], g3, AX.X, ALU.add))
                        link(dve.reciprocal(gsum[:, :], gsum[:, :]))
                        link(dve.tensor_tensor(g3, g3, gsum[:, :].unsqueeze(2).broadcast_to((P, PH, TOPK)), ALU.mult))

                    def dot_rows(i, lo, hi):
                        with dve.Fori(lo, hi) as j:
                            for s in range(GS):
                                arrived(dve, s, 2 * i, j)
                                dve.tensor_tensor_reduce(out=slots[:, s, :], in0=slots[:, s, :], in1=n_row[:, i, :],
                                                         scale=1.0, scalar=0.0, op0=ALU.mult, op1=ALU.add,
                                                         accum_out=dots[:, s:s + 1]).then_inc(u_used.sem, 1)
                            dve.wait_ge(*u_used.n(j * GS + (i * K_ALL + GS)))
                            dve.tensor_copy(pre[:, i, bass.ds(j * GS, GS)], dots[:, :]).then_inc(kept.sem, 1)
                            dve.wait_ge(*kept.n(j + (i * TURNS + 1)))

                    def add_rows(i):
                        n = len(DVE_SLOTS)
                        with dve.Fori(DVE_FROM[i], TURNS) as j:
                            for m, s in enumerate(DVE_SLOTS):
                                arrived(dve, s, 2 * i + 1, j)
                                dve.scalar_tensor_tensor(out=acc[:, i, :], in0=slots[:, s, :],
                                                         scalar=pre[:, i, bass.ds(j * GS + s, 1)], in1=acc[:, i, :],
                                                         op0=ALU.mult, op1=ALU.add).then_inc(v_used[s].sem, 1)
                                dve.wait_ge(*v_used[s].n(j + (i * TURNS + 1)))

                    def finish(i):
                        for s in range(GS):
                            dve.wait_ge(*v_used[s].n((i + 1) * TURNS))
                        ins = residual_norm(dve, i, 4 + 2 * i, gb, ln_rows.n(32), 1 + i, acc[:, i, :])
                        if l == LAYERS - 1:
                            ins.then_inc(signal("result").sem, 1)

                    mid = PH // 2
                    best_keys(0, 0, mid)
                    best_sums(0, 0, mid)
                    expert_numbers(0, 0, mid)
                    dot_rows(0, 0, 1)
                    best_keys(0, mid, PH)
                    dot_rows(0, 1, 4)
                    best_sums(0, mid, PH)
                    dot_rows(0, 4, 7)
                    expert_numbers(0, mid, PH)
                    gates(0)
                    dot_rows(0, 7, TURNS)
                    for i in range(NT):
                        if i > 0:
                            dot_rows(i, 0, TURNS)
                        dve.engine_nop().then_inc(gelu_in.sem, 1)
                        dve.wait_ge(*gelu.n(i + 1))
                        dve.tensor_tensor(pre[:, i, :], pre[:, i, :], gate[:, i, :], ALU.mult).then_inc(weights.sem, 1)
                        dve.wait_ge(*weights.n(i + 1))
                        if i + 1 < NT:
                            best_keys(i + 1, 0, PH)
                            best_sums(i + 1, 0, PH)
                            expert_numbers(i + 1, 0, PH)
                            gates(i + 1)
                            link(dve.memset(acc[:, :, :], 0.0))
                        else:
                            finish(0)
                        add_rows(i)
                    finish(1)
            advance(mod_rows=1, gate_rows=1, gate_row=1, rows_normed=NT, turned=4, hT_done=4, layer_small=32, ln_rows=32,
                    query_done=PEER_UNITS,
                    query_copied=NT * PEER_UNITS,
                    key_scores=NT, keys_kept=NT, indices_ready=NT + 1, gate_in=NT, gate_exp=NT, u_used=NT * K_ALL,
                    dots_kept=NT * TURNS, gelu_in=NT, gelu=NT, expert_weights=NT,
                    diagonal=diagonals(NT - 1, TURNS), staged=2 * NT * K_ALL, mean_squares=2, rooted=2,
                    **{f"gathered{s}": 2 * NT * TURNS * 16 for s in range(GS)},
                    **{f"v_used{s}": NT * TURNS for s in range(GS)})
            ph.close()

        for l in range(LAYERS):
            attention(l)
            if stop_after <= 3 + 2 * l:
                return
            peer(l)
            if stop_after <= 4 + 2 * l:
                return


def column_vectors(v):
    import numpy as np
    parts = []
    for name in COLS:
        a = np.asarray(v[name]).reshape(-1, P)
        parts.append(a.T)
    return np.ascontiguousarray(np.concatenate(parts, axis=1))


def constant_matrices():
    import numpy as np
    s, t = np.arange(P)[:, None], np.arange(P)[None, :]
    m = {"ident": s == t, "ones": s >= 0 * t, "heads64": s // 64 == t // 64, "tri": s >= t, "quarters": s % 32 == 0 * t,
         "neg00": -1.0 * (s < t), "neg01": -1.0 * (s >= 0 * t), "neg11": -1.0 * (s < t),
         "fill00": NEG * (s >= t), "fill01": 0.0 * (s >= t), "fill11": NEG * (s >= t)}
    for h in (64, 32, 16, 8, 4, 2, 1):
        m[f"level{h}"] = (s // (2 * h) == t // (2 * h)) & (s % (2 * h) < h) & (t % (2 * h) >= h)
    return np.ascontiguousarray(np.stack([np.broadcast_to(m[n], (P, P)).astype(np.float32) for n in CONSTS], axis=1))


def layouts(v):
    import numpy as np
    v = {k: np.asarray(a) for k, a in v.items()}

    def by_columns(w, n):
        *lead, k, cols = w.shape
        w = w.reshape(*lead, k // P, P, cols // n, n)
        i = len(lead)
        w = w.transpose(*range(i), i + 2, i + 1, i, i + 3)
        return np.ascontiguousarray(w.reshape(*lead, cols // n, P, k // P * n))

    def by_rows(w, c):
        *lead, k, cols = w.shape
        w = w.reshape(*lead, k // P // c, c, P, cols)
        i = len(lead)
        w = w.transpose(*range(i), i, i + 2, i + 1, i + 3)
        return np.ascontiguousarray(w.reshape(*lead, k // P // c, P, c * cols))

    def rows(a, n=P):
        return np.ascontiguousarray(np.broadcast_to(a.reshape(1, -1), (n, a.size)))

    out = {
        "x": v["x"].reshape(NT, P, D).transpose(1, 0, 2),
        "consts": constant_matrices(),
        "cols": column_vectors(v),
        "iota": rows(np.arange(P, dtype=np.float32)),
        "w_in": by_columns(v["w_in"][0], 256),
        "w_out": by_rows(v["w_out"][0], 2),
        "w_route": np.concatenate([v["w_route_group"][0], v["w_route_expert"][0]], axis=1)
                     .reshape(DC, P, GROUPS + E).transpose(1, 0, 2),
        "b_route": rows(np.concatenate([v["b_route_group"][0], v["b_route_expert"][0]])),
        "norm_ffn_g": rows(v["norm_ffn_g"]),
        "norm_final_g": rows(v["norm_final_g"]),
        "w1": by_rows(v["w1"][0], 4),
        "w3": by_rows(v["w3"][0], 4),
        "w2": by_rows(v["w2"][0], 2),
        "w_ada_2": by_columns(v["w_ada_2"], 256),
        "w_in_2": by_columns(v["w_in_2"], 256),
        "w_up_a_2": by_columns(v["w_up_a_2"], 512),
        "w_up_b_2": by_columns(v["w_up_b_2"], 512),
        "w_o_2": by_rows(v["w_o_2"], 2),
        "w_pq_2": by_columns(v["w_pq_2"], 256),
        "sub_keys_2": v["sub_keys_2"].transpose(0, 1, 4, 2, 3).reshape(LAYERS, P, PH, P),
        "peer_u_2": v["peer_u_2"].reshape(-1, D),
        "peer_v_2": v["peer_v_2"].reshape(-1, D),
        "ln_g_2": np.broadcast_to(v["ln_g_2"][:, :, None, :], (LAYERS, 2, P, D)),
        "ln_b_2": np.broadcast_to(v["ln_b_2"][:, :, None, :], (LAYERS, 2, P, D)),
    }
    return {k: np.ascontiguousarray(a) for k, a in out.items()}


def kernel(**inputs):
    import numpy as np
    import concourse.bacc as bacc
    from concourse.bass_utils import run_bass_kernel_spmd

    arrays = layouts(inputs)
    nc = bacc.Bacc("TRN2", target_bir_lowering=False, num_devices=1)
    dram = {n: nc.dram_tensor("in_" + n, a.shape, mybir.dt.from_np(a.dtype), kind="ExternalInput").ap()
            for n, a in arrays.items()}
    out = nc.dram_tensor("y", (P, NT, D), F32, kind="ExternalOutput").ap()
    build(nc, dram, out)
    got = run_bass_kernel_spmd(nc, [{"in_" + n: a for n, a in arrays.items()}], core_ids=[0]).results[0]["y"]
    return np.ascontiguousarray(got.transpose(1, 0, 2)).reshape(1, S, D)
```
